# Optimizing a Trainium2 kernel written in Bass

```python
import jax
import jax.numpy as jnp
from jax import lax
import numpy as np
import jax, jax.numpy as jnp

D_MODEL = 1024
BATCH = 1
SEQ = 256
DEPTH = 1

GLA_HEADS = 4
GLA_DK = 128
GLA_DV = 128
GLA_RANK = 16
GLA_TAU = 16.0
GLA_CHUNK = 16
DIL_PATTERNS = ((128, 1), (512, 4), (2048, 16))
DIL_GROUPS = 3
DIL_HEADS = 4
DIL_DH = 128
DIL_BLOCK = 128
N_GROUPS = 4
EXPERTS_PER_GROUP = 8
N_EXPERTS = N_GROUPS * EXPERTS_PER_GROUP
TOP_K = 2
D_EXPERT = 512
MOE_BLOCK = 128
EPS = 1e-6

GLA_QK_W = GLA_HEADS * GLA_DK
GLA_V_W = GLA_HEADS * GLA_DV
DIL_W = DIL_HEADS * DIL_DH
SPLIT_SIZES = (GLA_QK_W, GLA_QK_W, GLA_V_W, GLA_V_W, GLA_RANK) + (DIL_W,) * (3 * DIL_GROUPS)
IN_COLS = sum(SPLIT_SIZES)
SPLIT_POINTS = tuple(int(v) for v in np.cumsum(SPLIT_SIZES)[:-1])
ALIBI_SLOPES = tuple(2.0 ** (-8.0 * (i + 1) / (DIL_GROUPS * DIL_HEADS)) for i in range(DIL_GROUPS * DIL_HEADS))


def rms_norm(x, g):
    xf = x.astype(jnp.float32)
    y = xf * lax.rsqrt(jnp.mean(xf * xf, axis=-1, keepdims=True) + EPS)
    return (y * g.astype(jnp.float32)).astype(x.dtype)

def gla_chunked(q, k, v, log_a):
    B, S, H, DK = q.shape
    DV = v.shape[-1]
    C = GLA_CHUNK
    N = S // C
    def chunks(t):
        return t.astype(jnp.float32).reshape(B, N, C, H, t.shape[-1]).transpose(1, 0, 3, 2, 4)
    qc = chunks(q) * (DK ** -0.5)
    kc = chunks(k)
    vc = chunks(v)
    b = jnp.cumsum(chunks(log_a), axis=3)
    b_last = b[:, :, :, -1:, :]
    q_in = qc * jnp.exp(b)
    k_in = kc * jnp.exp(-b)
    k_end = kc * jnp.exp(b_last - b)
    causal = jnp.tril(jnp.ones((C, C), dtype=bool))
    att = jnp.where(causal, jnp.einsum('nbhik,nbhjk->nbhij', q_in, k_in), 0.0)
    o_intra = jnp.einsum('nbhij,nbhjv->nbhiv', att, vc)

    def step(state, xs):
        q_n, k_n, v_n, dec_n = xs
        o_n = jnp.einsum('bhik,bhkv->bhiv', q_n, state)
        state = dec_n[:, :, 0, :, None] * state + jnp.einsum('bhjk,bhjv->bhkv', k_n, v_n)
        return state, o_n

    state0 = jnp.zeros((B, H, DK, DV), jnp.float32)
    _, o_inter = lax.scan(step, state0, (q_in, k_end, vc, jnp.exp(b_last)))
    o = o_intra + o_inter
    return o.transpose(1, 0, 3, 2, 4).reshape(B, S, H, DV)

def dilated_group(q, k, v, slopes, window, dilation):
    B, S, H, E = q.shape
    L = S // dilation
    Q = DIL_BLOCK
    span = window // dilation
    nb = -(-L // Q)
    Lp = nb * Q

    def to_sub(t):
        t = jnp.swapaxes(t.reshape(B, L, dilation, H, E), 1, 2)
        return jnp.pad(t, ((0, 0), (0, 0), (0, Lp - L), (0, 0), (0, 0)))

    def kv_blocks(t):
        t = jnp.pad(to_sub(t), ((0, 0), (0, 0), (Q, 0), (0, 0), (0, 0))).reshape(B, dilation, nb + 1, Q, H, E)
        return jnp.concatenate([t[:, :, :-1], t[:, :, 1:]], axis=3)

    def from_sub(t):
        t = t.reshape((B, dilation, Lp) + t.shape[4:])[:, :, :L]
        t = jnp.swapaxes(t, 1, 2)
        return t.reshape((B, S) + t.shape[3:])

    qb = to_sub(q).reshape(B, dilation, nb, Q, H, E)
    kb = kv_blocks(k)
    vb = kv_blocks(v)
    s = jnp.einsum('bdnqhe,bdnkhe->bdnhqk', qb, kb, preferred_element_type=jnp.float32) * (E ** -0.5)
    dist = jnp.arange(Q)[:, None] + Q - jnp.arange(2 * Q)[None, :]
    key_pos = jnp.arange(nb)[:, None, None] * Q + jnp.arange(2 * Q)[None, None, :] - Q
    valid = (dist >= 0) & (dist <= span) & (key_pos >= 0)
    bias = -slopes[:, None, None] * (dilation * dist).astype(jnp.float32)
    s = jnp.where(valid[:, None], s + bias, -jnp.inf)
    m = jnp.max(s, axis=-1)
    p = jnp.exp(s - m[..., None])
    den = jnp.sum(p, axis=-1)
    den_t = jnp.swapaxes(den, -1, -2)
    o = jnp.einsum('bdnhqk,bdnkhe->bdnqhe', p, vb.astype(jnp.float32)) / den_t[..., None]
    return from_sub(o), from_sub(jnp.swapaxes(m, -1, -2)), from_sub(den_t)

def hier_moe(h, w_rg, b_rg, w_re, b_re, w_gate, w_up, w_down):
    B, S, D = h.shape
    T = B * S
    hf = h.reshape(T, D)
    g_logit = (hf @ w_rg).astype(jnp.float32) + b_rg
    g_prob = jax.nn.softmax(g_logit, axis=-1)
    g_sel = jnp.argmax(g_logit, axis=-1)
    g_p = jnp.take_along_axis(g_prob, g_sel[:, None], axis=-1)[:, 0]
    e_logit = ((hf @ w_re).astype(jnp.float32) + b_re).reshape(T, N_GROUPS, EXPERTS_PER_GROUP)
    e_logit = jnp.take_along_axis(e_logit, g_sel[:, None, None], axis=1)[:, 0]
    top_v, top_i = lax.top_k(e_logit, TOP_K)
    gate = jax.nn.softmax(top_v, axis=-1) * g_p[:, None]
    eid = g_sel[:, None] * EXPERTS_PER_GROUP + top_i

    A = T * TOP_K
    flat_e = eid.reshape(A).astype(jnp.int32)
    flat_w = gate.reshape(A)
    flat_t = jnp.repeat(jnp.arange(T, dtype=jnp.int32), TOP_K)
    order = jnp.argsort(flat_e)
    se, st, sw = flat_e[order], flat_t[order], flat_w[order]
    counts = jnp.bincount(flat_e, length=N_EXPERTS)
    starts = jnp.cumsum(counts) - counts
    pcounts = (counts + MOE_BLOCK - 1) // MOE_BLOCK * MOE_BLOCK
    pends = jnp.cumsum(pcounts)
    pstarts = pends - pcounts
    dest = pstarts[se] + jnp.arange(A, dtype=jnp.int32) - starts[se]
    P = A + N_EXPERTS * MOE_BLOCK
    NB = P // MOE_BLOCK
    row_t = jnp.full((P,), T, jnp.int32).at[dest].set(st)
    row_w = jnp.zeros((P,), jnp.float32).at[dest].set(sw)
    blk_e = jnp.minimum(jnp.searchsorted(pends, jnp.arange(NB, dtype=jnp.int32) * MOE_BLOCK, side='right'), N_EXPERTS - 1)
    h_pad = jnp.concatenate([hf, jnp.zeros((1, D), hf.dtype)], axis=0)
    xin = h_pad[row_t].reshape(NB, MOE_BLOCK, D)

    def expert_block(args):
        xb, e = args
        return (jax.nn.silu(xb @ w_gate[e]) * (xb @ w_up[e])) @ w_down[e]

    yb = lax.map(expert_block, (xin, blk_e)).reshape(P, D)
    out = jnp.zeros((T + 1, D), jnp.float32).at[row_t].add(yb.astype(jnp.float32) * row_w[:, None])[:T]
    return out.reshape(B, S, D).astype(h.dtype)

def first_inputs(seed: int = 0) -> dict:
    key = jax.random.key(seed)
    ks = jax.random.split(key, 22)
    def nrm(k, shape, scale):
        return scale * jax.random.normal(k, shape, jnp.float32)
    L = DEPTH
    return {
        'x': nrm(ks[0], (BATCH, SEQ, D_MODEL), 1.0),
        'norm1_g': 1.0 + nrm(ks[1], (L, D_MODEL), 0.02),
        'w_in': nrm(ks[2], (L, D_MODEL, IN_COLS), D_MODEL ** -0.5),
        'w_gla_a2': nrm(ks[3], (L, GLA_RANK, GLA_QK_W), GLA_RANK ** -0.5),
        'b_gla_a': nrm(ks[4], (L, GLA_QK_W), 0.1),
        'gla_out_norm_g': 1.0 + nrm(ks[5], (L, GLA_DV), 0.02),
        'dil_q_norm_g': 1.0 + nrm(ks[6], (L, DIL_GROUPS, DIL_DH), 0.02),
        'dil_k_norm_g': 1.0 + nrm(ks[7], (L, DIL_GROUPS, DIL_DH), 0.02),
        'w_proj_gla': nrm(ks[8], (L, GLA_V_W, D_MODEL), GLA_V_W ** -0.5),
        'w_proj_attn': nrm(ks[9], (L, DIL_W, D_MODEL), DIL_W ** -0.5),
        'w_branch_gate': nrm(ks[10], (L, D_MODEL, 2 * D_MODEL), D_MODEL ** -0.5),
        'b_branch_gate': nrm(ks[11], (L, 2 * D_MODEL), 0.01),
        'w_out': nrm(ks[12], (L, D_MODEL, D_MODEL), D_MODEL ** -0.5),
        'norm2_g': 1.0 + nrm(ks[13], (L, D_MODEL), 0.02),
        'w_router_group': nrm(ks[14], (L, D_MODEL, N_GROUPS), D_MODEL ** -0.5),
        'b_router_group': nrm(ks[15], (L, N_GROUPS), 0.01),
        'w_router_expert': nrm(ks[16], (L, D_MODEL, N_EXPERTS), D_MODEL ** -0.5),
        'b_router_expert': nrm(ks[17], (L, N_EXPERTS), 0.01),
        'w_gate': nrm(ks[18], (L, N_EXPERTS, D_MODEL, D_EXPERT), D_MODEL ** -0.5),
        'w_up': nrm(ks[19], (L, N_EXPERTS, D_MODEL, D_EXPERT), D_MODEL ** -0.5),
        'w_down': nrm(ks[20], (L, N_EXPERTS, D_EXPERT, D_MODEL), D_EXPERT ** -0.5),
    }

def first_block(x, norm1_g, w_in, w_gla_a2, b_gla_a, gla_out_norm_g, dil_q_norm_g, dil_k_norm_g,
              w_proj_gla, w_proj_attn, w_branch_gate, b_branch_gate, w_out, norm2_g,
              w_router_group, b_router_group, w_router_expert, b_router_expert, w_gate, w_up, w_down):
    B, S, D = x.shape
    slopes = jnp.asarray(ALIBI_SLOPES, jnp.float32).reshape(DIL_GROUPS, DIL_HEADS)
    def heads(t, e):
        return t.reshape(B, S, -1, e)
    for l in range(DEPTH):
        h = rms_norm(x, norm1_g[l])
        parts = jnp.split(h @ w_in[l], list(SPLIT_POINTS), axis=-1)
        gq, gk, gv, gr, ga_lr = parts[:5]
        log_a = jax.nn.log_sigmoid((ga_lr @ w_gla_a2[l] + b_gla_a[l]).astype(jnp.float32)) / GLA_TAU
        o_gla = gla_chunked(heads(gq, GLA_DK), heads(gk, GLA_DK), heads(gv, GLA_DV), heads(log_a, GLA_DK))
        o_gla = rms_norm(o_gla, gla_out_norm_g[l]).reshape(B, S, GLA_V_W) * jax.nn.silu(gr.astype(jnp.float32))
        y_gla = o_gla.astype(x.dtype) @ w_proj_gla[l]
        outs, maxes, dens = [], [], []
        for gi, (window, dilation) in enumerate(DIL_PATTERNS):
            q, k, v = parts[5 + 3 * gi: 8 + 3 * gi]
            q = rms_norm(heads(q, DIL_DH), dil_q_norm_g[l, gi])
            k = rms_norm(heads(k, DIL_DH), dil_k_norm_g[l, gi])
            o_g, m_g, d_g = dilated_group(q, k, heads(v, DIL_DH), slopes[gi], window, dilation)
            outs.append(o_g)
            maxes.append(m_g)
            dens.append(d_g)
        m_all = jnp.stack(maxes)
        wts = jnp.stack(dens) * jnp.exp(m_all - jnp.max(m_all, axis=0))
        o_att = jnp.sum(wts[..., None] * jnp.stack(outs), axis=0) / jnp.sum(wts, axis=0)[..., None]
        y_att = o_att.reshape(B, S, DIL_W).astype(x.dtype) @ w_proj_attn[l]
        g_gla, g_att = jnp.split(jax.nn.sigmoid(h @ w_branch_gate[l] + b_branch_gate[l]), 2, axis=-1)
        x = x + ((g_gla * y_gla + g_att * y_att) @ w_out[l]).astype(x.dtype)
        x = x + hier_moe(rms_norm(x, norm2_g[l]), w_router_group[l], b_router_group[l], w_router_expert[l],
                         b_router_expert[l], w_gate[l], w_up[l], w_down[l])
    return x


DEPTH_2 = 2

HEAD_DIM = 64
A_HEADS = D_MODEL // 256
B_HEADS = D_MODEL // 256
C_HEADS = D_MODEL // 128
A_WIDTH = A_HEADS * HEAD_DIM
B_WIDTH = B_HEADS * HEAD_DIM
C_WIDTH = C_HEADS * HEAD_DIM
D_MIX = A_WIDTH + B_WIDTH + C_WIDTH
CHUNK = 128
LN_EPS = 1e-5
RW_DECAY_LORA = 64
RW_A_LORA = 64
RW_GATE_LORA = 128
GN_EPS = 64e-5
C_KV_GROUPS = 2
C_Q_PER_GROUP = C_HEADS // C_KV_GROUPS
C_KV_WIDTH = C_KV_GROUPS * HEAD_DIM
CMP_BLOCK = 32
CMP_STRIDE = 16
CMP_HIDDEN = 2 * HEAD_DIM
SLC_BLOCK = 64
SLC_TOPK = 16
WINDOW = 512
Q_BLOCK = 128
NEG_INF = -1e30
FORCE = 1e4
ROPE_THETA = 500000.0
ROPE_DIM = HEAD_DIM // 4
D_FF = 2816
N_EXPERTS_2 = 8
PLE_DIM = 256
RMS_EPS = 1e-6
N_DENSE = (DEPTH_2 + 1) // 2
N_MOE = DEPTH_2 // 2
A_SIZES = (A_WIDTH, A_WIDTH)
B_SIZES = (B_WIDTH, B_WIDTH, B_WIDTH, RW_DECAY_LORA, RW_A_LORA, RW_GATE_LORA)
C_SIZES = (C_WIDTH,) + (C_KV_WIDTH,) * 6 + (3 * C_HEADS,)
A_COLS = 2 * A_WIDTH
B_COLS = 3 * B_WIDTH + RW_DECAY_LORA + RW_A_LORA + RW_GATE_LORA
C_COLS = C_WIDTH + 6 * C_KV_WIDTH + 3 * C_HEADS
D_IN = A_COLS + B_COLS + C_COLS


def split_cols(z, sizes):
    out, off = [], 0
    for s in sizes:
        out.append(z[..., off:off + s])
        off += s
    return out

def rms_norm_2(x, g):
    xf = x.astype(jnp.float32)
    y = xf * lax.rsqrt(jnp.mean(xf * xf, axis=-1, keepdims=True) + RMS_EPS)
    return (y * g.astype(jnp.float32)).astype(x.dtype)

def layer_norm(x, g, b, eps):
    xf = x.astype(jnp.float32)
    mu = jnp.mean(xf, axis=-1, keepdims=True)
    var = jnp.mean(jnp.square(xf - mu), axis=-1, keepdims=True)
    return ((xf - mu) * lax.rsqrt(var + eps) * g.astype(jnp.float32) + b.astype(jnp.float32)).astype(x.dtype)

def rope_tables(positions):
    inv = 1.0 / (ROPE_THETA ** (jnp.arange(0, ROPE_DIM, 2, dtype=jnp.float32) / ROPE_DIM))
    ang = positions.astype(jnp.float32)[..., None] * inv
    return jnp.cos(ang), jnp.sin(ang)

def apply_partial_rope(x, cos, sin):
    bshape = cos.shape[:2] + (1,) * (x.ndim - 3) + cos.shape[-1:]
    c = cos.reshape(bshape).astype(x.dtype)
    s = sin.reshape(bshape).astype(x.dtype)
    half = ROPE_DIM // 2
    x1, x2, xp = x[..., :half], x[..., half:ROPE_DIM], x[..., ROPE_DIM:]
    return jnp.concatenate([x1 * c - x2 * s, x1 * s + x2 * c, xp], axis=-1)

def masked_softmax(s, mask):
    s32 = jnp.where(mask, s.astype(jnp.float32), NEG_INF)
    pr = jax.nn.softmax(s32, axis=-1)
    return jnp.where(mask, pr, 0.0).astype(s.dtype)

def swiglu(x, w1, w3, w2):
    return (jax.nn.silu(x @ w1) * (x @ w3)) @ w2

def chunked_spatial_gating(z_a, ln_g, ln_b, w_s, b_s):
    Bn, S, _ = z_a.shape
    nc = S // CHUNK
    u, v = split_cols(jax.nn.gelu(z_a), A_SIZES)
    u = u.reshape(Bn, nc, CHUNK, A_HEADS, HEAD_DIM)
    v = layer_norm(v.reshape(Bn, nc, CHUNK, A_HEADS, HEAD_DIM), ln_g, ln_b, LN_EPS)
    causal = jnp.tril(jnp.ones((CHUNK, CHUNK), dtype=bool))
    w = jnp.where(causal[None], w_s, 0.0).astype(v.dtype)
    mixed = jnp.einsum('hts,bnshd->bnthd', w, v) + b_s.T[None, None, :, :, None]
    return (u * mixed).reshape(Bn, S, A_WIDTH)

def rwkv7_time_mix(z_b, mu, w0, w_up, a0, a_up, g_up, k_k, k_a, r_k, gn_g, gn_b):
    Bn, S, _ = z_b.shape
    f32 = jnp.float32
    z_prev = jnp.pad(z_b[:, :-1], ((0, 0), (1, 0), (0, 0)))
    z = z_b + (z_prev - z_b) * mu
    r, k, v, wd, ad, gd = split_cols(z, B_SIZES)
    w_logit = -jax.nn.softplus(-(w0 + jnp.tanh(wd) @ w_up).astype(f32)) - 0.5
    decay = jnp.exp(-jnp.exp(w_logit))
    a = jax.nn.sigmoid((a0 + ad @ a_up).astype(f32))
    g = jax.nn.sigmoid(gd) @ g_up
    hs = lambda t: t.astype(f32).reshape(Bn, S, B_HEADS, HEAD_DIM)
    kk = hs(k * k_k)
    kk = kk * lax.rsqrt(jnp.maximum(jnp.sum(kk * kk, axis=-1, keepdims=True), 1e-24))
    k_a_h = k_a.astype(f32).reshape(B_HEADS, HEAD_DIM)
    k = hs(k) * (1.0 + (hs(a) - 1.0) * k_a_h)
    r_h, v_h, a_h, w_h = hs(r), hs(v), hs(a), hs(decay)

    def step(state, inp):
        r_t, w_t, k_t, v_t, kk_t, a_t = inp
        sa = jnp.einsum('bhvk,bhk->bhv', state, -kk_t)
        state = (state * w_t[:, :, None, :] + sa[..., None] * (kk_t * a_t)[:, :, None, :]
                 + v_t[..., None] * k_t[:, :, None, :])
        return state, jnp.einsum('bhvk,bhk->bhv', state, r_t)

    xs = tuple(jnp.moveaxis(t, 1, 0) for t in (r_h, w_h, k, v_h, kk, a_h))
    s0 = jnp.zeros((Bn, B_HEADS, HEAD_DIM, HEAD_DIM), f32)
    _, ys = lax.scan(step, s0, xs)
    y = jnp.moveaxis(ys, 0, 1)
    mu_y = jnp.mean(y, axis=-1, keepdims=True)
    var_y = jnp.mean(jnp.square(y - mu_y), axis=-1, keepdims=True)
    y = ((y - mu_y) * lax.rsqrt(var_y + GN_EPS)).reshape(Bn, S, B_WIDTH)
    y = y * gn_g.astype(f32) + gn_b.astype(f32)
    bonus = jnp.sum(r_h * k * r_k.astype(f32), axis=-1, keepdims=True) * v_h
    y = y + bonus.reshape(Bn, S, B_WIDTH)
    return (y * g.astype(f32)).astype(z_b.dtype)

def nsa_attention(z_c, cos, sin, cmp_pos, kc_w1, kc_w2, vc_w1, vc_w2):
    Bn, S, _ = z_c.shape
    G, J, Dh = C_KV_GROUPS, C_Q_PER_GROUP, HEAD_DIM
    scale = HEAD_DIM ** -0.5
    q, kc, vc, ks, vs, kw, vw, gates = split_cols(z_c, C_SIZES)
    q = q.reshape(Bn, S, G, J, Dh)
    kv = lambda t: t.reshape(Bn, S, G, Dh)
    kc, vc, ks, vs, kw, vw = map(kv, (kc, vc, ks, vs, kw, vw))
    gates = jax.nn.sigmoid(gates.astype(jnp.float32)).astype(z_c.dtype).reshape(Bn, S, G, J, 3)
    q_rot = apply_partial_rope(q, cos, sin)
    ks = apply_partial_rope(ks, cos, sin)
    kw = apply_partial_rope(kw, cos, sin)

    n_cmp = (S - CMP_BLOCK) // CMP_STRIDE + 1
    cmp_idx = np.arange(n_cmp)[:, None] * CMP_STRIDE + np.arange(CMP_BLOCK)[None, :]
    cmp_end = jnp.asarray(cmp_idx[:, -1])

    def compress(t, w1, w2):
        blk = t[:, cmp_idx] + cmp_pos[None, None, :, None, :]
        blk = blk.transpose(0, 1, 3, 2, 4).reshape(Bn, n_cmp, G, CMP_BLOCK * Dh)
        return jax.nn.gelu(blk @ w1) @ w2

    k_cmp = compress(kc, kc_w1, kc_w2)
    v_cmp = compress(vc, vc_w1, vc_w2)

    n_slc = S // SLC_BLOCK
    n_sel = min(SLC_TOPK, n_slc)
    slc_start = np.arange(n_slc) * SLC_BLOCK
    overlap = jnp.asarray(((cmp_idx[:, :1] < slc_start[None, :] + SLC_BLOCK)
                           & (cmp_idx[:, -1:] >= slc_start[None, :])).astype(np.float32))
    ks_blk = ks.reshape(Bn, n_slc, SLC_BLOCK, G, Dh).transpose(0, 3, 1, 2, 4)
    vs_blk = vs.reshape(Bn, n_slc, SLC_BLOCK, G, Dh).transpose(0, 3, 1, 2, 4)
    kw_pad = jnp.pad(kw, ((0, 0), (WINDOW, 0), (0, 0), (0, 0)))
    vw_pad = jnp.pad(vw, ((0, 0), (WINDOW, 0), (0, 0), (0, 0)))
    bi = jnp.arange(Bn)[:, None, None, None]
    gi = jnp.arange(G)[None, :, None, None]
    m_ids = jnp.arange(n_slc)

    def query_block(qb):
        start = qb * Q_BLOCK
        t = start + jnp.arange(Q_BLOCK)
        q_raw = lax.dynamic_slice_in_dim(q, start, Q_BLOCK, axis=1)
        q_r = lax.dynamic_slice_in_dim(q_rot, start, Q_BLOCK, axis=1)
        g_t = lax.dynamic_slice_in_dim(gates, start, Q_BLOCK, axis=1)
        s_c = jnp.einsum('btgjd,bngd->bgjtn', q_raw, k_cmp) * scale
        p_c = masked_softmax(s_c, cmp_end[None, :] <= t[:, None])
        o_c = jnp.einsum('bgjtn,bngd->btgjd', p_c, v_cmp)
        imp = jnp.einsum('bgjtn,nm->bgtm', p_c.astype(jnp.float32), overlap)
        blk_t = (t // SLC_BLOCK)[:, None]
        valid = m_ids[None, :] <= blk_t
        forced = (m_ids[None, :] == 0) | (m_ids[None, :] == blk_t) | (m_ids[None, :] == blk_t - 1)
        imp = jnp.where(valid, imp + FORCE * forced.astype(jnp.float32), -FORCE)
        top_v, top_i = lax.top_k(imp, n_sel)
        sel_ok = top_v > -0.5 * FORCE
        k_sel = ks_blk[bi, gi, top_i]
        v_sel = vs_blk[bi, gi, top_i]
        kpos = top_i[..., None] * SLC_BLOCK + jnp.arange(SLC_BLOCK)
        m_s = (sel_ok[..., None] & (kpos <= t[None, None, :, None, None]))
        m_s = m_s.reshape(Bn, G, 1, Q_BLOCK, n_sel * SLC_BLOCK)
        s_s = jnp.einsum('btgjd,bgtksd->bgjtks', q_r, k_sel) * scale
        p_s = masked_softmax(s_s.reshape(Bn, G, J, Q_BLOCK, n_sel * SLC_BLOCK), m_s)
        p_s = p_s.reshape(Bn, G, J, Q_BLOCK, n_sel, SLC_BLOCK)
        o_s = jnp.einsum('bgjtks,bgtksd->btgjd', p_s, v_sel)
        k_win = lax.dynamic_slice_in_dim(kw_pad, start, WINDOW + Q_BLOCK, axis=1)
        v_win = lax.dynamic_slice_in_dim(vw_pad, start, WINDOW + Q_BLOCK, axis=1)
        kpos_w = start - WINDOW + jnp.arange(WINDOW + Q_BLOCK)
        m_w = ((kpos_w[None, :] <= t[:, None]) & (kpos_w[None, :] > t[:, None] - WINDOW)
               & (kpos_w[None, :] >= 0))
        s_w = jnp.einsum('btgjd,bkgd->bgjtk', q_r, k_win) * scale
        p_w = masked_softmax(s_w, m_w)
        o_w = jnp.einsum('bgjtk,bkgd->btgjd', p_w, v_win)
        o = g_t[..., 0:1] * o_c + g_t[..., 1:2] * o_s + g_t[..., 2:3] * o_w
        return o.reshape(Bn, Q_BLOCK, C_WIDTH)

    out = lax.map(query_block, jnp.arange(S // Q_BLOCK))
    return out.transpose(1, 0, 2, 3).reshape(Bn, S, C_WIDTH)

def moe_swiglu(x, router_w, router_b, w1, w3, w2):
    logits = (x @ router_w + router_b).astype(jnp.float32)
    top_v, top_i = lax.top_k(logits, TOP_K)
    top_p = jax.nn.softmax(top_v, axis=-1)
    gate = jnp.sum(jax.nn.one_hot(top_i, N_EXPERTS_2, dtype=jnp.float32) * top_p[..., None], axis=-2)
    gate = gate.astype(x.dtype)
    out = jnp.zeros_like(x)
    for e in range(N_EXPERTS_2):
        out = out + gate[..., e:e + 1] * swiglu(x, w1[e], w3[e], w2[e])
    return out

def second_inputs(seed: int = 0) -> dict:
    key = jax.random.key(seed)
    ks = iter(jax.random.split(key, 64))
    f32 = jnp.float32

    def nrm(shape, scale):
        return scale * jax.random.normal(next(ks), shape, f32)

    def gain(shape):
        return 1.0 + 0.1 * jax.random.normal(next(ks), shape, f32)

    L = DEPTH_2
    x = nrm((BATCH, SEQ, D_MODEL), 1.0)
    p = nrm((DEPTH_2, BATCH, SEQ, PLE_DIM), 1.0)
    offset = jax.random.randint(next(ks), (BATCH, 1), 0, 1024, dtype=jnp.int32)
    positions = offset + jnp.arange(SEQ, dtype=jnp.int32)[None, :]
    return {
        "x": x, "p": p, "positions": positions,
        "g_mix": gain((L, D_MODEL)),
        "w_in": nrm((L, D_MODEL, D_IN), D_MODEL ** -0.5),
        "w_out": nrm((L, D_MIX, D_MODEL), D_MIX ** -0.5),
        "gm_ln_g": gain((L, A_HEADS, HEAD_DIM)),
        "gm_ln_b": nrm((L, A_HEADS, HEAD_DIM), 0.1),
        "gm_ws": nrm((L, A_HEADS, CHUNK, CHUNK), CHUNK ** -0.5),
        "gm_bs": gain((L, A_HEADS, CHUNK)),
        "rw_mu": jax.random.uniform(next(ks), (L, B_COLS), f32),
        "rw_w0": nrm((L, B_WIDTH), 0.5),
        "rw_w_up": nrm((L, RW_DECAY_LORA, B_WIDTH), 0.1),
        "rw_a0": nrm((L, B_WIDTH), 0.5),
        "rw_a_up": nrm((L, RW_A_LORA, B_WIDTH), RW_A_LORA ** -0.5),
        "rw_g_up": nrm((L, RW_GATE_LORA, B_WIDTH), RW_GATE_LORA ** -0.5),
        "rw_k_k": 0.85 + nrm((L, B_WIDTH), 0.1),
        "rw_k_a": gain((L, B_WIDTH)),
        "rw_r_k": nrm((L, B_HEADS, HEAD_DIM), 0.1),
        "rw_gn_g": gain((L, B_WIDTH)),
        "rw_gn_b": nrm((L, B_WIDTH), 0.1),
        "nsa_cmp_pos": nrm((L, CMP_BLOCK, HEAD_DIM), 0.1),
        "nsa_kc_w1": nrm((L, CMP_BLOCK * HEAD_DIM, CMP_HIDDEN), (CMP_BLOCK * HEAD_DIM) ** -0.5),
        "nsa_kc_w2": nrm((L, CMP_HIDDEN, HEAD_DIM), CMP_HIDDEN ** -0.5),
        "nsa_vc_w1": nrm((L, CMP_BLOCK * HEAD_DIM, CMP_HIDDEN), (CMP_BLOCK * HEAD_DIM) ** -0.5),
        "nsa_vc_w2": nrm((L, CMP_HIDDEN, HEAD_DIM), CMP_HIDDEN ** -0.5),
        "g_ffn": gain((L, D_MODEL)),
        "ffn_w1": nrm((N_DENSE, D_MODEL, D_FF), D_MODEL ** -0.5),
        "ffn_w3": nrm((N_DENSE, D_MODEL, D_FF), D_MODEL ** -0.5),
        "ffn_w2": nrm((N_DENSE, D_FF, D_MODEL), D_FF ** -0.5),
        "router_w": nrm((N_MOE, D_MODEL, N_EXPERTS_2), D_MODEL ** -0.5),
        "router_b": nrm((N_MOE, N_EXPERTS_2), 0.01),
        "moe_w1": nrm((N_MOE, N_EXPERTS_2, D_MODEL, D_FF), D_MODEL ** -0.5),
        "moe_w3": nrm((N_MOE, N_EXPERTS_2, D_MODEL, D_FF), D_MODEL ** -0.5),
        "moe_w2": nrm((N_MOE, N_EXPERTS_2, D_FF, D_MODEL), D_FF ** -0.5),
        "g_ple": gain((L, D_MODEL)),
        "ple_gate_w": nrm((L, D_MODEL, D_MODEL), D_MODEL ** -0.5),
        "ple_proj_w": nrm((L, PLE_DIM, D_MODEL), PLE_DIM ** -0.5),
        "g_final": gain((D_MODEL,)),
    }

def second_block(x, p, positions, g_mix, w_in, w_out, gm_ln_g, gm_ln_b, gm_ws, gm_bs,
              rw_mu, rw_w0, rw_w_up, rw_a0, rw_a_up, rw_g_up, rw_k_k, rw_k_a, rw_r_k, rw_gn_g, rw_gn_b,
              nsa_cmp_pos, nsa_kc_w1, nsa_kc_w2, nsa_vc_w1, nsa_vc_w2,
              g_ffn, ffn_w1, ffn_w3, ffn_w2, router_w, router_b, moe_w1, moe_w3, moe_w2,
              g_ple, ple_gate_w, ple_proj_w, g_final):
    cos, sin = rope_tables(positions)
    h = x
    for i in range(DEPTH_2):
        hn = rms_norm_2(h, g_mix[i])
        z = hn @ w_in[i]
        z_a, z_b, z_c = split_cols(z, (A_COLS, B_COLS, C_COLS))
        y_a = chunked_spatial_gating(z_a, gm_ln_g[i], gm_ln_b[i], gm_ws[i], gm_bs[i])
        y_b = rwkv7_time_mix(z_b, rw_mu[i], rw_w0[i], rw_w_up[i], rw_a0[i], rw_a_up[i], rw_g_up[i],
                             rw_k_k[i], rw_k_a[i], rw_r_k[i], rw_gn_g[i], rw_gn_b[i])
        y_c = nsa_attention(z_c, cos, sin, nsa_cmp_pos[i], nsa_kc_w1[i], nsa_kc_w2[i],
                            nsa_vc_w1[i], nsa_vc_w2[i])
        h = h + jnp.concatenate([y_a, y_b, y_c], axis=-1) @ w_out[i]
        hn = rms_norm_2(h, g_ffn[i])
        if i % 2 == 0:
            j = i // 2
            f = swiglu(hn, ffn_w1[j], ffn_w3[j], ffn_w2[j])
        else:
            j = i // 2
            f = moe_swiglu(hn, router_w[j], router_b[j], moe_w1[j], moe_w3[j], moe_w2[j])
        h = h + f
        gate = jax.nn.sigmoid(rms_norm_2(h, g_ple[i]) @ ple_gate_w[i])
        h = h + (p[i] @ ple_proj_w[i]) * gate
    return rms_norm_2(h, g_final)


def setup_inputs(seed=0):
    out = dict(first_inputs(seed))
    for name, value in second_inputs(seed + 1).items():
        if name != "x":
            out[name + "_2"] = value
    return out


def reference(
    x, norm1_g, w_in, w_gla_a2, b_gla_a, gla_out_norm_g, dil_q_norm_g, dil_k_norm_g, w_proj_gla,
    w_proj_attn, w_branch_gate, b_branch_gate, w_out, norm2_g, w_router_group, b_router_group,
    w_router_expert, b_router_expert, w_gate, w_up, w_down, p_2, positions_2, g_mix_2, w_in_2,
    w_out_2, gm_ln_g_2, gm_ln_b_2, gm_ws_2, gm_bs_2, rw_mu_2, rw_w0_2, rw_w_up_2, rw_a0_2,
    rw_a_up_2, rw_g_up_2, rw_k_k_2, rw_k_a_2, rw_r_k_2, rw_gn_g_2, rw_gn_b_2, nsa_cmp_pos_2,
    nsa_kc_w1_2, nsa_kc_w2_2, nsa_vc_w1_2, nsa_vc_w2_2, g_ffn_2, ffn_w1_2, ffn_w3_2, ffn_w2_2,
    router_w_2, router_b_2, moe_w1_2, moe_w3_2, moe_w2_2, g_ple_2, ple_gate_w_2, ple_proj_w_2,
    g_final_2,
):
    x = first_block(
        x, norm1_g, w_in, w_gla_a2, b_gla_a, gla_out_norm_g, dil_q_norm_g, dil_k_norm_g,
        w_proj_gla, w_proj_attn, w_branch_gate, b_branch_gate, w_out, norm2_g, w_router_group,
        b_router_group, w_router_expert, b_router_expert, w_gate, w_up, w_down,
    )
    return second_block(
        x, p_2, positions_2, g_mix_2, w_in_2, w_out_2, gm_ln_g_2, gm_ln_b_2, gm_ws_2, gm_bs_2,
        rw_mu_2, rw_w0_2, rw_w_up_2, rw_a0_2, rw_a_up_2, rw_g_up_2, rw_k_k_2, rw_k_a_2,
        rw_r_k_2, rw_gn_g_2, rw_gn_b_2, nsa_cmp_pos_2, nsa_kc_w1_2, nsa_kc_w2_2, nsa_vc_w1_2,
        nsa_vc_w2_2, g_ffn_2, ffn_w1_2, ffn_w3_2, ffn_w2_2, router_w_2, router_b_2, moe_w1_2,
        moe_w3_2, moe_w2_2, g_ple_2, ple_gate_w_2, ple_proj_w_2, g_final_2,
    )


_drawn_inputs = setup_inputs


def setup_inputs(seed=0):
    import zlib

    import numpy as np

    out = dict(_drawn_inputs(seed))
    spreads = {}
    factors = {'dil_k_norm_g': 4.219,
     'b_branch_gate': 4.479,
     'b_router_group': 8.0,
     'rw_k_k_2': 4.023,
     'router_b_2': 2.765}
    for name, (base, spread) in spreads.items():
        noise = np.random.default_rng([zlib.crc32(name.encode()), seed]).standard_normal(out[name].shape)
        drawn = base * np.exp(spread * noise) if base else spread * noise
        out[name] = jnp.asarray(drawn.astype(out[name].dtype))
    for name, factor in factors.items():
        out[name] = (out[name] * factor).astype(out[name].dtype)
    return out
```

```python
from contextlib import ExitStack

import numpy as np

import concourse.bass as bass
from concourse import mybir

F32 = mybir.dt.float32
I32 = mybir.dt.int32
ALU = mybir.AluOpType
ACT = mybir.ActivationFunctionType
AX = mybir.AxisListType.X

P = 128
S = 256
NT = S // P
D = 1024
KC = D // P
EPS = 1e-6
BIG = 1e30

GH, GD, RANK, TAU, GCH = 4, 128, 16, 16.0, 16
GW = GH * GD
NCH = P // GCH
DG, DH, DD = 3, 4, 128
SLOPES = [2.0 ** (-8.0 * (i + 1) / (DG * DH)) for i in range(DG * DH)]
N_GROUPS, PER_GROUP = 4, 8
NE1, DE1 = 32, 512
ZA = 4 * GW + RANK
ZB = 9 * GW

LAYERS = 2
HD = 64
AH, BH, CH, CG = 4, 4, 8, 2
AW, BW, CW = AH * HD, BH * HD, CH * HD
RC = 64
ZW = 2840
ZB0, ZC0 = 2 * AW, 2 * AW + 1024
CQ, CKC, CVC, CKS, CVS, CKW, CVW, CGT = [ZC0 + o for o in (0, 512, 640, 768, 896, 1024, 1152, 1280)]
NCMP, CB, CST = 15, 32, 16
DFF, NE2 = 2816, 8
PLE = 256
LN_EPS, GN_EPS = 1e-5, 64e-5
ROPE_HALF = HD // 8
INV_FREQ = [float(np.float32(1.0) / np.float32(500000.0) ** np.float32(2 * i / (2 * ROPE_HALF))) for i in range(ROPE_HALF)]

SLOTS = 3
FB = 256
GU = KC * 2 * FB
DN = FB // P * D
SLOT = GU + DN
NB1, NB2 = DE1 // FB, DFF // FB


class Arena:

    def __init__(self, flat):
        self.flat, self.at = flat, 0

    def take(self, *shape):
        n = int(np.prod(shape))
        view = self.flat[:, self.at:self.at + n]
        self.at += n
        assert self.at <= self.flat.shape[1], (self.at, self.flat.shape)
        if len(shape) == 2:
            return view.rearrange("p (a b) -> p a b", a=shape[0])
        if len(shape) == 3:
            return view.rearrange("p (a b c) -> p a b c", a=shape[0], b=shape[1])
        if len(shape) == 4:
            return view.rearrange("p (a b c d) -> p a b c d", a=shape[0], b=shape[1], c=shape[2])
        return view


class Unit:

    def __init__(self, slot, copies, ready, after):
        self.slot, self.copies, self.ready, self.after = slot, copies, ready, after


class Job:

    def __init__(self, unit, first, off, n, tile, col, index, engine, evac):
        self.unit, self.first, self.off, self.n, self.tile, self.col = unit, first, off, n, tile, col
        self.index, self.engine, self.evac = index, engine, evac


def emit(nc, d, out):
    ctx = ExitStack()
    with ctx:
        ctx.enter_context(nc.allow_non_contiguous_dma(reason="small per-feature parameters"))

        def sb(name, shape, dt=F32):
            return ctx.enter_context(nc.sbuf_tensor(name, shape, dt))

        def sem(name):
            return ctx.enter_context(nc.semaphore(name))

        ps = ctx.enter_context(nc.psum_tensor("ps", [P, 8, 512], F32))

        ring = sb("ring", [P, SLOTS, SLOT])
        x = sb("x", [P, NT, D])
        hT = sb("hT", [P, KC, S])
        ident = sb("ident", [P, P])
        diff = sb("diff", [P, P])
        xor_f = sb("xor_f", [P, P])
        gla_mask = sb("gla_mask", [P, P])
        tri_inc = sb("tri_inc", [P, P])
        tri_str = sb("tri_str", [P, P])
        same_chunk = sb("same_chunk", [P, P])
        causal_up = sb("causal_up", [P, P])
        low_b = sb("low_b", [P, 6, P])
        up_b = sb("up_b", [P, 6, P])
        shift_dn = sb("shift_dn", [P, P])
        shift_dn_edge = sb("shift_dn_edge", [P, P])
        shift_up = sb("shift_up", [P, P])
        shift_up_edge = sb("shift_up_edge", [P, P])
        negdist = sb("negdist", [P, S])
        dil_mask = sb("dil_mask", [P, DG, S])
        causal_neg = sb("causal_neg", [P, S])
        block16 = sb("block16", [P, NCH])
        half_ind = sb("half_ind", [P, 2])
        scan_keep = sb("scan_keep", [P, S])
        cmp_ok = sb("cmp_ok", [P, NT, 16])
        cmp_neg = sb("cmp_neg", [P, NT, 16])
        desc = sb("desc", [P, 32])
        ones = sb("ones", [P, 1])
        small = sb("small", [P, 128])
        gate_w = sb("gate_w", [P, NT, 32])
        g1T = sb("g1T", [P, KC])
        g2T = sb("g2T", [P, KC])
        gla_bT = sb("gla_bT", [P, GH])
        gla_og = sb("gla_og", [P, GD])
        gla_a2 = sb("gla_a2", [RANK, GW])
        dil_gT = sb("dil_gT", [P, 2, DG])
        r1_w = sb("r1_w", [P, KC, 36])
        r1_b = sb("r1_b", [P, 36])
        l_gT = sb("l_gT", [P, 3 * LAYERS, KC])
        l_mu = sb("l_mu", [P, 1024])
        l_row = sb("l_row", [P, 9, 256])
        l_bsT = sb("l_bsT", [P, AH])
        l_lora = sb("l_lora", [P, 2, 256])
        l_ws = sb("l_ws", [P, AH, P])
        l_posT = sb("l_posT", [P, 16])
        l_w2 = sb("l_w2", [P, 3, HD])
        r2_w = sb("r2_w", [P, KC, NE2])
        r2_b = sb("r2_b", [P, NE2])
        pos_i = sb("pos_i", [P, NT], I32)
        freq = sb("freq", [P, ROPE_HALF])
        cos_t = sb("cos_t", [P, NT, ROPE_HALF])
        sin_t = sb("sin_t", [P, NT, ROPE_HALF])
        n_arena = (nc.sbuf_bytes_remaining - 512) // 4 // 8 * 8
        arena = sb("arena", [P, n_arena])

        stage_done = sem("stage_done")
        slot_ready = [sem(f"slot{s}_ready") for s in range(SLOTS)]
        proj_done = sem("proj_done")
        evac_act = sem("evac_act")
        evac_dve = sem("evac_dve")
        ffn_used = sem("ffn_used")
        cmp_w_used = sem("cmp_w_used")
        dve_step = sem("dve_step")
        act_step = sem("act_step")
        sems = {}

        def sig(name):
            if name not in sems:
                sems[name] = sem(name)
            return sems[name]

        units, jobs_of = [], {}
        slot_val = [0] * SLOTS
        slot_free = [None] * SLOTS
        count = {"slot": 0, "job": 0, "act": 0, "dve": 0}

        def new_unit(copies):
            s = count["slot"] % SLOTS
            count["slot"] += 1
            slot_val[s] += 16 * len(copies)
            u = Unit(s, copies, slot_val[s], slot_free[s])
            units.append(u)
            return u

        def project(name, weight, kc, width, block, engines):
            jobs = []
            rows = weight.rearrange("(p c) n -> p c n", c=kc)
            for c0 in range(0, width, block):
                n = min(block, width - c0)
                s = count["slot"] % SLOTS
                dst = ring[:, s, 0:kc * n].rearrange("p (c n) -> p c n", c=kc)
                u = new_unit([(dst, rows[:, :, c0:c0 + n])])
                u.view = dst
                first = True
                for off in range(0, n, 512):
                    for t in range(NT):
                        e = engines[len(jobs) % len(engines)]
                        count[e] += 1
                        jobs.append(Job(u, first, off, min(512, n - off), t, c0 + off, count["job"], e, count[e]))
                        count["job"] += 1
                        first = False
                slot_free[s] = (proj_done, count["job"])
            jobs_of[name] = jobs

        class Ffn:
            pass

        step_count = [0]

        def align_slots():
            while count["slot"] % SLOTS:
                count["slot"] += 1

        def plan_ffn(name, w1, w3, w2, experts, nb, group):
            align_slots()
            f = Ffn()
            f.name, f.e, f.nb, f.group = name, experts, nb, group
            f.w1 = w1.rearrange("e (p c) n -> e p c n", c=KC)
            f.w3 = w3.rearrange("e (p c) n -> e p c n", c=KC)
            f.w2 = w2.rearrange("e (b p c) n -> e b p (c n)", p=P, c=FB // P)
            f.step0 = step_count[0]
            f.ready0 = list(slot_val)
            f.free0 = list(slot_free)
            for e in range(experts):
                for b in range(nb):
                    k = (e % group) * nb + b
                    slot_val[k % SLOTS] += 48
                    step_count[0] += 1
                    slot_free[k % SLOTS] = (ffn_used, step_count[0])
            f.fills = [len([k for k in range(group * nb) if k % SLOTS == s]) for s in range(SLOTS)]
            return f

        project("in_a", d["w_in"][0][:, 0:ZA], KC, ZA, 512, ["act"])
        project("in_b", d["w_in"][0][:, ZA:ZA + ZB], KC, ZB, 512, ["act", "dve"])
        project("gates", d["w_branch_gate"][0], KC, 2 * D, 512, ["dve"])
        project("y_gla", d["w_proj_gla"][0], GW // P, D, D, ["dve"])
        project("y_att", d["w_proj_attn"][0], GW // P, D, D, ["dve"])
        project("out_1", d["w_out"][0], KC, D, 512, ["dve"])
        ffn1 = plan_ffn("moe1", d["w_gate"][0], d["w_up"][0], d["w_down"][0], NE1, NB1, SLOTS)
        n_units_1 = len(units)
        ffn2, n_units_2, cmp_unit = [None, None], [0, 0], [None, None]
        n_units_3 = [0, 0]
        for l in range(LAYERS):
            project(f"in_{l}", d["w_in_2"][l], KC, ZW, 512, ["act", "dve"])
            s = count["slot"] % SLOTS
            dst = ring[:, s, 0:2 * 16 * P].rearrange("p (k i h) -> p k i h", k=2, i=16)
            cmp_unit[l] = new_unit([(dst[:, k], d[w][l].rearrange("(i p) h -> p i h", p=P))
                                    for k, w in enumerate(("nsa_kc_w1_2", "nsa_vc_w1_2"))])
            cmp_unit[l].view = dst
            slot_free[s] = (cmp_w_used, l + 1)
            project(f"out_{l}_2", d["w_out_2"][l], KC, D, 512, ["dve"])
            n_units_2[l] = len(units)
            if l % 2 == 0:
                ffn2[l] = plan_ffn(f"ffn{l}", d["ffn_w1_2"], d["ffn_w3_2"], d["ffn_w2_2"], 1, NB2, 1)
            else:
                ffn2[l] = plan_ffn(f"moe{l}", d["moe_w1_2"][0], d["moe_w3_2"][0], d["moe_w2_2"][0], NE2, NB2, 1)
            project(f"ple_g{l}", d["ple_gate_w_2"][l], KC, D, 512, ["act"])
            project(f"ple_p{l}", d["ple_proj_w_2"][l], PLE // P, D, D, ["dve"])
            n_units_3[l] = len(units)

        stage_no = {"tensor": 0, "vector": 0, "scalar": 0, "gpsimd": 0}

        def end_stage(eng, name):
            stage_no[name] += 1
            eng.drain().then_inc(stage_done, 1)
            eng.wait_ge(stage_done, 4 * stage_no[name])

        steps = {"dve": 0, "act": 0}

        def vstep(dve, ins):
            steps["dve"] += 1
            ins.then_inc(dve_step, 1)
            dve.wait_ge(dve_step, steps["dve"])

        def astep(act, ins):
            steps["act"] += 1
            ins.then_inc(act_step, 1)
            act.wait_ge(act_step, steps["act"])

        def stream(sp, lot):
            for u in lot:
                if u.after:
                    sp.wait_ge(*u.after)
                for dst, src in u.copies:
                    sp.dma_start(dst, src).then_inc(slot_ready[u.slot], 16)

        def load_step(sp, f, slot, e, b):
            gu = ring[:, slot, 0:GU].rearrange("p (c k n) -> p c k n", c=KC, k=2)
            if isinstance(e, int):
                w1, w3, w2 = f.w1[e], f.w3[e], f.w2[e]
            else:
                w1 = f.w1[bass.ds(e, 1)].rearrange("a p c n -> (a p) c n")
                w3 = f.w3[bass.ds(e, 1)].rearrange("a p c n -> (a p) c n")
                w2 = f.w2[bass.ds(e, 1)].rearrange("a b p n -> (a b) p n")
            cols = slice(b * FB, b * FB + FB) if isinstance(b, int) else bass.ds(b * FB, FB)
            down = w2[b] if isinstance(b, int) else w2[bass.ds(b, 1)].rearrange("a p n -> (a p) n")
            sp.dma_start(gu[:, :, 0, :], w1[:, :, cols]).then_inc(slot_ready[slot], 16)
            sp.dma_start(gu[:, :, 1, :], w3[:, :, cols]).then_inc(slot_ready[slot], 16)
            sp.dma_start(ring[:, slot, GU:SLOT], down).then_inc(slot_ready[slot], 16)

        def rounds(f):
            if f.e == 1:
                return 0, 0, 1
            g = f.group
            return g, f.e // g, f.e % g

        def stream_ffn(sp, f):
            def one(e, b, k, g_index):
                slot = k % SLOTS
                if isinstance(g_index, int) and g_index == 0 and k < SLOTS:
                    if f.free0[slot]:
                        sp.wait_ge(*f.free0[slot])
                else:
                    prev = k - SLOTS
                    if prev < 0:
                        last = max(q for q in range(f.group * f.nb) if q % SLOTS == slot)
                        prev = last - f.group * f.nb
                    sp.wait_ge(ffn_used, f.step0 + g_index * (f.group * f.nb) + prev + 1)
                load_step(sp, f, slot, e, b)

            g, n, left = rounds(f)
            if n:
                for k in range(g * f.nb):
                    one(k // f.nb, k % f.nb, k, 0)
                with sp.Fori(1, n) as i:
                    for k in range(g * f.nb):
                        one(i * g + k // f.nb, k % f.nb, k, i)
            for k in range(left * f.nb):
                one(n * g + k // f.nb, k % f.nb, k, n)

        def pe_project(pe, name, xT):
            jobs = jobs_of[name]
            for q, j in enumerate(jobs):
                if j.first:
                    pe.wait_ge(slot_ready[j.unit.slot], j.unit.ready)
                if q >= 4:
                    p = jobs[q - 4]
                    pe.wait_ge(evac_act if p.engine == "act" else evac_dve, p.evac)
                kc = j.unit.view.shape[1]
                for c in range(kc):
                    mm = pe.matmul(ps[:, q % 4, 0:j.n], xT[:, c, j.tile * P:(j.tile + 1) * P],
                                   j.unit.view[:, c, j.off:j.off + j.n], start=(c == 0), stop=(c == kc - 1))
                mm.then_inc(proj_done, 1)

        def evacuate(eng, name, engine, copy):
            for q, j in enumerate(jobs_of[name]):
                if j.engine == engine:
                    eng.wait_ge(proj_done, j.index + 1)
                    copy(j, ps[:, q % 4, 0:j.n]).then_inc(evac_act if engine == "act" else evac_dve, 1)

        nt_xn = arena[:, 0:NT * D].rearrange("p (t n) -> p t n", t=NT)
        nt_sq = arena[:, NT * D:NT * D + D]

        def pe_transpose_x(pe, src, kc, n, ready, value):
            pe.wait_ge(ready, value)
            for c in range(kc):
                for t in range(NT):
                    mm = pe.transpose(ps[:, c // 2, (c % 2) * S + t * P:(c % 2) * S + (t + 1) * P],
                                      src[:, t, c::kc], ident[:])
                mm.then_inc(sig("xT_psum"), 1)

        def pe_norm(pe, n):
            pe_transpose_x(pe, nt_xn, KC, n, sig("norm_xn"), n + 1)

        def evac_norm(eng, engine, base, gain, kc=KC):
            for b in range(0 if engine == "act" else 1, kc // 2, 2):
                eng.wait_ge(sig("xT_psum"), base + 2 * b + 2)
                for c in (2 * b, 2 * b + 1):
                    src = ps[:, b, (c % 2) * S:(c % 2 + 1) * S]
                    if engine == "act":
                        if gain is None:
                            eng.copy(hT[:, c, :], src)
                        else:
                            eng.activation(hT[:, c, :], src, ACT.Identity, scale=gain[:, c:c + 1])
                    elif gain is None:
                        eng.tensor_copy(hT[:, c, :], src)
                    else:
                        eng.tensor_scalar(hT[:, c, :], src, gain[:, c:c + 1], None, ALU.mult)

        def act_norm_stats(act, n):
            for t in range(NT):
                ins = act.activation(nt_sq, x[:, t, :], ACT.Square, accum_out=small[:, t:t + 1])
                if t + 1 < NT:
                    astep(act, ins)
            ins.then_inc(sig("norm_sq"), 1)
            act.wait_ge(sig("norm_ms"), n + 1)
            act.activation(small[:, 4:6], small[:, 2:4], ACT.Sqrt).then_inc(sig("norm_rt"), 1)

        def dve_norm_scale(dve, n, dst):
            dve.wait_ge(sig("norm_sq"), n + 1)
            dve.tensor_scalar(small[:, 2:4], small[:, 0:2], 1.0 / D, EPS, ALU.mult, ALU.add).then_inc(sig("norm_ms"), 1)
            dve.wait_ge(sig("norm_rt"), n + 1)
            vstep(dve, dve.reciprocal(small[:, 6:8], small[:, 4:6]))
            for t in range(NT):
                ins = dve.tensor_scalar(dst[:, t, :], x[:, t, :], small[:, 6 + t:7 + t], None, ALU.mult)
            return ins

        XT_ORDER, XT_AT = [], {}

        def xt(name, kc):
            XT_AT[name] = sum(k for _, k in XT_ORDER)
            XT_ORDER.append((name, kc))

        xt("n1", KC), xt("ym", KC), xt("n2", KC)
        for l in range(LAYERS):
            xt(f"mix{l}", KC), xt(f"cat{l}", KC), xt(f"ffn{l}", KC), xt(f"ple{l}", KC)
        NORMS = ["n1", "n2"] + [f"{k}{l}" for l in range(LAYERS) for k in ("mix", "ffn", "ple")] + ["final"]

        def stage_norm(name, gain):
            n = NORMS.index(name)

            def pe_(pe):
                pe_norm(pe, n)
                end_stage(pe, "tensor")

            def act_(act):
                act_norm_stats(act, n)
                evac_norm(act, "act", XT_AT[name], gain)
                end_stage(act, "scalar")

            def dve_(dve):
                dve_norm_scale(dve, n, nt_xn).then_inc(sig("norm_xn"), 1)
                evac_norm(dve, "dve", XT_AT[name], gain)
                end_stage(dve, "vector")

            def pool_(pool):
                end_stage(pool, "gpsimd")

            return pe_, act_, dve_, pool_

        def stage_turn(name, src):
            def pe_(pe):
                for c in range(KC):
                    for t in range(NT):
                        mm = pe.transpose(ps[:, c // 2, (c % 2) * S + t * P:(c % 2) * S + (t + 1) * P],
                                          src[:, t, c::KC], ident[:])
                    mm.then_inc(sig("xT_psum"), 1)
                end_stage(pe, "tensor")

            def act_(act):
                evac_norm(act, "act", XT_AT[name], None)
                end_stage(act, "scalar")

            def dve_(dve):
                evac_norm(dve, "dve", XT_AT[name], None)
                end_stage(dve, "vector")

            def pool_(pool):
                end_stage(pool, "gpsimd")

            return pe_, act_, dve_, pool_

        def stage_project(name, xT, act_copy=None, dve_copy=None, act_more=None, dve_more=None):
            def pe_(pe):
                pe_project(pe, name, xT)
                end_stage(pe, "tensor")

            def act_(act):
                if act_copy:
                    evacuate(act, name, "act", lambda j, src: act_copy(act, j, src))
                if act_more:
                    act_more(act)
                end_stage(act, "scalar")

            def dve_(dve):
                if dve_copy:
                    evacuate(dve, name, "dve", lambda j, src: dve_copy(dve, j, src))
                if dve_more:
                    dve_more(dve)
                end_stage(dve, "vector")

            def pool_(pool):
                end_stage(pool, "gpsimd")

            return pe_, act_, dve_, pool_

        P1_LOADS = [
            (gla_bT[:], d["b_gla_a"][0].rearrange("(h p) -> p h", p=P)),
            (gla_og[:], d["gla_out_norm_g"].to_broadcast([P, GD])),
            (gla_a2[:], d["w_gla_a2"][0]),
            (dil_gT[:, 0, :], d["dil_q_norm_g"][0].rearrange("g p -> p g")),
            (dil_gT[:, 1, :], d["dil_k_norm_g"][0].rearrange("g p -> p g")),
            (g2T[:], d["norm2_g"][0].rearrange("(p c) -> p c", c=KC)),
            (r1_w[:, :, 0:N_GROUPS], d["w_router_group"][0].rearrange("(p c) n -> p c n", c=KC)),
            (r1_w[:, :, N_GROUPS:36], d["w_router_expert"][0].rearrange("(p c) n -> p c n", c=KC)),
            (r1_b[:, 0:N_GROUPS], d["b_router_group"].to_broadcast([P, N_GROUPS])),
            (r1_b[:, N_GROUPS:36], d["b_router_expert"].to_broadcast([P, NE1])),
            (pos_i[:], d["positions_2"][0].rearrange("(t p) -> p t", p=P)),
            (r2_w[:], d["router_w_2"][0].rearrange("(p c) n -> p c n", c=KC)),
            (r2_b[:], d["router_b_2"].to_broadcast([P, NE2])),
        ]
        for l in range(LAYERS):
            for k, g in enumerate(("g_mix_2", "g_ffn_2", "g_ple_2")):
                P1_LOADS.append((l_gT[:, 3 * l + k, :], d[g][l].rearrange("(p c) -> p c", c=KC)))

        def layer_loads(l):
            lot = [(l_mu[:], d["rw_mu_2"][l:l + 1].to_broadcast([P, 1024]))]
            for k, n in enumerate(("rw_w0_2", "rw_a0_2", "rw_k_k_2", "rw_k_a_2", "rw_r_k_2", "rw_gn_g_2", "rw_gn_b_2",
                                   "gm_ln_g_2", "gm_ln_b_2")):
                src = d[n][l:l + 1]
                if len(src.shape) == 3:
                    src = src.rearrange("a h n -> a (h n)")
                lot.append((l_row[:, k, :], src.to_broadcast([P, 256])))
            lot += [(l_bsT[:], d["gm_bs_2"][l].rearrange("h p -> p h")),
                    (l_lora[0:64, 0, :], d["rw_w_up_2"][l]),
                    (l_lora[64:128, 0, :], d["rw_a_up_2"][l]),
                    (l_lora[:, 1, :], d["rw_g_up_2"][l]),
                    (l_ws[:], d["gm_ws_2"][l].rearrange("h t s -> t h s")),
                    (l_posT[0:64, :], d["nsa_cmp_pos_2"][l].rearrange("(i k) n -> k n i", k=2)[0]),
                    (l_posT[64:128, :], d["nsa_cmp_pos_2"][l].rearrange("(i k) n -> k n i", k=2)[1]),
                    (l_w2[:, 0, :], d["nsa_kc_w2_2"][l]),
                    (l_w2[:, 1, :], d["nsa_kc_w2_2"][l]),
                    (l_w2[:, 2, :], d["nsa_vc_w2_2"][l])]
            return lot

        N_LAYER_LOADS = len(layer_loads(0))

        def load_layer(act, l):
            for dst, src in layer_loads(l):
                act.dma_start(dst, src).then_inc(sig("layer_params"), 16)

        MI = Arena(arena)
        MI.at = NT * D + D
        m_row, m_col, m_xor = [MI.take(S).bitcast(I32) for _ in range(3)]
        m_rowf, m_colf, m_t, m_u = [MI.take(S) for _ in range(4)]
        m_b16 = MI.take(NCH)
        m_half = MI.take(2)
        m_cmp = MI.take(NT, 16)
        m_i16 = MI.take(64).bitcast(I32)
        m_half_i = m_i16[:, 16:18]
        m_cmp_i = m_i16[:, 18:50].rearrange("p (t n) -> p t n", t=NT)
        m_desc_i = MI.take(32).bitcast(I32)

        def setup_pool(pool):
            pool.iota(m_row, [[0, S]], base=0, channel_multiplier=1)
            pool.iota(m_col, [[1, S]], base=0, channel_multiplier=0)
            pool.iota(m_i16[:, 0:NCH], [[-GCH, NCH]], base=0, channel_multiplier=1)
            pool.iota(m_half_i, [[-RC, 2]], base=0, channel_multiplier=1)
            for t in range(NT):
                pool.iota(m_cmp_i[:, t, :], [[-CST, 16]], base=t * P - (CB - 1), channel_multiplier=1)
            pool.iota(m_desc_i, [[-1, 32]], base=32, channel_multiplier=0).then_inc(sig("iota_done"), 1)
            end_stage(pool, "gpsimd")

        def setup_act(act):
            act.dma_start(x[:], d["x"][0].rearrange("(t p) n -> p t n", p=P)).then_inc(sig("x_ready"), 16)
            act.dma_start(g1T[:], d["norm1_g"][0].rearrange("(p c) -> p c", c=KC)).then_inc(sig("x_ready"), 16)
            for dst, src in P1_LOADS:
                act.dma_start(dst, src).then_inc(sig("params"), 16)
            load_layer(act, 0)
            act.wait_ge(sig("x_ready"), 32)
            end_stage(act, "scalar")

        def setup_dve(dve):
            dve.wait_ge(sig("iota_done"), 1)
            dve.tensor_copy(m_rowf, m_row)
            vstep(dve, dve.tensor_copy(m_colf, m_col))
            vstep(dve, dve.tensor_tensor(diff[:], m_colf[:, 0:P], m_rowf[:, 0:P], ALU.subtract))
            vstep(dve, dve.tensor_scalar(ident[:], diff[:], 0.0, None, ALU.is_equal))
            end_stage(dve, "vector")

        def setup_pe(pe):
            end_stage(pe, "tensor")

        def masks_dve(dve):
            dve.tensor_tensor(m_xor[:, 0:P], m_row[:, 0:P], m_col[:, 0:P], ALU.bitwise_xor)
            vstep(dve, dve.tensor_tensor(negdist[:], m_colf, m_rowf, ALU.subtract))
            vstep(dve, dve.tensor_copy(xor_f[:], m_xor[:, 0:P]))
            vstep(dve, dve.tensor_copy(m_xor, negdist[:]))
            dve.tensor_scalar(same_chunk[:], xor_f[:], float(RC), None, ALU.is_lt)
            dve.tensor_scalar(gla_mask[:], xor_f[:], float(GCH), None, ALU.is_lt)
            dve.tensor_scalar(causal_up[:], diff[:], 0.0, None, ALU.is_ge)
            dve.tensor_scalar(m_u[:, 0:P], diff[:], 0.0, None, ALU.is_lt)
            dve.tensor_scalar(m_u[:, P:S], diff[:], 0.0, None, ALU.is_gt)
            dve.tensor_scalar(shift_dn_edge[:], diff[:], float(1 - P), None, ALU.is_equal)
            dve.tensor_scalar(shift_up[:], diff[:], -1.0, None, ALU.is_equal)
            dve.tensor_scalar(shift_up_edge[:], diff[:], float(P - 1), None, ALU.is_equal)
            vstep(dve, dve.tensor_scalar(shift_dn[:], diff[:], 1.0, None, ALU.is_equal))
            dve.tensor_tensor(shift_dn[:], shift_dn[:], ident[:], ALU.subtract)
            dve.tensor_tensor(tri_inc[:], causal_up[:], same_chunk[:], ALU.mult)
            dve.tensor_tensor(tri_str[:], m_u[:, P:S], same_chunk[:], ALU.mult)
            vstep(dve, dve.tensor_tensor(gla_mask[:], gla_mask[:], causal_up[:], ALU.mult))
            for k in range(6):
                b = float(1 << k)
                dve.scalar_tensor_tensor(out=low_b[:, k, :], in0=xor_f[:], scalar=b, in1=m_u[:, 0:P],
                                         op0=ALU.is_ge, op1=ALU.mult)
                vstep(dve, dve.scalar_tensor_tensor(out=up_b[:, k, :], in0=xor_f[:], scalar=b, in1=m_u[:, P:S],
                                                    op0=ALU.is_ge, op1=ALU.mult))
                dve.scalar_tensor_tensor(out=low_b[:, k, :], in0=xor_f[:], scalar=2 * b, in1=low_b[:, k, :],
                                         op0=ALU.is_lt, op1=ALU.mult)
                vstep(dve, dve.scalar_tensor_tensor(out=up_b[:, k, :], in0=xor_f[:], scalar=2 * b, in1=up_b[:, k, :],
                                                    op0=ALU.is_lt, op1=ALU.mult))
            vstep(dve, dve.tensor_scalar(negdist[:], negdist[:], float(-P), None, ALU.add))
            vstep(dve, dve.tensor_scalar(m_t, negdist[:], 0.0, None, ALU.is_le))
            dve.tensor_scalar(causal_neg[:], m_t, BIG, -BIG, ALU.mult, ALU.add)
            vstep(dve, dve.scalar_tensor_tensor(out=dil_mask[:, 0, :], in0=negdist[:], scalar=-128.0, in1=m_t,
                                                op0=ALU.is_ge, op1=ALU.mult))
            for g, r in ((1, 4), (2, 16)):
                vstep(dve, dve.tensor_scalar(m_row, m_xor, r - 1, None, ALU.bitwise_and))
                vstep(dve, dve.tensor_copy(m_rowf, m_row))
                vstep(dve, dve.scalar_tensor_tensor(out=dil_mask[:, g, :], in0=m_rowf, scalar=0.0, in1=m_t,
                                                    op0=ALU.is_equal, op1=ALU.mult))
            dve.tensor_scalar(dil_mask[:], dil_mask[:], BIG, -BIG, ALU.mult, ALU.add)
            vstep(dve, dve.tensor_scalar(m_row, m_col, GCH - 1, None, ALU.bitwise_and))
            vstep(dve, dve.tensor_copy(m_rowf, m_row))
            dve.tensor_scalar(scan_keep[:], m_rowf, 0.0, None, ALU.not_equal)
            dve.tensor_copy(m_b16, m_i16[:, 0:NCH])
            dve.tensor_copy(m_half, m_half_i)
            vstep(dve, dve.tensor_copy(m_cmp, m_cmp_i))
            vstep(dve, dve.tensor_scalar(m_t[:, 0:NCH], m_b16, float(GCH), None, ALU.is_lt))
            dve.scalar_tensor_tensor(out=block16[:], in0=m_b16, scalar=0.0, in1=m_t[:, 0:NCH], op0=ALU.is_ge, op1=ALU.mult)
            vstep(dve, dve.tensor_scalar(m_t[:, 16:18], m_half, float(RC), None, ALU.is_lt))
            dve.scalar_tensor_tensor(out=half_ind[:], in0=m_half, scalar=0.0, in1=m_t[:, 16:18], op0=ALU.is_ge, op1=ALU.mult)
            vstep(dve, dve.tensor_scalar(cmp_ok[:], m_cmp, 0.0, None, ALU.is_ge))
            dve.tensor_scalar(cmp_neg[:], cmp_ok[:], BIG, -BIG, ALU.mult, ALU.add)
            dve.tensor_copy(desc[:], m_desc_i)
            dve.memset(ones[:], 1.0)
            for k in range(ROPE_HALF):
                dve.memset(freq[:, k:k + 1], INV_FREQ[k])

        B1 = Arena(arena)
        ogT = B1.take(GW // P, S)
        oaT = B1.take(GW // P, S)
        b1_at = B1.at
        MA = Arena(arena)
        MA.at = b1_at
        g_qT, g_kT = MA.take(GH, S), MA.take(GH, S)
        g_lrT = MA.take(S)
        g_y, g_a, g_b, g_c = [MA.take(GH, S) for _ in range(4)]
        g_att = MA.take(GH * NT, P)
        g_ke = MA.take(GH * NT, P)
        g_vm = MA.take(2, NCH, GD)
        g_st = MA.take(NT, NCH, GD)
        g_dec = MA.take(GH, S // GCH)
        za = MA.take(NT, ZA)
        g_oT = g_a
        g_otok = g_b.rearrange("p h s -> p (h s)").rearrange("p (t h v) -> p t h v", t=NT, h=GH)
        g_sq = g_c.rearrange("p h s -> p (h s)").rearrange("p (t h v) -> p t h v", t=NT, h=GH)
        g_sil = g_y.rearrange("p h s -> p (h s)").rearrange("p (t h v) -> p t h v", t=NT, h=GH)
        COMBOS = [(h, t) for h in range(GH) for t in range(NT)]

        def flat(ap):
            return ap.rearrange("p a b -> p (a b)")

        def gla_pe(pe):
            for k, c0 in ((0, 0), (2, GW)):
                for h in range(GH):
                    for t in range(NT):
                        mm = pe.transpose(ps[:, k + h // 2, (h % 2) * S + t * P:(h % 2) * S + (t + 1) * P],
                                          za[:, t, c0 + h * GD:c0 + (h + 1) * GD], ident[:])
                mm.then_inc(sig("gla_turned"), 1)
            for t in range(NT):
                mm = pe.transpose(ps[0:RANK, 4, t * P:(t + 1) * P], za[:, t, 4 * GW:ZA], ident[:])
            mm.then_inc(sig("gla_turned"), 1)
            pe.wait_ge(sig("gla_lr"), 1)
            for h in range(GH):
                mm = pe.matmul(ps[:, 5 + h // 2, (h % 2) * S:(h % 2 + 1) * S], gla_a2[:, h * GD:(h + 1) * GD],
                               g_lrT[0:RANK, :], start=True, stop=True)
            mm.then_inc(sig("gla_logit"), 1)
            pe.wait_ge(sig("gla_scaled"), 1)
            for k, (h, t) in enumerate(COMBOS):
                mm = pe.matmul(ps[:, k // 4, (k % 4) * P:(k % 4 + 1) * P], g_kT[:, h, t * P:(t + 1) * P],
                               g_qT[:, h, t * P:(t + 1) * P], start=True, stop=True)
            mm.then_inc(sig("gla_scores"), 1)
            for k, (h, t) in enumerate(COMBOS):
                mm = pe.transpose(ps[:, 2 + k // 4, (k % 4) * P:(k % 4 + 1) * P], g_y[:, h, t * P:(t + 1) * P], ident[:])
            mm.then_inc(sig("gla_ke_turned"), 1)
            pe.wait_ge(sig("gla_att"), 1)
            pe.wait_ge(sig("gla_ke"), 1)

            def kv(k):
                pe.wait_ge(sig("gla_vm"), k + 1)
                if k >= 2:
                    pe.wait_ge(sig("gla_kv_used"), k - 1)
                vm = g_vm[:, k % 2].rearrange("p n v -> p (n v)")
                for b in range(2):
                    mm = pe.matmul(ps[:, 2 * (k % 2) + b, :], g_ke[:, k, :], vm[:, b * 512:(b + 1) * 512],
                                   start=True, stop=True)
                mm.then_inc(sig("gla_kv"), 1)

            kv(0)
            for k, (h, t) in enumerate(COMBOS):
                if k + 1 < len(COMBOS):
                    kv(k + 1)
                oT = ps[:, 4 + k // 4, (k % 4) * P:(k % 4 + 1) * P]
                pe.matmul(oT, za[:, t, 2 * GW + h * GD:2 * GW + (h + 1) * GD], g_att[:, k, :], start=True, stop=False)
                pe.wait_ge(sig("gla_state"), k + 1)
                for n in range(NCH):
                    if t == 0 and n == 0:
                        continue
                    mm = pe.matmul(oT[:, n * GCH:(n + 1) * GCH], g_st[:, t, n, :],
                                   g_qT[:, h, t * P + n * GCH:t * P + (n + 1) * GCH], start=False, stop=(n == NCH - 1))
                mm.then_inc(sig("gla_o"), 1)
            pe.wait_ge(sig("gla_oT"), 1)
            for k, (h, t) in enumerate(COMBOS):
                mm = pe.transpose(ps[:, 6 + t, h * GD:(h + 1) * GD], g_oT.rearrange("p h s -> p (h s)")[:, k * P:(k + 1) * P],
                                  ident[:])
            mm.then_inc(sig("gla_o_turned"), 1)
            pe.wait_ge(sig("gla_gated"), 1)
            for c in range(GW // P):
                for t in range(NT):
                    mm = pe.transpose(ps[:, c // 2, (c % 2) * S + t * P:(c % 2) * S + (t + 1) * P],
                                      g_otok[:, t].rearrange("p h v -> p (h v)")[:, c::GW // P], ident[:])
            mm.then_inc(sig("gla_out"), 1)
            end_stage(pe, "tensor")

        def gla_act(act):
            act.wait_ge(sig("gla_turned"), 1)
            act.mul(flat(g_qT), ps[:, 0:2, :].rearrange("p a b -> p (a b)"), float(GD) ** -0.5)
            act.wait_ge(sig("gla_turned"), 3)
            act.copy(g_lrT[0:RANK, :], ps[0:RANK, 4, 0:S]).then_inc(sig("gla_lr"), 1)
            act.wait_ge(sig("gla_y"), 1)
            astep(act, act.activation(flat(g_a), flat(g_y), ACT.Abs))
            astep(act, act.activation(flat(g_a), flat(g_a), ACT.Exp, scale=-1.0))
            act.activation(flat(g_a), flat(g_a), ACT.Ln, bias=1.0).then_inc(sig("gla_ln"), 1)
            act.wait_ge(sig("gla_cum"), 1)
            act.activation(flat(g_b), flat(g_a), ACT.Exp, scale=1.0 / TAU).then_inc(sig("gla_exp"), 1)
            act.activation(flat(g_c), flat(g_a), ACT.Exp, scale=-1.0 / TAU).then_inc(sig("gla_exp"), 1)
            act.wait_ge(sig("gla_cum"), 2)
            act.activation(flat(g_y), flat(g_y), ACT.Exp, scale=1.0 / TAU).then_inc(sig("gla_exp"), 1)
            act.wait_ge(sig("gla_ke_turned"), 1)
            act.copy(flat(g_ke), ps[:, 2:4, :].rearrange("p a b -> p (a b)")).then_inc(sig("gla_ke"), 1)
            act.wait_ge(sig("gla_o"), len(COMBOS))
            act.copy(flat(g_oT), ps[:, 4:6, :].rearrange("p a b -> p (a b)")).then_inc(sig("gla_oT"), 1)
            act.activation(g_sil.rearrange("p t h v -> p t (h v)"), za[:, :, 3 * GW:4 * GW], ACT.Silu).then_inc(sig("gla_silu"), 1)
            act.wait_ge(sig("gla_o_turned"), 1)
            act.copy(g_otok.rearrange("p t h v -> p (t h v)"), ps[:, 6:8, :].rearrange("p a b -> p (a b)"))
            act.activation(g_sq.rearrange("p t h v -> p (t h v)"), ps[:, 6:8, :].rearrange("p a b -> p (a b)"),
                           ACT.Square).then_inc(sig("gla_sq"), 1)
            act.wait_ge(sig("gla_ms"), 1)
            act.activation(small[:, 16:24], small[:, 8:16], ACT.Sqrt).then_inc(sig("gla_rt"), 1)
            act.wait_ge(sig("gla_out"), 1)
            act.copy(flat(ogT), ps[:, 0:2, :].rearrange("p a b -> p (a b)"))
            end_stage(act, "scalar")

        def gla_dve(dve):
            dve.wait_ge(sig("gla_turned"), 2)
            dve.tensor_copy(flat(g_kT), ps[:, 2:4, :].rearrange("p a b -> p (a b)"))
            dve.wait_ge(sig("gla_logit"), 1)
            for h in range(GH):
                ins = dve.tensor_scalar(g_y[:, h, :], ps[:, 5 + h // 2, (h % 2) * S:(h % 2 + 1) * S], gla_bT[:, h:h + 1],
                                        None, ALU.add)
            ins.then_inc(sig("gla_y"), 1)
            dve.wait_ge(sig("gla_ln"), 1)
            vstep(dve, dve.scalar_tensor_tensor(out=flat(g_y), in0=flat(g_y), scalar=0.0, in1=flat(g_a), op0=ALU.min,
                                                op1=ALU.subtract))
            for h in range(GH):
                ins = dve.tensor_tensor_scan(g_a[:, h, :], scan_keep[:], g_y[:, h, :], 0.0, ALU.mult, ALU.add)
            ins.then_inc(sig("gla_cum"), 1)
            dve.wait_ge(sig("gla_cum"), 1)
            a4 = g_a.rearrange("p h (n i) -> p (h n) i", i=GCH)
            y4 = g_y.rearrange("p h (n i) -> p (h n) i", i=GCH)
            dve.tensor_tensor(y4, a4[:, :, GCH - 1:GCH].to_broadcast([P, GH * S // GCH, GCH]), a4,
                              ALU.subtract).then_inc(sig("gla_cum"), 1)
            dve.wait_ge(sig("gla_exp"), 3)
            b4 = g_b.rearrange("p h (n i) -> p h n i", i=GCH)
            dve.tensor_copy(g_dec, b4[:, :, :, GCH - 1])
            dve.tensor_tensor(flat(g_qT), flat(g_qT), flat(g_b), ALU.mult)
            vstep(dve, dve.tensor_tensor(flat(g_y), flat(g_y), flat(g_kT), ALU.mult))
            dve.tensor_tensor(flat(g_kT), flat(g_kT), flat(g_c), ALU.mult).then_inc(sig("gla_scaled"), 1)
            dve.wait_ge(sig("gla_scores"), 1)
            dve.tensor_tensor(g_att, ps[:, 0:2, :].rearrange("p a (b n) -> p (a b) n", n=P),
                              gla_mask[:].unsqueeze(1).to_broadcast([P, GH * NT, P]), ALU.mult).then_inc(sig("gla_att"), 1)
            for k, (h, t) in enumerate(COMBOS):
                dve.wait_ge(sig("gla_kv"), k + 1)
                if k >= 2:
                    dve.wait_ge(sig("gla_o"), k - 1)
                for n in range(NCH):
                    add = ps[:, 2 * (k % 2) + n // 4, (n % 4) * GD:(n % 4 + 1) * GD]
                    last = n == NCH - 1
                    if last and t == NT - 1:
                        dve.drain().then_inc(sig("gla_state"), 1)
                        continue
                    dst = g_st[:, t + 1, 0, :] if last else g_st[:, t, n + 1, :]
                    if last:
                        if k >= 1:
                            dve.wait_ge(sig("gla_o"), k)
                        dve.drain().then_inc(sig("gla_state"), 1)
                    if t == 0 and n == 0:
                        ins = dve.tensor_copy(dst, add)
                    else:
                        ins = dve.scalar_tensor_tensor(out=dst, in0=g_st[:, t, n, :],
                                                       scalar=g_dec[:, h, t * NCH + n:t * NCH + n + 1],
                                                       in1=add, op0=ALU.mult, op1=ALU.add)
                    vstep(dve, ins)
                dve.drain().then_inc(sig("gla_kv_used"), 1)
            dve.wait_ge(sig("gla_sq"), 1)
            vstep(dve, dve.tensor_reduce(small[:, 0:8], g_sq.rearrange("p t h v -> p (t h) v"), AX, ALU.add))
            dve.tensor_scalar(small[:, 8:16], small[:, 0:8], 1.0 / GD, EPS, ALU.mult, ALU.add).then_inc(sig("gla_ms"), 1)
            dve.wait_ge(sig("gla_rt"), 1)
            vstep(dve, dve.reciprocal(small[:, 24:32], small[:, 16:24]))
            o8 = g_otok.rearrange("p t h v -> p (t h) v")
            vstep(dve, dve.tensor_tensor(o8, o8, small[:, 24:32].unsqueeze(2).to_broadcast([P, NT * GH, GD]), ALU.mult))
            vstep(dve, dve.tensor_tensor(o8, o8, gla_og[:].unsqueeze(1).to_broadcast([P, NT * GH, GD]), ALU.mult))
            dve.wait_ge(sig("gla_silu"), 1)
            dve.tensor_tensor(o8, o8, g_sil.rearrange("p t h v -> p (t h) v"), ALU.mult).then_inc(sig("gla_gated"), 1)
            end_stage(dve, "vector")

        def gla_pool(pool):
            for k, (h, t) in enumerate(COMBOS):
                if k >= 2:
                    pool.wait_ge(sig("gla_kv"), k - 1)
                v = za[:, t, 2 * GW + h * GD:2 * GW + (h + 1) * GD]
                pool.tensor_tensor(g_vm[:, k % 2], v.unsqueeze(1).to_broadcast([P, NCH, GD]),
                                   block16[:].unsqueeze(2).to_broadcast([P, NCH, GD]), ALU.mult).then_inc(sig("gla_vm"), 1)
            end_stage(pool, "gpsimd")

        MB = Arena(arena)
        MB.at = b1_at
        zb = MB.take(NT, ZB)
        zb5 = zb.rearrange("p t (g k h e) -> p t g k h e", g=DG, k=3, h=DH)
        t_sq = MB.take(2 * DH, DD)
        t_qk = MB.take(DG, 2, S)
        t_s0 = MB.take(DG, P)
        t_s1 = MB.take(DG, S)
        t_pT = MB.take(9, P)
        t_o = MB.take(NT, GW)
        t_ss = MB.take(NT, DG, 2 * DH)
        t_rs = MB.take(NT, DG, 2 * DH)
        t_mx = MB.take(NT * DG)
        t_nm = MB.take(NT)
        t_den = MB.take(NT)
        t_rd = MB.take(NT)

        def qk_psum(g, k):
            return ps[:, ((0, 1), (2, 7))[k][g // 2], (g % 2) * S:(g % 2 + 1) * S]

        def dil_pe(pe):
            pe.wait_ge(sig("dil_normed"), 1)
            for h in range(DH):
                if h >= 1:
                    pe.wait_ge(sig("dil_pT"), h)
                for g in range(DG):
                    for k in range(2):
                        for t in range(NT):
                            mm = pe.transpose(qk_psum(g, k)[:, t * P:(t + 1) * P], zb5[:, t, g, k, h, :], ident[:])
                mm.then_inc(sig("dil_turned"), 1)
                pe.wait_ge(sig("dil_qT"), h + 1)
                pe.wait_ge(sig("dil_kT"), h + 1)
                if h >= 1:
                    pe.wait_ge(sig("dil_max"), h)
                for g in range(DG):
                    pe.matmul(ps[:, 3, g * P:(g + 1) * P], t_qk[:, g, 0, 0:P], t_qk[:, g, 1, 0:P], start=True, stop=True)
                for g in range(DG):
                    mm = pe.matmul(ps[:, 4 + g // 2, (g % 2) * S:(g % 2 + 1) * S], t_qk[:, g, 0, P:S], t_qk[:, g, 1, :],
                                   start=True, stop=True)
                mm.then_inc(sig("dil_scores"), 1)
                pe.wait_ge(sig("dil_probs"), h + 1)
                for g in range(DG):
                    pe.transpose(ps[:, 0, g * P:(g + 1) * P], t_s0[:, g, :], ident[:])
                for g in range(DG):
                    for b in range(2):
                        q = 2 * g + b
                        mm = pe.transpose(ps[:, 1 + q // 4, (q % 4) * P:(q % 4 + 1) * P], t_s1[:, g, b * P:(b + 1) * P], ident[:])
                mm.then_inc(sig("dil_pturned"), 1)
                pe.wait_ge(sig("dil_pT"), h + 1)
                if h >= 1:
                    pe.wait_ge(sig("dil_o"), h)
                for g in range(DG):
                    pe.matmul(ps[:, 6, 0:DD], t_pT[:, g, :], zb5[:, 0, g, 2, h, :], start=(g == 0), stop=(g == DG - 1))
                for g in range(DG):
                    for b in range(2):
                        mm = pe.matmul(ps[:, 6, DD:2 * DD], t_pT[:, 3 + 2 * g + b, :], zb5[:, b, g, 2, h, :],
                                       start=(g == 0 and b == 0), stop=(g == DG - 1 and b == 1))
                mm.then_inc(sig("dil_pv"), 1)
            pe.wait_ge(sig("dil_o"), DH)
            for c in range(GW // P):
                for t in range(NT):
                    mm = pe.transpose(ps[:, c // 2, (c % 2) * S + t * P:(c % 2) * S + (t + 1) * P],
                                      t_o[:, t, c::GW // P], ident[:])
            mm.then_inc(sig("dil_out"), 1)
            end_stage(pe, "tensor")

        def dil_act(act):
            act.wait_ge(sig("dil_ms"), 1)
            act.activation(t_rs.rearrange("p t g k -> p (t g k)"), t_ss.rearrange("p t g k -> p (t g k)"),
                           ACT.Sqrt).then_inc(sig("dil_rt"), 1)
            for h in range(DH):
                act.wait_ge(sig("dil_turned"), h + 1)
                if h >= 1:
                    act.wait_ge(sig("dil_scores"), h)
                for g in range(DG):
                    ins = act.activation(t_qk[:, g, 0, :], qk_psum(g, 0), ACT.Identity, scale=dil_gT[:, 0, g:g + 1])
                ins.then_inc(sig("dil_qT"), 1)
                act.wait_ge(sig("dil_max"), h + 1)
                act.activation(t_s0, t_s0, ACT.Exp, bias=t_nm[:, 0:1], accum_out=t_den[:, 0:1])
                act.activation(t_s1, t_s1, ACT.Exp, bias=t_nm[:, 1:2], accum_out=t_den[:, 1:2]).then_inc(sig("dil_probs"), 1)
                act.wait_ge(sig("dil_pturned"), h + 1)
                act.copy(t_pT[:, 0:3, :], ps[:, 0, 0:3 * P].rearrange("p (g n) -> p g n", n=P))
                act.copy(t_pT[:, 3:9, :].rearrange("p g n -> p (g n)"),
                         ps[:, 1:3, :].rearrange("p a b -> p (a b)")[:, 0:6 * P]).then_inc(sig("dil_pT"), 1)
            act.wait_ge(sig("dil_out"), 1)
            act.copy(flat(oaT), ps[:, 0:2, :].rearrange("p a b -> p (a b)"))
            end_stage(act, "scalar")

        def dil_dve(dve):
            for t in range(NT):
                for g in range(DG):
                    qk = zb5[:, t, g, 0:2].rearrange("p k h e -> p (k h) e")
                    vstep(dve, dve.tensor_tensor(t_sq, qk, qk, ALU.mult))
                    vstep(dve, dve.tensor_reduce(t_ss[:, t, g, :], t_sq, AX, ALU.add))
            ss, rs = [a.rearrange("p t g k -> p (t g k)") for a in (t_ss, t_rs)]
            dve.tensor_scalar(ss, ss, 1.0 / DD, EPS, ALU.mult, ALU.add).then_inc(sig("dil_ms"), 1)
            dve.wait_ge(sig("dil_rt"), 1)
            vstep(dve, dve.reciprocal(ss, rs))
            dve.tensor_scalar(dil_gT[:, 0, :], dil_gT[:, 0, :], float(DD) ** -0.5, None, ALU.mult)
            for t in range(NT):
                for g in range(DG):
                    qk = zb5[:, t, g, 0:2].rearrange("p k h e -> p (k h) e")
                    ins = dve.tensor_tensor(qk, qk, t_ss[:, t, g, :].unsqueeze(2).to_broadcast([P, 2 * DH, DD]), ALU.mult)
            ins.then_inc(sig("dil_normed"), 1)
            for h in range(DH):
                dve.wait_ge(sig("dil_turned"), h + 1)
                if h >= 1:
                    dve.wait_ge(sig("dil_scores"), h)
                for g in range(DG):
                    ins = dve.tensor_scalar(t_qk[:, g, 1, :], qk_psum(g, 1), dil_gT[:, 1, g:g + 1], None, ALU.mult)
                ins.then_inc(sig("dil_kT"), 1)
                dve.wait_ge(sig("dil_scores"), h + 1)
                if h >= 1:
                    dve.wait_ge(sig("dil_pturned"), h)
                for g in range(DG):
                    sl = SLOPES[g * DH + h]
                    dve.scalar_tensor_tensor(out=t_s0[:, g, :], in0=negdist[:, P:S], scalar=sl,
                                             in1=ps[:, 3, g * P:(g + 1) * P], op0=ALU.mult, op1=ALU.add)
                    ins = dve.scalar_tensor_tensor(out=t_s1[:, g, :], in0=negdist[:], scalar=sl,
                                                   in1=ps[:, 4 + g // 2, (g % 2) * S:(g % 2 + 1) * S], op0=ALU.mult, op1=ALU.add)
                vstep(dve, ins)
                dve.tensor_tensor(t_s0, t_s0, dil_mask[:, :, P:S], ALU.add)
                vstep(dve, dve.tensor_tensor(t_s1, t_s1, dil_mask[:], ALU.add))
                dve.tensor_reduce(t_mx[:, 0:1], t_s0.rearrange("p g n -> p (g n)"), AX, ALU.max)
                vstep(dve, dve.tensor_reduce(t_mx[:, 1:2], t_s1.rearrange("p g n -> p (g n)"), AX, ALU.max))
                if h >= 1:
                    dve.wait_ge(sig("dil_probs"), h)
                dve.tensor_scalar(t_nm, t_mx[:, 0:2], -1.0, None, ALU.mult).then_inc(sig("dil_max"), 1)
                dve.wait_ge(sig("dil_probs"), h + 1)
                vstep(dve, dve.reciprocal(t_rd, t_den))
                dve.wait_ge(sig("dil_pv"), h + 1)
                for t in range(NT):
                    ins = dve.tensor_scalar(t_o[:, t, h * DD:(h + 1) * DD], ps[:, 6, t * DD:(t + 1) * DD], t_rd[:, t:t + 1],
                                            None, ALU.mult)
                ins.then_inc(sig("dil_o"), 1)
            end_stage(dve, "vector")

        def idle_pool(pool):
            end_stage(pool, "gpsimd")

        MC = Arena(arena)
        MC.at = b1_at
        c_bias = MC.take(2 * D)
        c_gate = MC.take(NT, 2 * D)
        c_y = MC.take(NT, D)
        c_t = MC.take(NT, D)

        def gates_copy(dve, j, src):
            return dve.tensor_tensor(c_gate[:, j.tile, j.col:j.col + j.n], src, c_bias[:, j.col:j.col + j.n], ALU.add)

        def y_gla_copy(dve, j, src):
            return dve.tensor_tensor(c_y[:, j.tile, j.col:j.col + j.n], src, c_gate[:, j.tile, j.col:j.col + j.n], ALU.mult)

        def y_att_copy(dve, j, src):
            return dve.tensor_tensor(c_t[:, j.tile, j.col:j.col + j.n], src,
                                     c_gate[:, j.tile, D + j.col:D + j.col + j.n], ALU.mult)

        def residual_copy(dve, j, src):
            cols = x[:, j.tile, j.col:j.col + j.n]
            return dve.tensor_tensor(cols, cols, src, ALU.add)

        MR = Arena(arena)
        MR.at = 8192
        r_log = MR.take(NT, 36)
        r_gs, r_oh1, r_oh2, r_em = MR.take(N_GROUPS), MR.take(32), MR.take(32), MR.take(32)
        r_c = MR.take(16)

        def router_pe(pe, w, n, nth):
            for t in range(NT):
                for c in range(KC):
                    mm = pe.matmul(ps[:, 4 + t, 0:n], hT[:, c, t * P:(t + 1) * P], w[:, c, :], start=(c == 0), stop=(c == KC - 1))
            mm.then_inc(sig("router_logits"), 1)
            end_stage(pe, "tensor")

        def first_max(dve, v, n, mx, tie, hot):
            vstep(dve, dve.tensor_reduce(mx, v, AX, ALU.max))
            vstep(dve, dve.tensor_scalar(hot, v, mx, None, ALU.is_equal))
            vstep(dve, dve.tensor_tensor(hot, hot, desc[:, 32 - n:32], ALU.mult))
            vstep(dve, dve.tensor_reduce(tie, hot, AX, ALU.max))
            vstep(dve, dve.tensor_scalar(hot, hot, tie, None, ALU.is_equal))

        def top_two(dve, v, n, gate, scale, turn):
            first_max(dve, v, n, r_c[:, 0:1], r_c[:, 1:2], r_oh1[:, 0:n])
            vstep(dve, dve.scalar_tensor_tensor(out=v, in0=r_oh1[:, 0:n], scalar=-4 * BIG, in1=v, op0=ALU.mult, op1=ALU.add))
            first_max(dve, v, n, r_c[:, 2:3], r_c[:, 3:4], r_oh2[:, 0:n])
            dve.tensor_tensor(r_c[:, 4:5], r_c[:, 2:3], r_c[:, 0:1], ALU.subtract).then_inc(sig("router_gap"), 1)
            dve.wait_ge(sig("router_exp"), turn)
            vstep(dve, dve.tensor_scalar(r_c[:, 6:7], r_c[:, 5:6], 1.0, None, ALU.add))
            vstep(dve, dve.reciprocal(r_c[:, 7:8], r_c[:, 6:7]))
            if scale is not None:
                vstep(dve, dve.tensor_tensor(r_c[:, 7:8], r_c[:, 7:8], scale, ALU.mult))
            vstep(dve, dve.tensor_tensor(r_c[:, 8:9], r_c[:, 7:8], r_c[:, 5:6], ALU.mult))
            vstep(dve, dve.tensor_scalar(gate, r_oh1[:, 0:n], r_c[:, 7:8], None, ALU.mult))
            vstep(dve, dve.scalar_tensor_tensor(out=gate, in0=r_oh2[:, 0:n], scalar=r_c[:, 8:9], in1=gate, op0=ALU.mult, op1=ALU.add))

        def router1_act(act):
            for t in range(NT):
                act.wait_ge(sig("router_group"), t + 1)
                act.activation(r_gs, r_log[:, t, 0:N_GROUPS], ACT.Exp, bias=r_c[:, 9:10], accum_out=r_c[:, 10:11])\
                    .then_inc(sig("router_gexp"), 1)
                act.wait_ge(sig("router_gap"), t + 1)
                act.activation(r_c[:, 5:6], r_c[:, 4:5], ACT.Exp).then_inc(sig("router_exp"), 1)
            end_stage(act, "scalar")

        def router1_dve(dve):
            dve.wait_ge(sig("router_logits"), 1)
            for t in range(NT):
                lg = r_log[:, t]
                vstep(dve, dve.tensor_tensor(lg, ps[:, 4 + t, 0:36], r1_b[:], ALU.add))
                hot = r_oh2[:, 0:N_GROUPS]
                first_max(dve, lg[:, 0:N_GROUPS], N_GROUPS, r_c[:, 11:12], r_c[:, 12:13], hot)
                dve.tensor_scalar(r_c[:, 9:10], r_c[:, 11:12], -1.0, None, ALU.mult).then_inc(sig("router_group"), 1)
                e8 = lg[:, N_GROUPS:36].rearrange("p (g k) -> p g k", g=N_GROUPS)
                m8 = r_em.rearrange("p (g k) -> p g k", g=N_GROUPS)
                vstep(dve, dve.tensor_tensor(m8, e8, hot.unsqueeze(2).to_broadcast([P, N_GROUPS, PER_GROUP]), ALU.mult))
                vstep(dve, dve.tensor_scalar(hot, hot, BIG, -BIG, ALU.mult, ALU.add))
                vstep(dve, dve.tensor_tensor(m8, m8, hot.unsqueeze(2).to_broadcast([P, N_GROUPS, PER_GROUP]), ALU.add))
                dve.wait_ge(sig("router_gexp"), t + 1)
                vstep(dve, dve.reciprocal(r_c[:, 13:14], r_c[:, 10:11]))
                top_two(dve, r_em, NE1, gate_w[:, t, :], r_c[:, 13:14], t + 1)
            end_stage(dve, "vector")

        def router2_act(act):
            for t in range(NT):
                act.wait_ge(sig("router_gap"), NT + t + 1)
                act.activation(r_c[:, 5:6], r_c[:, 4:5], ACT.Exp).then_inc(sig("router_exp"), 1)
            end_stage(act, "scalar")

        def router2_dve(dve):
            dve.wait_ge(sig("router_logits"), 2)
            for t in range(NT):
                vstep(dve, dve.tensor_tensor(r_log[:, t, 0:NE2], ps[:, 4 + t, 0:NE2], r2_b[:], ALU.add))
                top_two(dve, r_log[:, t, 0:NE2], NE2, gate_w[:, t, 0:NE2], None, NT + t + 1)
            end_stage(dve, "vector")

        MF = Arena(arena)
        f_sg = MF.take(NT, FB)
        f_hid = MF.take(NT, FB)
        f_hidT = MF.take(NT, FB // P, P)

        def ffn_lots(f):
            g, n, left = rounds(f)
            body = [(k, k // f.nb) for k in range(g * f.nb)]
            rest = [(k, k // f.nb) for k in range(left * f.nb)]
            return n, body, rest

        def ffn_run(eng, f, part):
            n, body, rest = ffn_lots(f)
            if n:
                with eng.Fori(0, n) as i:
                    part(eng, f, body, i)
            if rest:
                part(eng, f, rest, n)

        def step_of(f, k, g):
            return f.step0 + g * (f.group * f.nb) + k

        def ffn_pe_part(pe, f, lot, g):
            def turn(n, t):
                pe.wait_ge(sig("ffn_hid"), 2 * n + t + 3)
                pe.wait_ge(sig("ffn_hidT"), 2 * n + t + 1)
                for c in range(FB // P):
                    mm = pe.transpose(ps[:, 6 + t, c * P:(c + 1) * P], f_hid[:, t, c::FB // P], ident[:])
                mm.then_inc(sig("ffn_turned"), 1)

            def down(n, k, t):
                w = ring[:, k % SLOTS, GU:SLOT].rearrange("p (c n) -> p c n", c=FB // P)
                pe.wait_ge(sig("ffn_hidT"), 2 * n + t + 3)
                for c in range(FB // P):
                    for b in range(2):
                        mm = pe.matmul(ps[:, 2 * t + b, :], f_hidT[:, t, c, :], w[:, c, b * 512:(b + 1) * 512],
                                       start=False, stop=False, skip_group_check=True)
                if t == NT - 1:
                    mm.then_inc(ffn_used, 1)

            held = None
            for k, e in lot:
                n = step_of(f, k, g)
                s = k % SLOTS
                w = ring[:, s, 0:GU].rearrange("p (c n) -> p c n", c=KC)
                pe.wait_ge(slot_ready[s], f.ready0[s] + 48 * (g * f.fills[s] + k // SLOTS + 1))
                for t in range(NT):
                    pe.wait_ge(sig("ffn_hid"), 2 * n + t + 1)
                    for c in range(KC):
                        if c == KC - 2 and held:
                            turn(held[0], held[2])
                        mm = pe.matmul(ps[:, 4 + t, :], hT[:, c, t * P:(t + 1) * P], w[:, c, :],
                                       start=(c == 0), stop=(c == KC - 1))
                    mm.then_inc(sig("ffn_gu"), 1)
                    if held:
                        down(*held)
                    held = (n, k, t)
            turn(held[0], held[2])
            down(*held)

        def ffn_act_part(act, f, lot, g):
            for k, e in lot:
                n = step_of(f, k, g)
                for t in range(NT):
                    act.wait_ge(sig("ffn_gu"), 2 * n + t + 1)
                    act.activation(f_sg[:, t, :], ps[:, 4 + t, 0:FB], ACT.Silu).then_inc(sig("ffn_silu"), 1)

        def ffn_dve_part(dve, f, lot, g):
            def copy(n, t):
                dve.wait_ge(sig("ffn_turned"), 2 * n + t + 1)
                dve.tensor_copy(f_hidT[:, t].rearrange("p c n -> p (c n)"), ps[:, 6 + t, 0:FB]).then_inc(sig("ffn_hidT"), 1)

            held = None
            for k, e in lot:
                n = step_of(f, k, g)
                for t in range(NT):
                    if held:
                        copy(*held)
                    dve.wait_ge(sig("ffn_silu"), 2 * n + t + 1)
                    if f.e == 1:
                        gate = ones[:, 0:1]
                    elif isinstance(g, int):
                        gate = gate_w[:, t, g * f.group + e:g * f.group + e + 1]
                    else:
                        gate = gate_w[:, t, bass.ds(g * f.group + e, 1)]
                    dve.scalar_tensor_tensor(out=f_hid[:, t, :], in0=ps[:, 4 + t, FB:2 * FB], scalar=gate,
                                             in1=f_sg[:, t, :], op0=ALU.mult, op1=ALU.mult).then_inc(sig("ffn_hid"), 1)
                    held = (n, t)
            copy(*held)

        def stage_ffn(f, nth):
            def pe_(pe):
                for t in range(NT):
                    for b in range(2):
                        pe.matmul(ps[:, 2 * t + b, :], ident[:], x[:, t, b * 512:(b + 1) * 512], start=True, stop=False,
                                  skip_group_check=True)
                ffn_run(pe, f, ffn_pe_part)
                pe.drain().then_inc(sig("ffn_end"), 1)
                end_stage(pe, "tensor")

            def act_(act):
                ffn_run(act, f, ffn_act_part)
                act.wait_ge(sig("ffn_end"), nth + 1)
                act.copy(x[:, 0, :], ps[:, 0:2, :].rearrange("p a b -> p (a b)"))
                end_stage(act, "scalar")

            def dve_(dve):
                if nth == 0:
                    dve.drain().then_inc(sig("ffn_hid"), 2)
                    dve.drain().then_inc(sig("ffn_hidT"), 2)
                ffn_run(dve, f, ffn_dve_part)
                dve.wait_ge(sig("ffn_end"), nth + 1)
                dve.tensor_copy(x[:, 1, :], ps[:, 2:4, :].rearrange("p a b -> p (a b)"))
                end_stage(dve, "vector")

            return pe_, act_, dve_, idle_pool

        ML = Arena(arena)
        z = ML.take(NT, ZW)
        ycat = ML.take(NT, D)
        ml_at = ML.at

        def z_copy_act(act, j, src):
            return act.copy(z[:, j.tile, j.col:j.col + j.n], src)

        def z_copy_dve(dve, j, src):
            return dve.tensor_copy(z[:, j.tile, j.col:j.col + j.n], src)

        def rope_dve(dve):
            a, b = small[:, 32:48], small[:, 48:64]
            a2, b2 = [v.rearrange("p (t n) -> p t n", t=NT) for v in (a, b)]
            vstep(dve, dve.tensor_copy(small[:, 64:66], pos_i[:]))
            vstep(dve, dve.tensor_tensor(a2, small[:, 64:66].unsqueeze(2).to_broadcast([P, NT, ROPE_HALF]),
                                         freq[:].unsqueeze(1).to_broadcast([P, NT, ROPE_HALF]), ALU.mult))
            magic = 1.5 * 2.0 ** 23
            vstep(dve, dve.tensor_scalar(b, a, 1.0 / (2 * np.pi), magic, ALU.mult, ALU.add))
            vstep(dve, dve.tensor_scalar(b, b, -magic, None, ALU.add))
            rest = 2 * np.pi
            for bits in (8, 9, None):
                if bits is None:
                    part = float(np.float32(rest))
                else:
                    e = np.floor(np.log2(abs(rest)))
                    q = 2.0 ** (e - bits)
                    part = float(np.floor(rest / q) * q)
                rest -= part
                vstep(dve, dve.scalar_tensor_tensor(out=a, in0=b, scalar=-part, in1=a, op0=ALU.mult, op1=ALU.add))
            lim = float(np.nextafter(np.float32(np.pi), np.float32(0)))
            dve.tensor_scalar(a, a, lim, -lim, ALU.min, ALU.max).then_inc(sig("rope_angle"), 1)
            dve.wait_ge(sig("rope_sin"), 1)
            c = cos_t[:].rearrange("p t n -> p (t n)")
            vstep(dve, dve.tensor_tensor(c, c, c, ALU.mult))
            dve.tensor_scalar(c, c, -2.0, 1.0, ALU.mult, ALU.add)

        def rope_act(act):
            act.wait_ge(sig("rope_angle"), 1)
            a = small[:, 32:48]
            act.activation(sin_t[:].rearrange("p t n -> p (t n)"), a, ACT.Sin)
            act.activation(cos_t[:].rearrange("p t n -> p (t n)"), a, ACT.Sin, scale=0.5).then_inc(sig("rope_sin"), 1)

        MG = Arena(arena)
        MG.at = ml_at
        s_v = MG.take(NT, AH, HD)
        s_sq = MG.take(NT, AH, HD)
        s_wT = MG.take(AH, P)
        s_u = MG.take(NT, AW)

        def gating(l):
            def pe_(pe):
                for h in range(AH):
                    mm = pe.transpose(ps[:, 0, h * P:(h + 1) * P], l_ws[:, h, :], ident[:])
                mm.then_inc(sig("gat_wT"), 1)
                pe.wait_ge(sig("gat_v"), l + 1)
                for h in range(AH):
                    mm = pe.matmul(ps[:, 1, h * P:(h + 1) * P], s_wT[:, h, :], s_v[:, :, h, :], start=True, stop=True)
                mm.then_inc(sig("gat_mixed"), 1)
                end_stage(pe, "tensor")

            def act_(act):
                act.activation(s_v.rearrange("p t h n -> p t (h n)"), z[:, :, AW:2 * AW], ACT.Gelu_apprx_tanh)\
                    .then_inc(sig("gat_gelu"), 1)
                act.activation(s_u, z[:, :, 0:AW], ACT.Gelu_apprx_tanh).then_inc(sig("gat_gelu"), 1)
                act.wait_ge(sig("gat_var"), l + 1)
                act.activation(small[:, 24:32], small[:, 16:24], ACT.Sqrt).then_inc(sig("gat_sd"), 1)
                end_stage(act, "scalar")

            def dve_(dve):
                v8 = s_v.rearrange("p t h n -> p (t h) n")
                q8 = s_sq.rearrange("p t h n -> p (t h) n")
                dve.wait_ge(sig("gat_wT"), l + 1)
                dve.tensor_tensor(s_wT, ps[:, 0, :].rearrange("p (h n) -> p h n", h=AH),
                                  causal_up[:].unsqueeze(1).to_broadcast([P, AH, P]), ALU.mult)
                dve.wait_ge(sig("gat_gelu"), 2 * l + 1)
                vstep(dve, dve.tensor_reduce(small[:, 0:8], v8, AX, ALU.add))
                vstep(dve, dve.tensor_scalar(small[:, 8:16], small[:, 0:8], 1.0 / HD, None, ALU.mult))
                vstep(dve, dve.tensor_tensor(v8, v8, small[:, 8:16].unsqueeze(2).to_broadcast([P, 8, HD]), ALU.subtract))
                vstep(dve, dve.tensor_tensor(q8, v8, v8, ALU.mult))
                vstep(dve, dve.tensor_reduce(small[:, 0:8], q8, AX, ALU.add))
                dve.tensor_scalar(small[:, 16:24], small[:, 0:8], 1.0 / HD, LN_EPS, ALU.mult, ALU.add).then_inc(sig("gat_var"), 1)
                dve.wait_ge(sig("gat_sd"), l + 1)
                vstep(dve, dve.reciprocal(small[:, 0:8], small[:, 24:32]))
                vstep(dve, dve.tensor_tensor(v8, v8, small[:, 0:8].unsqueeze(2).to_broadcast([P, 8, HD]), ALU.mult))
                vf = s_v.rearrange("p t h n -> p t (h n)")
                vstep(dve, dve.tensor_tensor(vf, vf, l_row[:, 7, :].unsqueeze(1).to_broadcast([P, NT, AW]), ALU.mult))
                dve.tensor_tensor(vf, vf, l_row[:, 8, :].unsqueeze(1).to_broadcast([P, NT, AW]), ALU.add)\
                    .then_inc(sig("gat_v"), 1)
                dve.wait_ge(sig("gat_mixed"), l + 1)
                dve.wait_ge(sig("gat_gelu"), 2 * l + 2)
                for h in range(AH):
                    dve.scalar_tensor_tensor(out=ycat[:, :, h * HD:(h + 1) * HD],
                                             in0=ps[:, 1, h * P:(h + 1) * P].rearrange("p (t n) -> p t n", t=NT),
                                             scalar=l_bsT[:, h:h + 1], in1=s_u[:, :, h * HD:(h + 1) * HD],
                                             op0=ALU.add, op1=ALU.mult)
                end_stage(dve, "vector")

            return pe_, act_, dve_, idle_pool

        MW = Arena(arena)
        MW.at = ml_at
        HP = BH // 2
        half_t = lambda: MW.take(NT, BW)
        w_lw, w_a, w_g, w_kk, w_km, w_R, w_K, w_A, w_Ke, w_B, w_Be = [half_t() for _ in range(11)]
        w_loT = MW.take(NT, S)
        w_AT, w_RT, w_BT, w_KT = [MW.take(HP, S) for _ in range(4)]
        w_MT, w_RB, w_RK = [[MW.take(BH, P) for _ in range(NT)] for _ in range(3)]
        w_TT = MW.take(BH, P)
        w_H = MW.take(HP, P)
        w_WT = w_lw.rearrange("p t n -> p (t n)").rearrange("p (h n) -> p h n", h=HP)
        w_htmp = w_loT[:, 1, :].rearrange("p (h n) -> p h n", h=HP)
        hT_flat = hT[:].rearrange("p c s -> p (c s)")
        w_T, w_Lm, w_LTm, w_Yb = [hT_flat[:, k * 512:(k + 1) * 512].rearrange("p (h n) -> p h n", h=BH) for k in range(4)]
        w_L, w_LT = [z[:, k, 0:512].rearrange("p (h n) -> p h n", h=BH) for k in range(2)]
        w_Zb = ycat[:, 0, 512:1024].rearrange("p (h n) -> p h n", h=BH)
        w_lora = ycat[:, :, 512:768]
        w_tmp = ycat[:, :, 768:1024]
        w_mv = w_loT[:, 0, :]
        w_Uv, w_U = w_kk, w_a
        w_y = w_lw
        w_ss = small[:, 0:8]
        w_cend = small[:, 96:104]
        LEV = 6
        zr, zk, zv = [z[:, :, ZB0 + k * BW:ZB0 + (k + 1) * BW] for k in range(3)]

        def row(k):
            return l_row[:, k, :].unsqueeze(1).to_broadcast([P, NT, BW])

        def heads(ap):
            return ap.rearrange("p t (h n) -> p t h n", h=BH)

        def per_head(v):
            return v.rearrange("p (t h) -> p t h", t=NT).unsqueeze(3).to_broadcast([P, NT, BH, HD])

        def rwkv(l):
            def at(name, k, per):
                return sig(name), l * per + k

            def pe_(pe):
                for t in range(NT):
                    for b in range(2):
                        cols = slice(ZB0 + b * 512, ZB0 + (b + 1) * 512)
                        mm = pe.matmul(ps[:, 2 * t + b, :], shift_dn[:], z[:, t, cols], start=True, stop=(t == 0))
                        if t:
                            mm = pe.matmul(ps[:, 2 * t + b, :], shift_dn_edge[:], z[:, t - 1, cols], start=False, stop=True)
                mm.then_inc(sig("rw_shift"), 1)
                pe.wait_ge(*at("rw_lora", 1, 1))
                for k in range(2):
                    for t in range(NT):
                        mm = pe.transpose(ps[:, 4, k * S + t * P:k * S + (t + 1) * P], w_lora[:, t, k * P:(k + 1) * P], ident[:])
                mm.then_inc(sig("rw_loT_psum"), 1)
                pe.wait_ge(*at("rw_loT", 1, 1))
                for t in range(NT):
                    tok = slice(t * P, (t + 1) * P)
                    pe.matmul(ps[:, 5, t * BW:(t + 1) * BW], w_loT[0:64, 0, tok], l_lora[0:64, 0, :], start=True, stop=True)
                    pe.matmul(ps[:, 6, t * BW:(t + 1) * BW], w_loT[64:128, 0, tok], l_lora[64:128, 0, :], start=True, stop=True)
                    mm = pe.matmul(ps[:, 7, t * BW:(t + 1) * BW], w_loT[:, 1, tok], l_lora[:, 1, :], start=True, stop=True)
                mm.then_inc(sig("rw_lin"), 1)
                pe.wait_ge(*at("rw_lw", 1, 1))
                for k, m in enumerate((tri_inc, tri_str, same_chunk)):
                    for t in range(NT):
                        pe.matmul(ps[:, k, t * BW:(t + 1) * BW], m[:], w_lw[:, t, :], start=True, stop=True)
                for t in range(NT):
                    for p in range(HP):
                        q = 2 * (t * HP + p)
                        mm = pe.matmul(ps[:, 3, q:q + 2], w_lw[:, t, p * P:(p + 1) * P], half_ind[:], start=True, stop=True)
                mm.then_inc(sig("rw_cum"), 1)
                pe.wait_ge(*at("rw_rkab", 1, 1))
                for q, a in enumerate((w_A, w_R, w_B, w_K)):
                    for p in range(HP):
                        for t in range(NT):
                            mm = pe.transpose(ps[:, q, p * S + t * P:p * S + (t + 1) * P], a[:, t, p * P:(p + 1) * P], ident[:])
                    mm.then_inc(sig("rw_turned"), 1)
                pe.wait_ge(*at("rw_AT", 1, 1))
                pe.wait_ge(*at("rw_BT", 1, 1))
                for t in range(NT):
                    tok = slice(t * P, (t + 1) * P)
                    if t:
                        pe.wait_ge(*at("rw_Uv", t, NT))
                    for s in range(2):
                        half = slice(64 * s, 64 * s + 64)
                        for k, (a, b) in enumerate(((w_BT, w_AT), (w_AT, w_BT), (w_KT, w_AT), (w_BT, w_RT), (w_KT, w_RT))):
                            for p in range(HP):
                                c = (k % 2) * S + p * P
                                mm = pe.matmul(ps[:, 3 * s + k // 2, c:c + P], a[half, p, tok], b[half, p, tok],
                                               start=True, stop=True)
                    mm.then_inc(sig("rw_scores"), 1)
                    for k in range(1, LEV):
                        n = t * (LEV - 1) + k
                        pe.wait_ge(*at("rw_tt", t * LEV + k, NT * LEV))
                        pe.wait_ge(*at("rw_lm", n, NT * (LEV - 1)))
                        for h in range(BH):
                            mm = pe.matmul(ps[:, 6, h * P:(h + 1) * P], w_Lm[:, h, :], w_TT[:, h, :], start=True, stop=True)
                        if k + 1 < LEV:
                            for h in range(BH):
                                mm = pe.matmul(ps[:, 7, h * P:(h + 1) * P], w_LTm[:, h, :], w_T[:, h, :], start=True, stop=True)
                        mm.then_inc(sig("rw_yz"), 1)
                        pe.wait_ge(*at("rw_y", n, NT * (LEV - 1)))
                        pe.wait_ge(*at("rw_z", n, NT * (LEV - 1)))
                        for h in range(BH):
                            mm = pe.matmul(ps[:, 6, h * P:(h + 1) * P], w_T[:, h, :], w_Yb[:, h, :], start=True, stop=True)
                        if k + 1 < LEV:
                            for h in range(BH):
                                mm = pe.matmul(ps[:, 7, h * P:(h + 1) * P], w_TT[:, h, :], w_Zb[:, h, :], start=True, stop=True)
                        mm.then_inc(sig("rw_dt"), 1)
                    pe.wait_ge(*at("rw_tt", (t + 1) * LEV, NT * LEV))
                    pe.wait_ge(*at("rw_masked", t + 1, NT))
                    for s in range(2):
                        for p in range(HP):
                            h = 2 * p + s
                            pe.matmul(ps[64 * s:64 * s + 64, 0, p * P:(p + 1) * P], w_A[:, t, h * HD:(h + 1) * HD],
                                      w_TT[:, s * HP + p, :], start=True, stop=True)
                            mm = pe.matmul(ps[:, 1, h * HD:(h + 1) * HD], w_MT[t][:, s * HP + p, :], zv[:, t, h * HD:(h + 1) * HD],
                                           start=True, stop=True)
                    mm.then_inc(sig("rw_mv_psum"), 1)
                    pe.wait_ge(*at("rw_mv", t + 1, NT))
                    for s in range(2):
                        for p in range(HP):
                            h = 2 * p + s
                            mm = pe.matmul(ps[:, 2, h * HD:(h + 1) * HD], w_TT[:, s * HP + p, :], w_mv[:, h * HD:(h + 1) * HD],
                                           start=True, stop=True)
                    mm.then_inc(sig("rw_Uv_psum"), 1)
                pe.wait_ge(*at("rw_Uv", NT, NT))
                for t in range(NT):
                    for h in range(BH):
                        i = (h % 2) * HP + h // 2
                        pe.matmul(ps[:, 4 + t, h * HD:(h + 1) * HD], w_RK[t][:, i, :], zv[:, t, h * HD:(h + 1) * HD],
                                  start=(h == 0), stop=False, skip_group_check=True)
                chunks = S // RC
                for n in range(chunks):
                    t, o = n * RC // P, n * RC % P
                    part, tok = slice(o, o + RC), slice(n * RC, (n + 1) * RC)
                    if n:
                        pe.wait_ge(*at("rw_H", n, chunks - 1))
                        for p in range(HP):
                            pe.matmul(ps[part, 3, p * P:(p + 1) * P], w_WT[:, p, tok], w_H[:, p, :], start=True, stop=True)
                        for p in range(HP):
                            mm = pe.matmul(ps[part, 4 + t, p * P:(p + 1) * P], w_RT[:, p, tok], w_H[:, p, :],
                                           start=False, stop=False, skip_group_check=True)
                        mm.then_inc(sig("rw_WH"), 1)
                    pe.wait_ge(*at("rw_U", n + 1, chunks))
                    if n + 1 < chunks:
                        for p in range(HP):
                            cols = slice(p * P, (p + 1) * P)
                            pe.matmul(ps[:, 6, cols], w_Be[part, t, cols], w_U[part, t, cols], start=True, stop=False)
                            mm = pe.matmul(ps[:, 6, cols], w_Ke[part, t, cols], z[part, t, ZB0 + 2 * BW + p * P:ZB0 + 2 * BW + (p + 1) * P],
                                           start=False, stop=True)
                        mm.then_inc(sig("rw_dH"), 1)
                for t in range(NT):
                    for h in range(BH):
                        i = (h % 2) * HP + h // 2
                        mm = pe.matmul(ps[:, 4 + t, h * HD:(h + 1) * HD], w_RB[t][:, i, :], w_U[:, t, h * HD:(h + 1) * HD],
                                       start=False, stop=(h == BH - 1), skip_group_check=True)
                mm.then_inc(sig("rw_Y"), 1)
                end_stage(pe, "tensor")

            def act_(act):
                act.wait_ge(*at("rw_mixed", 1, 1))
                act.activation(w_lora[:, :, 0:64], z[:, :, ZB0 + 768:ZB0 + 832], ACT.Tanh)
                act.copy(w_lora[:, :, 64:128], z[:, :, ZB0 + 832:ZB0 + 896])
                act.activation(w_lora[:, :, 128:256], z[:, :, ZB0 + 896:ZB0 + 1024], ACT.Sigmoid).then_inc(sig("rw_lora"), 1)
                act.wait_ge(*at("rw_logit", 1, 1))
                act.activation(w_lw, w_lw, ACT.Sigmoid).then_inc(sig("rw_sig"), 1)
                act.activation(w_a, w_a, ACT.Sigmoid).then_inc(sig("rw_sig"), 1)
                act.copy(w_g.rearrange("p t n -> p (t n)"), ps[:, 7, :])
                act.wait_ge(*at("rw_kk2", 1, 1))
                act.activation(small[:, 16:24], small[:, 8:16], ACT.Sqrt).then_inc(sig("rw_kkrt"), 1)
                act.wait_ge(*at("rw_cum", 1, 1))
                f = lambda a: a.rearrange("p t n -> p (t n)")
                act.copy(f(w_Ke), ps[:, 2, :])
                act.activation(f(w_R), ps[:, 0, :], ACT.Exp)
                act.activation(f(w_K), ps[:, 0, :], ACT.Exp, scale=-1.0).then_inc(sig("rw_total"), 1)
                act.activation(f(w_A), ps[:, 1, :], ACT.Exp)
                act.activation(w_cend, ps[:, 3, 0:8], ACT.Exp)
                act.wait_ge(*at("rw_toend", 1, 1))
                act.activation(f(w_Ke), f(w_Ke), ACT.Exp).then_inc(sig("rw_exp"), 1)
                act.wait_ge(*at("rw_turned", 2, 4))
                act.copy(w_AT, ps[:, 0, :].rearrange("p (h n) -> p h n", h=HP))
                act.copy(w_RT, ps[:, 1, :].rearrange("p (h n) -> p h n", h=HP)).then_inc(sig("rw_AT"), 1)
                for t in range(NT):
                    act.wait_ge(*at("rw_scores", t + 1, NT))
                    for s in range(2):
                        act.copy(w_LT[:, s * HP:(s + 1) * HP, :], ps[:, 3 * s, 0:S].rearrange("p (h n) -> p h n", h=HP))
                        ins = act.copy(w_L[:, s * HP:(s + 1) * HP, :], ps[:, 3 * s, S:2 * S].rearrange("p (h n) -> p h n", h=HP))
                    ins.then_inc(sig("rw_L"), 1)
                    for k in range(1, LEV):
                        act.wait_ge(*at("rw_yz", t * (LEV - 1) + k, NT * (LEV - 1)))
                        act.copy(w_Yb, ps[:, 6, :].rearrange("p (h n) -> p h n", h=BH)).then_inc(sig("rw_y"), 1)
                    act.wait_ge(*at("rw_mv_psum", t + 1, NT))
                    act.copy(w_WT[:, :, t * P:(t + 1) * P], ps[:, 0, 0:S].rearrange("p (h n) -> p h n", h=HP))
                    act.copy(w_mv, ps[:, 1, 0:BW]).then_inc(sig("rw_mv"), 1)
                act.wait_ge(*at("rw_var", 1, 1))
                act.activation(small[:, 24:32], small[:, 16:24], ACT.Sqrt).then_inc(sig("rw_sd"), 1)
                end_stage(act, "scalar")

            def pool_(pool):
                for t in range(NT):
                    pool.wait_ge(*at("rw_L", t + 1, NT))
                    for k in range(1, LEV):
                        if t or k > 1:
                            pool.wait_ge(*at("rw_yz", t * (LEV - 1) + k - 1, NT * (LEV - 1)))
                        pool.tensor_tensor(w_Lm, w_L, low_b[:, k, :].unsqueeze(1).to_broadcast([P, BH, P]), ALU.mult)
                        pool.tensor_tensor(w_LTm, w_LT, up_b[:, k, :].unsqueeze(1).to_broadcast([P, BH, P]), ALU.mult)\
                            .then_inc(sig("rw_lm"), 1)
                end_stage(pool, "gpsimd")

            def dve_(dve):
                f = lambda a: a.rearrange("p t n -> p (t n)")
                dve.wait_ge(*at("rw_shift", 1, 1))
                mixt = arena[:, ml_at + 5 * 512:ml_at + 5 * 512 + 1024]
                for t in range(NT):
                    zb_t = z[:, t, ZB0:ZC0]
                    vstep(dve, dve.tensor_tensor(mixt, ps[:, 2 * t:2 * t + 2, :].rearrange("p a b -> p (a b)"), l_mu[:], ALU.mult))
                    ins = dve.tensor_tensor(zb_t, zb_t, mixt, ALU.add)
                    if t + 1 < NT:
                        vstep(dve, ins)
                ins.then_inc(sig("rw_mixed"), 1)
                dve.wait_ge(*at("rw_mixed", 1, 1))
                dve.wait_ge(*at("rw_loT_psum", 1, 1))
                dve.tensor_copy(w_loT.rearrange("p t n -> p (t n)"), ps[:, 4, :]).then_inc(sig("rw_loT"), 1)
                vstep(dve, dve.tensor_tensor(w_kk, zk, row(2), ALU.mult))
                vstep(dve, dve.tensor_tensor(w_B, w_kk, w_kk, ALU.mult))
                vstep(dve, dve.tensor_reduce(w_ss, w_B.rearrange("p t (h n) -> p (t h) n", h=BH), AX, ALU.add))
                dve.tensor_scalar(small[:, 8:16], w_ss, 1e-24, None, ALU.max).then_inc(sig("rw_kk2"), 1)
                dve.wait_ge(*at("rw_lin", 1, 1))
                dve.tensor_tensor(w_lw, ps[:, 5, :].rearrange("p (t n) -> p t n", t=NT), row(0), ALU.add)
                dve.tensor_tensor(w_a, ps[:, 6, :].rearrange("p (t n) -> p t n", t=NT), row(1), ALU.add)\
                    .then_inc(sig("rw_logit"), 1)
                dve.wait_ge(*at("rw_sig", 1, 2))
                dve.tensor_scalar(f(w_lw), f(w_lw), -float(np.exp(-0.5)), None, ALU.mult).then_inc(sig("rw_lw"), 1)
                dve.wait_ge(*at("rw_kkrt", 1, 1))
                vstep(dve, dve.reciprocal(small[:, 0:8], small[:, 16:24]))
                vstep(dve, dve.tensor_tensor(heads(w_kk), heads(w_kk), per_head(small[:, 0:8]), ALU.mult))
                dve.wait_ge(*at("rw_sig", 2, 2))
                vstep(dve, dve.scalar_tensor_tensor(out=w_km, in0=w_a, scalar=-1.0, in1=row(3), op0=ALU.add, op1=ALU.mult))
                vstep(dve, dve.scalar_tensor_tensor(out=w_km, in0=w_km, scalar=1.0, in1=zk, op0=ALU.add, op1=ALU.mult))
                vstep(dve, dve.tensor_tensor(f(w_B), f(w_kk), f(w_a), ALU.mult))
                dve.wait_ge(*at("rw_total", 1, 1))
                dve.tensor_tensor(f(w_Ke), f(w_Ke), ps[:, 0, :], ALU.subtract).then_inc(sig("rw_toend"), 1)
                dve.wait_ge(*at("rw_exp", 1, 1))
                dve.tensor_tensor(w_R, w_R, zr, ALU.mult)
                dve.scalar_tensor_tensor(out=f(w_A), in0=f(w_kk), scalar=-1.0, in1=f(w_A), op0=ALU.mult, op1=ALU.mult)
                vstep(dve, dve.tensor_tensor(f(w_Be), f(w_B), f(w_Ke), ALU.mult))
                dve.tensor_tensor(f(w_Ke), f(w_km), f(w_Ke), ALU.mult)
                vstep(dve, dve.tensor_tensor(f(w_B), f(w_B), f(w_K), ALU.mult))
                dve.tensor_tensor(f(w_K), f(w_K), f(w_km), ALU.mult).then_inc(sig("rw_rkab"), 1)
                dve.wait_ge(*at("rw_turned", 4, 4))
                dve.tensor_copy(w_BT, ps[:, 2, :].rearrange("p (h n) -> p h n", h=HP))
                dve.tensor_copy(w_KT, ps[:, 3, :].rearrange("p (h n) -> p h n", h=HP)).then_inc(sig("rw_BT"), 1)
                for t in range(NT):
                    dve.wait_ge(*at("rw_scores", t + 1, NT))
                    dve.wait_ge(*at("rw_L", t + 1, NT))
                    idn = ident[:].unsqueeze(1).to_broadcast([P, BH, P])
                    dve.tensor_tensor(w_T, w_L, low_b[:, 0, :].unsqueeze(1).to_broadcast([P, BH, P]), ALU.mult)
                    vstep(dve, dve.tensor_tensor(w_TT, w_LT, up_b[:, 0, :].unsqueeze(1).to_broadcast([P, BH, P]), ALU.mult))
                    dve.tensor_tensor(w_T, w_T, idn, ALU.add)
                    dve.tensor_tensor(w_TT, w_TT, idn, ALU.add).then_inc(sig("rw_tt"), 1)
                    for s in range(2):
                        hs = slice(s * HP, (s + 1) * HP)
                        for k, (dst, m) in enumerate(((w_MT[t], tri_str), (w_RB[t], tri_inc), (w_RK[t], tri_inc))):
                            c = (k % 2) * S
                            ins = dve.tensor_tensor(dst[:, hs, :], ps[:, 3 * s + 1 + k // 2, c:c + S].rearrange("p (h n) -> p h n", h=HP),
                                                    m[:].unsqueeze(1).to_broadcast([P, HP, P]), ALU.mult)
                    ins.then_inc(sig("rw_masked"), 1)
                    for k in range(1, LEV):
                        n = t * (LEV - 1) + k
                        dve.wait_ge(*at("rw_yz", n, NT * (LEV - 1)))
                        if k + 1 < LEV:
                            dve.tensor_copy(w_Zb, ps[:, 7, :].rearrange("p (h n) -> p h n", h=BH)).then_inc(sig("rw_z"), 1)
                        else:
                            dve.drain().then_inc(sig("rw_z"), 1)
                        dve.wait_ge(*at("rw_dt", n, NT * (LEV - 1)))
                        if k + 1 < LEV:
                            dve.tensor_tensor(w_T, w_T, ps[:, 7, :].rearrange("p (h n) -> p h n", h=BH), ALU.add)
                        dve.tensor_tensor(w_TT, w_TT, ps[:, 6, :].rearrange("p (h n) -> p h n", h=BH), ALU.add)\
                            .then_inc(sig("rw_tt"), 1)
                    dve.wait_ge(*at("rw_Uv_psum", t + 1, NT))
                    dve.tensor_copy(w_Uv[:, t, :], ps[:, 2, 0:BW]).then_inc(sig("rw_Uv"), 1)
                dve.wait_ge(*at("rw_Uv", NT, NT))
                chunks = S // RC
                for n in range(chunks):
                    t, o = n * RC // P, n * RC % P
                    part = slice(o, o + RC)
                    if n:
                        dve.wait_ge(*at("rw_WH", n, chunks - 1))
                        dve.tensor_tensor(w_U[part, t, :], ps[part, 3, 0:BW], w_Uv[part, t, :], ALU.add).then_inc(sig("rw_U"), 1)
                    else:
                        dve.tensor_copy(w_U[part, t, :], w_Uv[part, t, :]).then_inc(sig("rw_U"), 1)
                    if n + 1 < chunks:
                        dve.wait_ge(*at("rw_dH", n + 1, chunks - 1))
                        dst = w_htmp if n else w_H
                        ins = dve.tensor_tensor(dst, ps[:, 6, 0:HP * P].rearrange("p (h n) -> p h n", h=HP),
                                                same_chunk[:].unsqueeze(1).to_broadcast([P, HP, P]), ALU.mult)
                        if n:
                            vstep(dve, ins)
                            for p in range(HP):
                                q = 2 * (t * HP + p) + n % 2
                                ins = dve.scalar_tensor_tensor(out=w_H[:, p, :], in0=w_H[:, p, :], scalar=w_cend[:, q:q + 1],
                                                               in1=w_htmp[:, p, :], op0=ALU.mult, op1=ALU.add)
                        ins.then_inc(sig("rw_H"), 1)
                dve.wait_ge(*at("rw_Y", 1, 1))
                Y = ps[:, 4:6, 0:BW]
                y8 = w_y.rearrange("p t (h n) -> p (t h) n", h=BH)
                vstep(dve, dve.tensor_copy(w_y, Y))
                vstep(dve, dve.tensor_reduce(small[:, 0:8], y8, AX, ALU.add))
                vstep(dve, dve.tensor_scalar(small[:, 8:16], small[:, 0:8], 1.0 / HD, None, ALU.mult))
                vstep(dve, dve.tensor_tensor(heads(w_y), heads(w_y), per_head(small[:, 8:16]), ALU.subtract))
                vstep(dve, dve.tensor_tensor(f(w_B), f(w_y), f(w_y), ALU.mult))
                vstep(dve, dve.tensor_reduce(small[:, 0:8], w_B.rearrange("p t (h n) -> p (t h) n", h=BH), AX, ALU.add))
                dve.tensor_scalar(small[:, 16:24], small[:, 0:8], 1.0 / HD, GN_EPS, ALU.mult, ALU.add).then_inc(sig("rw_var"), 1)
                vstep(dve, dve.tensor_tensor(w_km, w_km, zr, ALU.mult))
                vstep(dve, dve.tensor_tensor(w_km, w_km, row(4), ALU.mult))
                vstep(dve, dve.tensor_reduce(small[:, 32:40], w_km.rearrange("p t (h n) -> p (t h) n", h=BH), AX, ALU.add))
                vstep(dve, dve.tensor_tensor(heads(w_km), heads(zv), per_head(small[:, 32:40]), ALU.mult))
                dve.wait_ge(*at("rw_sd", 1, 1))
                vstep(dve, dve.reciprocal(small[:, 0:8], small[:, 24:32]))
                vstep(dve, dve.tensor_tensor(heads(w_y), heads(w_y), per_head(small[:, 0:8]), ALU.mult))
                vstep(dve, dve.tensor_tensor(w_y, w_y, row(5), ALU.mult))
                vstep(dve, dve.tensor_tensor(w_y, w_y, row(6), ALU.add))
                vstep(dve, dve.tensor_tensor(f(w_y), f(w_y), f(w_km), ALU.add))
                dve.tensor_tensor(ycat[:, :, AW:AW + BW], w_y, w_g, ALU.mult)
                end_stage(dve, "vector")

            return pe_, act_, dve_, pool_

        MN = Arena(arena)
        MN.at = ml_at
        n_qT = MN.take(CH // 2, S)
        n_qrT = MN.take(CH // 2, S)
        n_kT = MN.take(2, CG, S)
        n_rt = MN.take(4, NT, CH, ROPE_HALF)
        n_blk = MN.take(4, 16, NCMP)
        n_hid = MN.take(4, 16)
        n_kcT = MN.take(CG, 16)
        n_hv = MN.take(2, CH // 2, 16)
        n_vbd = MN.take(CH, HD)
        n_sc = MN.take(NT, CH, 16)
        n_pcT = MN.take(S)
        n_cs = MN.take(2, NT * CH)
        n_sm = [MN.take(4, S) for _ in range(2)]
        n_pT = [MN.take(4, 2, P) for _ in range(2)]
        n_mx, n_den, n_rd = [MN.take(8 * 4) for _ in range(3)]
        n_o = MN.take(4, HD)
        n_gate = MN.take(NT, 3 * CH)
        n_qr = z[:, :, 512:1024]
        n_k2 = hT_flat[:, 0:NT * 2 * CG * 2 * HD].rearrange("p (t k g s n) -> p t k g s n", t=NT, k=2, g=CG, s=2)
        n_kc2 = z[:, :, 0:512].rearrange("p t (q k n) -> p t q k n", q=4, k=2)
        GROUPS = [(br, t, s) for br in range(2) for t in range(NT) for s in range(2)]
        SCALE = HD ** -0.5

        def nsa(l):
            def at(name, k, per):
                return sig(name), l * per + k

            def y_of(t, s):
                return ycat[:, t, AW + BW:D].rearrange("p (h s n) -> p h s n", h=CH // 2, s=2)[:, :, s, :]

            def gate_of(t, s, br):
                return n_gate[:, t, :].rearrange("p (h s b) -> p h s b", s=2, b=3)[:, :, s, br]

            def pe_(pe):
                for t in range(NT):
                    mm = pe.matmul(ps[:, 0, t * S:(t + 1) * S], shift_up[:], z[:, t, CKC:CKS], start=True, stop=(t == NT - 1))
                    if t + 1 < NT:
                        mm = pe.matmul(ps[:, 0, t * S:(t + 1) * S], shift_up_edge[:], z[:, t + 1, CKC:CKS], start=False, stop=True)
                mm.then_inc(sig("nsa_next"), 1)
                for p in range(CH // 2):
                    for t in range(NT):
                        mm = pe.transpose(ps[:, 1 + p // 2, (p % 2) * S + t * P:(p % 2) * S + (t + 1) * P],
                                          z[:, t, CQ + p * P:CQ + (p + 1) * P], ident[:])
                mm.then_inc(sig("nsa_q"), 1)
                pe.wait_ge(*at("nsa_pairs", 1, 1))
                for q in range(4):
                    for t in range(NT):
                        mm = pe.transpose(ps[:, 3 + q // 2, (q % 2) * S + t * P:(q % 2) * S + (t + 1) * P],
                                          n_kc2[:, t, q].rearrange("p k n -> p (k n)"), ident[:])
                mm.then_inc(sig("nsa_blkT"), 1)
                pe.wait_ge(*at("nsa_blk", 1, 1))
                u = cmp_unit[l]
                pe.wait_ge(slot_ready[u.slot], u.ready)
                for q in range(4):
                    for i in range(16):
                        mm = pe.matmul(ps[:, 5, q * 16:q * 16 + NCMP], u.view[:, q // 2, i, :], n_blk[:, q, i, :],
                                       start=(i == 0), stop=(i == 15))
                mm.then_inc(cmp_w_used, 1)
                pe.wait_ge(*at("nsa_hid", 1, 1))
                pe.matmul(ps[:, 6, 0:CG * 16], l_w2[:, 0:2, :].rearrange("p k n -> p (k n)"),
                          n_hid[:, 0:2, :].rearrange("p q n -> p (q n)"), start=True, stop=True)
                mm = pe.matmul(ps[:, 6, 64:64 + HD], n_hv.rearrange("p s h n -> p (s h n)"), l_w2[:, 2, :], start=True, stop=True)
                mm.then_inc(sig("nsa_cmp"), 1)
                pe.wait_ge(*at("nsa_kc", 1, 1))
                pe.wait_ge(*at("nsa_qT", 1, 1))
                for s in range(2):
                    half = slice(64 * s, 64 * s + 64)
                    for t in range(NT):
                        for p in range(CH // 2):
                            c = (t * 4 + p) * 16
                            mm = pe.matmul(ps[:, 3 + s, c:c + 16], n_qT[half, p, t * P:(t + 1) * P], n_kcT[half, p // 2, :],
                                           start=True, stop=True)
                mm.then_inc(sig("nsa_sc"), 1)
                pe.wait_ge(*at("nsa_rot", 1, 1))
                for p in range(CH // 2):
                    for t in range(NT):
                        mm = pe.transpose(ps[:, 1 + p // 2, (p % 2) * S + t * P:(p % 2) * S + (t + 1) * P],
                                          n_qr[:, t, p * P:(p + 1) * P], ident[:])
                mm.then_inc(sig("nsa_qr"), 1)
                pe.wait_ge(*at("nsa_vbd", 1, 1))
                for k in range(2):
                    for g in range(CG):
                        for t in range(NT):
                            mm = pe.transpose(ps[:, 6 + k, g * S + t * P:g * S + (t + 1) * P],
                                              n_k2[:, t, k, g].rearrange("p s n -> p (s n)"), ident[:])
                mm.then_inc(sig("nsa_k"), 1)
                pe.wait_ge(*at("nsa_pc", 1, 1))
                for t in range(NT):
                    mm = pe.transpose(ps[:, 0, t * P:(t + 1) * P], n_sc[:, t].rearrange("p h n -> p (h n)"), ident[:])
                mm.then_inc(sig("nsa_pcturned"), 1)
                pe.wait_ge(*at("nsa_pcT", 1, 1))
                for t in range(NT):
                    mm = pe.matmul(ps[:, 3 + t, :], n_pcT[:, t * P:(t + 1) * P], n_vbd.rearrange("p h n -> p (h n)"),
                                   start=True, stop=True)
                mm.then_inc(sig("nsa_oc"), 1)
                pe.wait_ge(*at("nsa_kT", 1, 1))
                pe.wait_ge(*at("nsa_ocdone", 1, 1))

                def scores(k):
                    br, t, s = GROUPS[k]
                    half = slice(64 * s, 64 * s + 64)
                    if k >= 2:
                        pe.wait_ge(*at("nsa_max", k - 1, 8))
                    for p in range(CH // 2):
                        nk = (t + 1) * P
                        c = p * nk
                        mm = pe.matmul(ps[:, 2 * (k % 2) + c // 512, c % 512:c % 512 + nk], n_qrT[half, p, t * P:(t + 1) * P],
                                       n_kT[half, br, p // 2, 0:nk], start=True, stop=True)
                    mm.then_inc(sig("nsa_scores"), 1)

                scores(0)
                for k, (br, t, s) in enumerate(GROUPS):
                    if k + 1 < len(GROUPS):
                        scores(k + 1)
                    pe.wait_ge(*at("nsa_probs", k + 1, 8))
                    if k >= 1:
                        pe.wait_ge(*at("nsa_pT", k, 8))
                    for p in range(CH // 2):
                        for b in range(t + 1):
                            q = p * (t + 1) + b
                            mm = pe.transpose(ps[:, 4 + q // 4, (q % 4) * P:(q % 4 + 1) * P], n_sm[k % 2][:, p, b * P:(b + 1) * P], ident[:])
                    mm.then_inc(sig("nsa_pturned"), 1)
                    pe.wait_ge(*at("nsa_pT", k + 1, 8))
                    if k >= 2:
                        pe.wait_ge(*at("nsa_o", k - 1, 8))
                    for p in range(CH // 2):
                        g = p // 2
                        c0 = (CVS, CVW)[br] + g * HD
                        for b in range(t + 1):
                            mm = pe.matmul(ps[:, 6 + k % 2, p * HD:(p + 1) * HD], n_pT[k % 2][:, p, b, :], z[:, b, c0:c0 + HD],
                                           start=(b == 0), stop=(b == t))
                    mm.then_inc(sig("nsa_pv"), 1)
                end_stage(pe, "tensor")

            def act_(act):
                act.activation(n_gate, z[:, :, CGT:ZW], ACT.Sigmoid)
                act.wait_ge(*at("nsa_q", 1, 1))
                act.copy(n_qT.rearrange("p h n -> p (h n)"), ps[:, 1:3, :].rearrange("p a b -> p (a b)")).then_inc(sig("nsa_qT"), 1)
                act.wait_ge(cmp_w_used, l + 1)
                act.wait_ge(*at("nsa_hid0", 1, 1))
                act.activation(n_hid[:, :, 0:NCMP], ps[:, 5, 0:64].rearrange("p (q n) -> p q n", q=4)[:, :, 0:NCMP],
                               ACT.Gelu_apprx_tanh).then_inc(sig("nsa_gelu"), 1)
                act.wait_ge(*at("nsa_cmax", 1, 1))
                act.activation(n_sc, n_sc, ACT.Exp).then_inc(sig("nsa_cexp"), 1)
                act.wait_ge(*at("nsa_qr", 1, 1))
                act.copy(n_qrT.rearrange("p h n -> p (h n)"), ps[:, 1:3, :].rearrange("p a b -> p (a b)"))
                act.wait_ge(*at("nsa_k", 1, 1))
                act.copy(n_kT.rearrange("p k g n -> p (k g n)"), ps[:, 6:8, :].rearrange("p a b -> p (a b)")).then_inc(sig("nsa_kT"), 1)
                for k, (br, t, s) in enumerate(GROUPS):
                    nk = (t + 1) * P
                    act.wait_ge(*at("nsa_max", k + 1, 8))
                    for p in range(CH // 2):
                        ins = act.activation(n_sm[k % 2][:, p, 0:nk], n_sm[k % 2][:, p, 0:nk], ACT.Exp,
                                             bias=n_mx[:, 4 * k + p:4 * k + p + 1], accum_out=n_den[:, 4 * k + p:4 * k + p + 1])
                    ins.then_inc(sig("nsa_probs"), 1)
                    act.wait_ge(*at("nsa_pturned", k + 1, 8))
                    if t == 0:
                        ins = act.copy(n_pT[k % 2][:, :, 0, :], ps[:, 4, :].rearrange("p (h n) -> p h n", n=P))
                    else:
                        ins = act.copy(n_pT[k % 2].rearrange("p h b n -> p (h b n)"), ps[:, 4:6, :].rearrange("p a b -> p (a b)"))
                    ins.then_inc(sig("nsa_pT"), 1)
                end_stage(act, "scalar")

            def rotate(dve, dst, src, n):
                a = src.rearrange("p t (h n) -> p t h n", n=HD)
                o = dst.rearrange("p t (h n) -> p t h n", n=HD)
                a1, a2 = a[:, :, :, 0:ROPE_HALF], a[:, :, :, ROPE_HALF:2 * ROPE_HALF]
                c, s = [v[:].unsqueeze(2).to_broadcast([P, NT, n, ROPE_HALF]) for v in (cos_t, sin_t)]
                r = [n_rt[:, k, :, 0:n, :] for k in range(4)]
                dve.tensor_tensor(r[0], a1, c, ALU.mult)
                dve.tensor_tensor(r[1], a2, s, ALU.mult)
                dve.tensor_tensor(r[2], a1, s, ALU.mult)
                vstep(dve, dve.tensor_tensor(r[3], a2, c, ALU.mult))
                dve.tensor_tensor(o[:, :, :, 0:ROPE_HALF], r[0], r[1], ALU.subtract)
                ins = dve.tensor_tensor(o[:, :, :, ROPE_HALF:2 * ROPE_HALF], r[2], r[3], ALU.add)
                vstep(dve, ins)

            def dve_(dve):
                dve.wait_ge(*at("nsa_next", 1, 1))
                for t in range(NT):
                    dve.tensor_copy(n_kc2[:, t, :, 0, :], z[:, t, CKC:CKS].rearrange("p (q n) -> p q n", q=4))
                    ins = dve.tensor_copy(n_kc2[:, t, :, 1, :], ps[:, 0, t * S:(t + 1) * S].rearrange("p (q n) -> p q n", q=4))
                ins.then_inc(sig("nsa_pairs"), 1)
                dve.memset(n_hid, 0.0).then_inc(sig("nsa_hid0"), 1)
                dve.wait_ge(*at("nsa_blkT", 1, 1))
                for q in range(4):
                    rows = ps[:, 3 + q // 2, (q % 2) * S:(q % 2 + 1) * S]
                    src = bass.AP(tensor=rows.tensor, offset=rows.offset, ap=[list(rows.ap[0]), [2, 16], [CST, NCMP]])
                    ins = dve.tensor_tensor(n_blk[:, q], src, l_posT[:].unsqueeze(2).to_broadcast([P, 16, NCMP]), ALU.add)
                ins.then_inc(sig("nsa_blk"), 1)
                vstep(dve, dve.tensor_copy(n_qr, z[:, :, CQ:CKC]))
                rotate(dve, n_qr, z[:, :, CQ:CKC], CH)
                rotate(dve, z[:, :, CKS:CVS], z[:, :, CKS:CVS], CG)
                rotate(dve, z[:, :, CKW:CVW], z[:, :, CKW:CVW], CG)
                for t in range(NT):
                    for k, c0 in enumerate((CKS, CKW)):
                        keys = z[:, t, c0:c0 + CG * HD].rearrange("p (g n) -> p g n", g=CG)
                        ins = dve.tensor_copy(n_k2[:, t, k], keys.unsqueeze(2).to_broadcast([P, CG, 2, HD]))
                ins.then_inc(sig("nsa_rot"), 1)
                dve.wait_ge(*at("nsa_gelu", 1, 1))
                for g in range(CG):
                    for s in range(2):
                        ins = dve.tensor_copy(n_hv[:, s, 2 * g:2 * g + 2, :], n_hid[:, 2 + g, :].unsqueeze(1).to_broadcast([P, 2, 16]))
                ins.then_inc(sig("nsa_hid"), 1)
                dve.wait_ge(*at("nsa_cmp", 1, 1))
                dve.tensor_copy(n_kcT.rearrange("p g n -> p (g n)"), ps[:, 6, 0:CG * 16]).then_inc(sig("nsa_kc"), 1)
                dve.tensor_tensor(n_vbd, ps[:, 6, 64:64 + HD].unsqueeze(1).to_broadcast([P, CH, HD]),
                                  block16[:].unsqueeze(2).to_broadcast([P, CH, HD]), ALU.mult).then_inc(sig("nsa_vbd"), 1)
                dve.wait_ge(*at("nsa_sc", 1, 1))
                for s in range(2):
                    for t in range(NT):
                        c = t * 64
                        ins = dve.scalar_tensor_tensor(out=n_sc[:, t, 4 * s:4 * s + 4, :], in0=ps[:, 3 + s, c:c + 64].rearrange("p (h n) -> p h n", h=4),
                                                       scalar=SCALE, in1=cmp_ok[:, t, :].unsqueeze(1).to_broadcast([P, 4, 16]),
                                                       op0=ALU.mult, op1=ALU.mult)
                vstep(dve, ins)
                for t in range(NT):
                    ins = dve.tensor_tensor(n_sc[:, t], n_sc[:, t], cmp_neg[:, t, :].unsqueeze(1).to_broadcast([P, CH, 16]), ALU.add)
                vstep(dve, ins)
                sc16 = n_sc.rearrange("p t h n -> p (t h) n")
                vstep(dve, dve.tensor_reduce(n_cs[:, 0, :], sc16, AX, ALU.max))
                dve.tensor_tensor(sc16, sc16, n_cs[:, 0, :].unsqueeze(2).to_broadcast([P, 16, 16]), ALU.subtract).then_inc(sig("nsa_cmax"), 1)
                dve.wait_ge(*at("nsa_cexp", 1, 1))
                vstep(dve, dve.tensor_reduce(n_cs[:, 0, :], sc16, AX, ALU.add))
                vstep(dve, dve.reciprocal(n_cs[:, 1, :], n_cs[:, 0, :]))
                vstep(dve, dve.tensor_tensor(sc16, sc16, n_cs[:, 1, :].unsqueeze(2).to_broadcast([P, 16, 16]), ALU.mult))
                for t in range(NT):
                    ins = dve.tensor_tensor(n_sc[:, t], n_sc[:, t], cmp_ok[:, t, :].unsqueeze(1).to_broadcast([P, CH, 16]), ALU.mult)
                ins.then_inc(sig("nsa_pc"), 1)
                dve.wait_ge(*at("nsa_pcturned", 1, 1))
                dve.tensor_copy(n_pcT, ps[:, 0, 0:S]).then_inc(sig("nsa_pcT"), 1)
                dve.wait_ge(*at("nsa_oc", 1, 1))
                dve.wait_ge(*at("nsa_kT", 1, 1))
                for t in range(NT):
                    for s in range(2):
                        o = ps[:, 3 + t, s * 256:(s + 1) * 256].rearrange("p (h n) -> p h n", h=4)
                        ins = dve.tensor_tensor(y_of(t, s), o, gate_of(t, s, 0).unsqueeze(2).to_broadcast([P, 4, HD]), ALU.mult)
                ins.then_inc(sig("nsa_ocdone"), 1)
                dve.wait_ge(*at("nsa_ocdone", 1, 1))

                def finish(k):
                    br, t, s = GROUPS[k]
                    q = slice(4 * k, 4 * k + 4)
                    dve.wait_ge(*at("nsa_probs", k + 1, 8))
                    vstep(dve, dve.reciprocal(n_rd[:, q], n_den[:, q]))
                    vstep(dve, dve.tensor_tensor(n_rd[:, q], n_rd[:, q], gate_of(t, s, 1 + br), ALU.mult))
                    dve.wait_ge(*at("nsa_pv", k + 1, 8))
                    vstep(dve, dve.tensor_tensor(n_o, ps[:, 6 + k % 2, 0:256].rearrange("p (h n) -> p h n", h=4),
                                                 n_rd[:, q].unsqueeze(2).to_broadcast([P, 4, HD]), ALU.mult))
                    ins = dve.tensor_tensor(y_of(t, s), y_of(t, s), n_o, ALU.add)
                    ins.then_inc(sig("nsa_o"), 1)
                    dve.wait_ge(*at("nsa_o", k + 1, 8))

                for k, (br, t, s) in enumerate(GROUPS):
                    nk = (t + 1) * P
                    dve.wait_ge(*at("nsa_scores", k + 1, 8))
                    if k >= 2:
                        dve.wait_ge(*at("nsa_pturned", k - 1, 8))
                    for p in range(CH // 2):
                        c = p * nk
                        ins = dve.tensor_tensor_reduce(out=n_sm[k % 2][:, p, 0:nk], in0=ps[:, 2 * (k % 2) + c // 512, c % 512:c % 512 + nk],
                                                       in1=causal_neg[:, S - nk:S], scale=SCALE, scalar=-3e38, op0=ALU.add, op1=ALU.max,
                                                       accum_out=n_mx[:, 4 * k + p:4 * k + p + 1])
                    vstep(dve, ins)
                    dve.tensor_scalar(n_mx[:, 4 * k:4 * k + 4], n_mx[:, 4 * k:4 * k + 4], -1.0, None, ALU.mult).then_inc(sig("nsa_max"), 1)
                    if k >= 1:
                        finish(k - 1)
                finish(len(GROUPS) - 1)
                end_stage(dve, "vector")

            return pe_, act_, dve_, idle_pool

        MP = Arena(arena)
        MP.at = 8192
        e_gate = MP.take(NT, D)
        e_p = MP.take(NT, PLE)
        e_pT = MP.take(PLE // P, S)
        e_t = MP.take(NT, D)

        def ple_gate_act(act, j, src):
            return act.activation(e_gate[:, j.tile, j.col:j.col + j.n], src, ACT.Sigmoid)

        def ple_turn(l):
            def pe_(pe):
                for c in range(PLE // P):
                    for t in range(NT):
                        mm = pe.transpose(ps[:, 4, c * S + t * P:c * S + (t + 1) * P], e_p[:, t, c::PLE // P], ident[:])
                mm.then_inc(sig("ple_turned"), 1)
                end_stage(pe, "tensor")

            def act_(act):
                act.wait_ge(sig("ple_turned"), l + 1)
                act.copy(e_pT.rearrange("p c s -> p (c s)"), ps[:, 4, :])
                end_stage(act, "scalar")

            return pe_, act_, lambda dve: end_stage(dve, "vector"), idle_pool

        def ple_copy(dve, j, src):
            t = e_t[:, j.tile, j.col:j.col + j.n]
            vstep(dve, dve.tensor_tensor(t, src, e_gate[:, j.tile, j.col:j.col + j.n], ALU.mult))
            cols = x[:, j.tile, j.col:j.col + j.n]
            return dve.tensor_tensor(cols, cols, t, ALU.add)

        def gates_act(act):
            act.wait_ge(evac_dve, jobs_of["gates"][-1].evac)
            act.activation(c_gate, c_gate, ACT.Sigmoid)

        def gates_load(act):
            act.dma_start(c_bias, d["b_branch_gate"].to_broadcast([P, 2 * D])).then_inc(sig("gate_bias"), 16)

        def with_before(stage, act_first=None, dve_first=None, act_last=None):
            pe_, act_, dve_, pool_ = stage

            def act2(act):
                if act_first:
                    act_first(act)
                act_(act)

            def dve2(dve):
                if dve_first:
                    dve_first(dve)
                dve_(dve)

            return pe_, act2, dve2, pool_

        def sum_dve(dve):
            dve.wait_ge(evac_dve, jobs_of["y_att"][-1].evac)
            for t in range(NT):
                dve.tensor_tensor(c_y[:, t, :], c_y[:, t, :], c_t[:, t, :], ALU.add)

        def za_copy(act, j, src):
            return act.copy(za[:, j.tile, j.col:j.col + j.n], src)

        def zb_copy_act(act, j, src):
            return act.copy(zb[:, j.tile, j.col:j.col + j.n], src)

        def zb_copy_dve(dve, j, src):
            return dve.tensor_copy(zb[:, j.tile, j.col:j.col + j.n], src)

        def params_wait(act):
            act.wait_ge(sig("params"), 16 * len(P1_LOADS))
            act.wait_ge(sig("layer_params"), 16 * N_LAYER_LOADS)

        MO = Arena(arena)
        o_gain = MO.take(D)
        o_y = MO.take(NT, D)

        def final_stage():
            n = NORMS.index("final")

            def act_(act):
                act.dma_start(o_gain, d["g_final_2"].rearrange("(a n) -> a n", a=1).to_broadcast([P, D])).then_inc(sig("final_gain"), 16)
                act_norm_stats(act, n)
                act.wait_ge(sig("final_out"), 1)
                act.dma_start(out[0].rearrange("(t p) n -> p t n", p=P), o_y).then_inc(sig("stored"), 16)
                act.wait_ge(sig("stored"), 16)
                end_stage(act, "scalar")

            def dve_(dve):
                vstep(dve, dve_norm_scale(dve, n, o_y))
                dve.wait_ge(sig("final_gain"), 16)
                for t in range(NT):
                    ins = dve.tensor_tensor(o_y[:, t, :], o_y[:, t, :], o_gain, ALU.mult)
                ins.then_inc(sig("final_out"), 1)
                end_stage(dve, "vector")

            return (lambda pe: end_stage(pe, "tensor")), act_, dve_, idle_pool

        stages = [
            (setup_pe, setup_act, setup_dve, setup_pool),
            stage_norm("n1", g1T),
            stage_project("in_a", hT, za_copy, act_more=params_wait, dve_more=masks_dve),
            (gla_pe, gla_act, gla_dve, gla_pool),
            stage_project("in_b", hT, zb_copy_act, zb_copy_dve),
            (dil_pe, dil_act, dil_dve, idle_pool),
            with_before(stage_project("gates", hT, dve_copy=gates_copy, act_more=gates_act), act_first=gates_load,
                        dve_first=lambda dve: dve.wait_ge(sig("gate_bias"), 16)),
            stage_project("y_gla", ogT, dve_copy=y_gla_copy),
            stage_project("y_att", oaT, dve_copy=y_att_copy, dve_more=sum_dve),
            stage_turn("ym", c_y),
            stage_project("out_1", hT, dve_copy=residual_copy),
            stage_norm("n2", g2T),
            ((lambda pe: router_pe(pe, r1_w, 36, 0)), router1_act, router1_dve, idle_pool),
            stage_ffn(ffn1, 0),
        ]
        for l in range(LAYERS):
            first = rope_act if l == 0 else None
            stages += [
                with_before(stage_norm(f"mix{l}", l_gT[:, 3 * l:3 * l + 1, :].rearrange("p a c -> p (a c)")),
                            act_first=first, dve_first=rope_dve if l == 0 else None),
                stage_project(f"in_{l}", hT, z_copy_act, z_copy_dve),
                gating(l),
                rwkv(l),
                nsa(l),
                with_before(stage_turn(f"cat{l}", ycat), act_first=(lambda act: load_layer(act, 1)) if l == 0 else None),
                stage_project(f"out_{l}_2", hT, dve_copy=residual_copy),
                stage_norm(f"ffn{l}", l_gT[:, 3 * l + 1:3 * l + 2, :].rearrange("p a c -> p (a c)")),
            ]
            if l % 2:
                stages.append(((lambda pe: router_pe(pe, r2_w, NE2, 1)), router2_act, router2_dve, idle_pool))

            def ple_load(act, l=l):
                act.dma_start(e_p, d["p_2"][l, 0].rearrange("(t p) n -> p t n", p=P)).then_inc(sig("ple_rows"), 16)
                if l == 0:
                    act.wait_ge(sig("layer_params"), 2 * 16 * N_LAYER_LOADS)

            def ple_wait(act, l=l):
                act.wait_ge(sig("ple_rows"), 16 * (l + 1))

            stages += [
                stage_ffn(ffn2[l], l + 1),
                with_before(stage_norm(f"ple{l}", l_gT[:, 3 * l + 2:3 * l + 3, :].rearrange("p a c -> p (a c)")), act_first=ple_load),
                stage_project(f"ple_g{l}", hT, ple_gate_act, act_more=ple_wait),
                ple_turn(l),
                stage_project(f"ple_p{l}", e_pT, dve_copy=ple_copy),
            ]
        stages.append(final_stage())

        block = ctx.enter_context(nc.Block())

        @block.sync
        def _(sp):
            stream(sp, units[0:n_units_1])
            stream_ffn(sp, ffn1)
            at = n_units_1
            for l in range(LAYERS):
                stream(sp, units[at:n_units_2[l]])
                stream_ffn(sp, ffn2[l])
                stream(sp, units[n_units_2[l]:n_units_3[l]])
                at = n_units_3[l]

        @block.tensor
        def _(pe):
            for s in stages:
                s[0](pe)

        @block.scalar
        def _(act):
            for s in stages:
                s[1](act)

        @block.vector
        def _(dve):
            for s in stages:
                s[2](dve)

        @block.gpsimd
        def _(pool):
            for s in stages:
                s[3](pool)


NAMES = """x norm1_g w_in w_gla_a2 b_gla_a gla_out_norm_g dil_q_norm_g dil_k_norm_g w_proj_gla
    w_proj_attn w_branch_gate b_branch_gate w_out norm2_g w_router_group b_router_group
    w_router_expert b_router_expert w_gate w_up w_down p_2 positions_2 g_mix_2 w_in_2
    w_out_2 gm_ln_g_2 gm_ln_b_2 gm_ws_2 gm_bs_2 rw_mu_2 rw_w0_2 rw_w_up_2 rw_a0_2
    rw_a_up_2 rw_g_up_2 rw_k_k_2 rw_k_a_2 rw_r_k_2 rw_gn_g_2 rw_gn_b_2 nsa_cmp_pos_2
    nsa_kc_w1_2 nsa_kc_w2_2 nsa_vc_w1_2 nsa_vc_w2_2 g_ffn_2 ffn_w1_2 ffn_w3_2 ffn_w2_2
    router_w_2 router_b_2 moe_w1_2 moe_w3_2 moe_w2_2 g_ple_2 ple_gate_w_2 ple_proj_w_2
    g_final_2""".split()


def kernel(**inputs):
    import concourse.bacc as bacc
    from concourse.bass_utils import run_bass_kernel_spmd

    nc = bacc.Bacc("TRN2", target_bir_lowering=False, num_devices=1)
    arrays = {n: np.ascontiguousarray(inputs[n]) for n in NAMES}
    d = {n: nc.dram_tensor(f"in_{n}", a.shape, mybir.dt.from_np(a.dtype), kind="ExternalInput").ap()
         for n, a in arrays.items()}
    out = nc.dram_tensor("out", (1, S, D), F32, kind="ExternalOutput").ap()
    emit(nc, d, out)
    r = run_bass_kernel_spmd(nc, [{f"in_{n}": a for n, a in arrays.items()}], core_ids=[0])
    return r.results[0]["out"]
```

```python
from contextlib import ExitStack

import numpy as np

import concourse.bass as bass
from concourse import mybir

F32 = mybir.dt.float32
I32 = mybir.dt.int32
F32R = mybir.dt.float32r
ALU = mybir.AluOpType
ACT = mybir.ActivationFunctionType
AX = mybir.AxisListType.X

P = 128
S = 256
NT = S // P
D = 1024
KC = D // P
EPS = 1e-6
BIG = 1e30

GH, GD, RANK, TAU, GCH = 4, 128, 16, 16.0, 16
GW = GH * GD
NCH = P // GCH
DG, DH, DD = 3, 4, 128
SLOPES = [2.0 ** (-8.0 * (i + 1) / (DG * DH)) for i in range(DG * DH)]
N_GROUPS, PER_GROUP = 4, 8
NE1, DE1 = 32, 512
ZA = 4 * GW + RANK
ZB = 9 * GW

LAYERS = 2
HD = 64
AH, BH, CH, CG = 4, 4, 8, 2
AW, BW, CW = AH * HD, BH * HD, CH * HD
RC = 64
ZW = 2840
ZB0, ZC0 = 2 * AW, 2 * AW + 1024
CQ, CKC, CVC, CKS, CVS, CKW, CVW, CGT = [ZC0 + o for o in (0, 512, 640, 768, 896, 1024, 1152, 1280)]
NCMP, CB, CST = 15, 32, 16
DFF, NE2 = 2816, 8
PLE = 256
LN_EPS, GN_EPS = 1e-5, 64e-5
ROPE_HALF = HD // 8
INV_FREQ = [float(np.float32(1.0) / np.float32(500000.0) ** np.float32(2 * i / (2 * ROPE_HALF))) for i in range(ROPE_HALF)]

SLOTS = 3
FB = 256
GU = KC * 2 * FB
DN = FB // P * D
SLOT = GU + DN
NB1, NB2 = DE1 // FB, DFF // FB


class Arena:

    def __init__(self, flat):
        self.flat, self.at = flat, 0

    def take(self, *shape):
        n = int(np.prod(shape))
        view = self.flat[:, self.at:self.at + n]
        self.at += n
        assert self.at <= self.flat.shape[1], (self.at, self.flat.shape)
        if len(shape) == 2:
            return view.rearrange("p (a b) -> p a b", a=shape[0])
        if len(shape) == 3:
            return view.rearrange("p (a b c) -> p a b c", a=shape[0], b=shape[1])
        if len(shape) == 4:
            return view.rearrange("p (a b c d) -> p a b c d", a=shape[0], b=shape[1], c=shape[2])
        return view


class Unit:

    def __init__(self, slot, copies, ready, after):
        self.slot, self.copies, self.ready, self.after = slot, copies, ready, after


class Job:

    def __init__(self, unit, first, off, n, tile, col, index, engine, evac):
        self.unit, self.first, self.off, self.n, self.tile, self.col = unit, first, off, n, tile, col
        self.index, self.engine, self.evac = index, engine, evac


def emit(nc, d, out):
    ctx = ExitStack()
    with ctx:
        ctx.enter_context(nc.allow_non_contiguous_dma(reason="small per-feature parameters"))

        def sb(name, shape, dt=F32):
            return ctx.enter_context(nc.sbuf_tensor(name, shape, dt))

        def sem(name):
            return ctx.enter_context(nc.semaphore(name))

        ps = ctx.enter_context(nc.psum_tensor("ps", [P, 8, 512], F32))

        def sb_split(name, shape):
            t = sb(name, shape)
            at = nc.sbuf_base - 4 * int(np.prod(shape[1:]))
            return t, nc.alloc_sbuf_tensor_at(f"{name}_parts", shape, F32R, offset=at)

        ring, ring_parts = sb_split("ring", [P, SLOTS, SLOT])
        x = sb("x", [P, NT, D])
        hT, hT_parts = sb_split("hT", [P, KC, S])
        ident = sb("ident", [P, P])
        diff = sb("diff", [P, P])
        xor_f = sb("xor_f", [P, P])
        gla_mask = sb("gla_mask", [P, P])
        tri_inc = sb("tri_inc", [P, P])
        tri_str = sb("tri_str", [P, P])
        same_chunk = sb("same_chunk", [P, P])
        causal_up = sb("causal_up", [P, P])
        low_b = sb("low_b", [P, 6, P])
        up_b = sb("up_b", [P, 6, P])
        shift_dn = sb("shift_dn", [P, P])
        shift_dn_edge = sb("shift_dn_edge", [P, P])
        shift_up = sb("shift_up", [P, P])
        shift_up_edge = sb("shift_up_edge", [P, P])
        negdist = sb("negdist", [P, S])
        dil_mask = sb("dil_mask", [P, DG, S])
        causal_neg = sb("causal_neg", [P, S])
        block16 = sb("block16", [P, NCH])
        half_ind = sb("half_ind", [P, 2])
        scan_keep = sb("scan_keep", [P, S])
        cmp_ok = sb("cmp_ok", [P, NT, 16])
        cmp_neg = sb("cmp_neg", [P, NT, 16])
        desc = sb("desc", [P, 32])
        ones = sb("ones", [P, P])
        small = sb("small", [P, 128])
        gate_w = sb("gate_w", [P, NT, 32])
        g1T = sb("g1T", [P, KC])
        g2T = sb("g2T", [P, KC])
        gla_bT = sb("gla_bT", [P, GH])
        gla_og = sb("gla_og", [P, GD])
        gla_a2 = sb("gla_a2", [RANK, GW])
        dil_gT = sb("dil_gT", [P, 2, DG])
        r1_w = sb("r1_w", [P, KC, 36])
        r1_b = sb("r1_b", [P, 36])
        l_gT = sb("l_gT", [P, 3 * LAYERS, KC])
        l_mu = sb("l_mu", [P, 1024])
        l_row = sb("l_row", [P, 9, 256])
        l_bsT = sb("l_bsT", [P, AH])
        l_lora = sb("l_lora", [P, 2, 256])
        l_ws = sb("l_ws", [P, AH, P])
        l_posT = sb("l_posT", [P, 16])
        l_w2 = sb("l_w2", [P, 3, HD])
        r2_w = sb("r2_w", [P, KC, NE2])
        r2_b = sb("r2_b", [P, NE2])
        pos_i = sb("pos_i", [P, NT], I32)
        most = sb("most", [P, 2], I32)
        slot_no = sb("slot_no", [P, P])
        freq = sb("freq", [P, ROPE_HALF])
        cos_t = sb("cos_t", [P, NT, ROPE_HALF])
        sin_t = sb("sin_t", [P, NT, ROPE_HALF])
        n_arena = (nc.sbuf_bytes_remaining - 512) // 4 // 8 * 8
        arena, arena_parts = sb_split("arena", [P, n_arena])

        stage_done = sem("stage_done")
        slot_ready = [sem(f"slot{s}_ready") for s in range(SLOTS)]
        proj_done = sem("proj_done")
        evac_act = sem("evac_act")
        evac_dve = sem("evac_dve")
        ffn_used = sem("ffn_used")
        cmp_w_used = sem("cmp_w_used")
        dve_step = sem("dve_step")
        act_step = sem("act_step")
        sems = {}

        step_place = {}

        def count_steps(name, order):
            total = sum(order.values())
            at = 0
            for step, n in order.items():
                step_place[step] = (name, at, total)
                at += n

        count_steps("gla_tensor", {"gla_turned": 3, "gla_logit": 1, "gla_scores": 1, "gla_ke_turned": 1,
                                   "gla_o_turned": 1, "gla_out": 1})
        count_steps("gla_scalar", {"gla_lr": 1, "gla_ln": 1, "gla_exp": 3, "gla_ke": 1, "gla_oT": 1, "gla_silu": 1,
                                   "gla_sq": 1, "gla_rt": 1})
        count_steps("gla_vector", {"gla_y": 1, "gla_cum": 2, "gla_scaled": 1, "gla_att": 1, "gla_ms": 1, "gla_gated": 1})
        count_steps("rw_tensor", {"rw_shift": 1, "rw_loT_psum": 1, "rw_lin": 1, "rw_cum": 1, "rw_turned": 4, "rw_Y": 1})
        count_steps("rw_scalar", {"rw_lora": 1, "rw_sig": 2, "rw_kkrt": 1, "rw_total": 1, "rw_exp": 1, "rw_AT": 1,
                                  "rw_sd": 1})
        count_steps("rw_vector", {"rw_mixed": 1, "rw_loT": 1, "rw_kk2": 1, "rw_logit": 1, "rw_lw": 1, "rw_toend": 1,
                                  "rw_rkab": 1, "rw_BT": 1, "rw_var": 1})
        count_steps("nsa_tensor", {"nsa_next": 1, "nsa_q": 1, "nsa_blkT": 1, "nsa_cmp": 1, "nsa_sc": 1, "nsa_qr": 1,
                                   "nsa_k": 1, "nsa_pcturned": 1, "nsa_oc": 1})
        count_steps("nsa_scalar", {"nsa_qT": 1, "nsa_gelu": 1, "nsa_cexp": 1, "nsa_kT": 1})
        count_steps("nsa_vector", {"nsa_pairs": 1, "nsa_hid0": 1, "nsa_blk": 1, "nsa_rot": 1, "nsa_hid": 1, "nsa_kc": 1,
                                   "nsa_vbd": 1, "nsa_cmax": 1, "nsa_pc": 1, "nsa_pcT": 1, "nsa_ocdone": 1})

        def sig(name):
            name = step_place[name][0] if name in step_place else name
            if name not in sems:
                sems[name] = sem(name)
            return sems[name]

        def ended(name, k=1, layer=0, per_layer=0):
            if name in step_place:
                _, before, total = step_place[name]
                return sig(name), layer * total + before + k
            return sig(name), layer * per_layer + k

        units, jobs_of = [], {}
        slot_val = [0] * SLOTS
        slot_free = [None] * SLOTS
        count = {"slot": 0, "job": 0, "act": 0, "dve": 0}

        def new_unit(copies):
            s = count["slot"] % SLOTS
            count["slot"] += 1
            slot_val[s] += 16 * len(copies)
            u = Unit(s, copies, slot_val[s], slot_free[s])
            units.append(u)
            return u

        def project(name, weight, kc, width, block, engines):
            jobs = []
            rows = weight.rearrange("(p c) n -> p c n", c=kc)
            for c0 in range(0, width, block):
                n = min(block, width - c0)
                s = count["slot"] % SLOTS
                dst = ring[:, s, 0:kc * n].rearrange("p (c n) -> p c n", c=kc)
                u = new_unit([(dst, rows[:, :, c0:c0 + n])])
                u.view = dst
                first = True
                for off in range(0, n, 512):
                    for t in range(NT):
                        e = engines[len(jobs) % len(engines)]
                        count[e] += 1
                        jobs.append(Job(u, first, off, min(512, n - off), t, c0 + off, count["job"], e, count[e]))
                        count["job"] += 1
                        first = False
                slot_free[s] = (proj_done, count["job"])
            jobs_of[name] = jobs

        class Ffn:
            pass

        def weights_of(w1, w3, w2):
            f = Ffn()
            f.w1 = w1.rearrange("e (p c) n -> e p c n", c=KC)
            f.w3 = w3.rearrange("e (p c) n -> e p c n", c=KC)
            f.w2 = w2.rearrange("e (b p c) n -> e b p (c n)", p=P, c=FB // P)
            return f

        def align_slots():
            while count["slot"] % SLOTS:
                count["slot"] += 1

        def plan_dense(w1, w3, w2, nb):
            align_slots()
            f = weights_of(w1, w3, w2)
            f.steps = nb
            f.slots = [k % SLOTS for k in range(nb)]
            f.ready0, f.free0 = list(slot_val), list(slot_free)
            for k in range(nb):
                slot_val[k % SLOTS] += 48
                slot_free[k % SLOTS] = (ffn_used, k + 1)
            return f

        moe_counts = {}

        def plan_moe(name, w1, w3, w2, buckets, per_bucket, nb, gain):
            align_slots()
            f = weights_of(w1, w3, w2)
            f.name, f.buckets, f.e, f.nb, f.gain = name, buckets, per_bucket, nb, gain
            f.number = 1 if name == "moe1" else 2
            f.steps = per_bucket * nb
            f.free0 = list(slot_free)
            f.slots = [k % SLOTS for k in range(f.steps)]
            f.fills = [f.slots.count(s) for s in range(SLOTS)]
            f.nth = [f.slots[:k + 1].count(s) for k, s in enumerate(f.slots)]
            f.before = dict(moe_counts)
            for n in ("hid", "turned", "hidT", "hidT_upper", "silu", "gu", "used"):
                moe_counts[n] = f.before.get(n, 0) + f.buckets * f.steps
            for n in ("rows", "rows_upper", "sel", "gathered", "places", "sel_turned", "y"):
                moe_counts[n] = f.before.get(n, 0) + f.buckets
            for n in ("upper", "split"):
                moe_counts[n] = f.before.get(n, 0) + 6 * f.buckets * f.steps
            moe_counts["scattered"] = f.before.get("scattered", 0) + 4 * f.buckets
            moe_counts["added"] = f.before.get("added", 0) + 4 * f.buckets + 4
            for s in range(SLOTS):
                moe_counts[f"slot{s}_ready"] = f.before.get(f"slot{s}_ready", 0) + 32 * f.buckets * f.fills[s]
                moe_counts[f"down{s}_ready"] = f.before.get(f"down{s}_ready", 0) + 16 * f.buckets * f.fills[s]
                slot_free[s] = (sig("moe_used"), moe_counts["used"])
            return f

        project("in_a", d["w_in"][0][:, 0:ZA], KC, ZA, 512, ["act"])
        project("in_b", d["w_in"][0][:, ZA:ZA + ZB], KC, ZB, 512, ["act", "dve"])
        project("gates", d["w_branch_gate"][0], KC, 2 * D, 512, ["dve"])
        project("y_gla", d["w_proj_gla"][0], GW // P, D, D, ["dve"])
        project("y_att", d["w_proj_attn"][0], GW // P, D, D, ["dve"])
        project("out_1", d["w_out"][0], KC, D, 512, ["dve"])
        moe1 = plan_moe("moe1", d["w_gate"][0], d["w_up"][0], d["w_down"][0], N_GROUPS, PER_GROUP, NB1, g2T[:])
        n_units_1 = len(units)
        n_units_2, cmp_unit = [0, 0], [None, None]
        n_units_3 = [0, 0]
        for l in range(LAYERS):
            project(f"in_{l}", d["w_in_2"][l], KC, ZW, 512, ["act", "dve"])
            s = count["slot"] % SLOTS
            dst = ring[:, s, 0:2 * 16 * P].rearrange("p (k i h) -> p k i h", k=2, i=16)
            cmp_unit[l] = new_unit([(dst[:, k], d[w][l].rearrange("(i p) h -> p i h", p=P))
                                    for k, w in enumerate(("nsa_kc_w1_2", "nsa_vc_w1_2"))])
            cmp_unit[l].view = dst
            slot_free[s] = (cmp_w_used, l + 1)
            project(f"out_{l}_2", d["w_out_2"][l], KC, D, 512, ["dve"])
            n_units_2[l] = len(units)
            if l == 0:
                ffn = plan_dense(d["ffn_w1_2"], d["ffn_w3_2"], d["ffn_w2_2"], NB2)
            else:
                moe2 = plan_moe("moe2", d["moe_w1_2"][0], d["moe_w3_2"][0], d["moe_w2_2"][0], NE2, 1, NB2,
                                l_gT[:, 3 * l + 1:3 * l + 2, :].rearrange("p a c -> p (a c)"))
            project(f"ple_g{l}", d["ple_gate_w_2"][l], KC, D, 512, ["act"])
            project(f"ple_p{l}", d["ple_proj_w_2"][l], PLE // P, D, D, ["dve"])
            n_units_3[l] = len(units)

        stage_no = {"tensor": 0, "vector": 0, "scalar": 0, "gpsimd": 0}

        def end_stage(eng, name):
            stage_no[name] += 1
            eng.drain().then_inc(stage_done, 1)
            eng.wait_ge(stage_done, 4 * stage_no[name])

        steps = {"dve": 0, "act": 0}

        def vstep(dve, ins):
            steps["dve"] += 1
            ins.then_inc(dve_step, 1)
            dve.wait_ge(dve_step, steps["dve"])

        def astep(act, ins):
            steps["act"] += 1
            ins.then_inc(act_step, 1)
            act.wait_ge(act_step, steps["act"])

        def stream(sp, lot):
            for u in lot:
                if u.after:
                    sp.wait_ge(*u.after)
                for dst, src in u.copies:
                    sp.dma_start(dst, src).then_inc(slot_ready[u.slot], 16)

        def load_gu(sp, f, slot, e, b, ready):
            gu = ring[:, slot, 0:GU].rearrange("p (c k n) -> p c k n", c=KC, k=2)
            cols = slice(b * FB, b * FB + FB)
            for k, w in enumerate((f.w1, f.w3)):
                w = w[e] if isinstance(e, int) else w[bass.ds(e, 1)].rearrange("a p c n -> (a p) c n")
                sp.dma_start(gu[:, :, k, :], w[:, :, cols]).then_inc(ready, 16)

        def load_down(sp, f, slot, e, b, ready):
            w = f.w2[e] if isinstance(e, int) else f.w2[bass.ds(e, 1)].rearrange("a b p n -> (a b) p n")
            sp.dma_start(ring[:, slot, GU:SLOT], w[b]).then_inc(ready, 16)

        def stream_dense(sp, f):
            for k in range(f.steps):
                slot = k % SLOTS
                if k >= SLOTS:
                    sp.wait_ge(ffn_used, k - SLOTS + 1)
                else:
                    sp.wait_ge(*f.free0[slot])
                load_gu(sp, f, slot, 0, k, slot_ready[slot])
                load_down(sp, f, slot, 0, k, slot_ready[slot])

        def stream_bucket(sp, f, m, g):
            def wait_free(step, k):
                users = [q for q in range(f.steps) if f.slots[q] == f.slots[k]]
                before = [q for q in users if q < k]
                if before:
                    sp.wait_ge(*m.at(step, g * f.steps + before[-1] + 1))
                elif not isinstance(g, int) or g > 0:
                    sp.wait_ge(*m.at(step, g * f.steps - f.steps + users[-1] + 1))

            def down(k):
                wait_free("used", k)
                load_down(sp, f, f.slots[k], g * f.e + k // f.nb, k % f.nb, m(f"down{f.slots[k]}_ready"))

            for k, slot in enumerate(f.slots):
                wait_free("gu", k)
                load_gu(sp, f, slot, g * f.e + k // f.nb, k % f.nb, m(f"slot{slot}_ready"))
                if k:
                    down(k - 1)
            down(f.steps - 1)

        def stream_moe(sp, f):
            for s in range(SLOTS):
                sp.wait_ge(*f.free0[s])
            m = Pass(f, 0)
            stream_bucket(sp, f, m, 0)
            with sp.Fori(1, f.buckets) as g:
                stream_bucket(sp, f, m, g)
            sp.wait_ge(sig("counted"), f.number)
            with overfull(sp, f):
                sp.wait_ge(*m.at("used", f.buckets * f.steps))
                m2 = Pass(f, 1)
                stream_bucket(sp, f, m2, 0)
                with sp.Fori(1, f.buckets) as g:
                    stream_bucket(sp, f, m2, g)
                sp.wait_ge(*m2.at("used", f.buckets * f.steps))
            sp.end_ifs()
            if f is moe1:
                sp.sem_inc(sig("rest_streamed"), 1)

        class Pass:

            def __init__(self, f, turn):
                self.prefix = ("moe", "moe_rest")[turn]
                self.before = {} if turn else f.before

            def __call__(self, name):
                return sig(f"{self.prefix}_{name}")

            def at(self, name, value):
                return self(name), self.before.get(name, 0) + value

        def overfull(eng, f):
            c = 0 if f.name == "moe1" else 1
            return eng.If(eng.value_load(most[0:1, c:c + 1], min_val=0, max_val=S) >= P + 1)

        hT_flat = hT[:].rearrange("p c s -> p (c s)")

        def pe_project(pe, name, xT):
            jobs = jobs_of[name]
            for q, j in enumerate(jobs):
                if j.first:
                    pe.wait_ge(slot_ready[j.unit.slot], j.unit.ready)
                if q >= 4:
                    p = jobs[q - 4]
                    pe.wait_ge(evac_act if p.engine == "act" else evac_dve, p.evac)
                kc = j.unit.view.shape[1]
                for c in range(kc):
                    mm = pe.matmul(ps[:, q % 4, 0:j.n], xT[:, c, j.tile * P:(j.tile + 1) * P],
                                   j.unit.view[:, c, j.off:j.off + j.n], start=(c == 0), stop=(c == kc - 1))
                mm.then_inc(proj_done, 1)

        def evacuate(eng, name, engine, copy):
            for q, j in enumerate(jobs_of[name]):
                if j.engine == engine:
                    eng.wait_ge(proj_done, j.index + 1)
                    copy(j, ps[:, q % 4, 0:j.n]).then_inc(evac_act if engine == "act" else evac_dve, 1)

        nt_xn = arena[:, 0:NT * D].rearrange("p (t n) -> p t n", t=NT)
        nt_sq = arena[:, NT * D:NT * D + D]

        def pe_transpose_x(pe, src, kc, n, ready, value):
            pe.wait_ge(ready, value)
            for c in range(kc):
                for t in range(NT):
                    mm = pe.transpose(ps[:, c // 2, (c % 2) * S + t * P:(c % 2) * S + (t + 1) * P],
                                      src[:, t, c::kc], ident[:])
                mm.then_inc(sig("xT_psum"), 1)

        def pe_norm(pe, n):
            pe_transpose_x(pe, nt_xn, KC, n, sig("norm_xn"), n + 1)

        def evac_norm(eng, engine, base, gain, kc=KC):
            for b in range(0 if engine == "act" else 1, kc // 2, 2):
                eng.wait_ge(sig("xT_psum"), base + 2 * b + 2)
                for c in (2 * b, 2 * b + 1):
                    src = ps[:, b, (c % 2) * S:(c % 2 + 1) * S]
                    if engine == "act":
                        if gain is None:
                            eng.copy(hT[:, c, :], src)
                        else:
                            eng.activation(hT[:, c, :], src, ACT.Identity, scale=gain[:, c:c + 1])
                    elif gain is None:
                        eng.tensor_copy(hT[:, c, :], src)
                    else:
                        eng.tensor_scalar(hT[:, c, :], src, gain[:, c:c + 1], None, ALU.mult)

        def act_norm_stats(act, n):
            for t in range(NT):
                ins = act.activation(nt_sq, x[:, t, :], ACT.Square, accum_out=small[:, t:t + 1])
                if t + 1 < NT:
                    astep(act, ins)
            ins.then_inc(sig("norm_sq"), 1)
            act.wait_ge(sig("norm_ms"), n + 1)
            act.activation(small[:, 4:6], small[:, 2:4], ACT.Sqrt).then_inc(sig("norm_rt"), 1)

        def dve_norm_scale(dve, n, dst):
            dve.wait_ge(sig("norm_sq"), n + 1)
            dve.tensor_scalar(small[:, 2:4], small[:, 0:2], 1.0 / D, EPS, ALU.mult, ALU.add).then_inc(sig("norm_ms"), 1)
            dve.wait_ge(sig("norm_rt"), n + 1)
            vstep(dve, dve.reciprocal(small[:, 6:8], small[:, 4:6]))
            for t in range(NT):
                ins = dve.tensor_scalar(dst[:, t, :], x[:, t, :], small[:, 6 + t:7 + t], None, ALU.mult)
            return ins

        XT_ORDER, XT_AT = [], {}

        def xt(name, kc):
            XT_AT[name] = sum(k for _, k in XT_ORDER)
            XT_ORDER.append((name, kc))

        xt("n1", KC), xt("ym", KC), xt("n2", KC)
        for l in range(LAYERS):
            xt(f"mix{l}", KC), xt(f"cat{l}", KC), xt(f"ffn{l}", KC), xt(f"ple{l}", KC)
        NORMS = ["n1", "n2"] + [f"{k}{l}" for l in range(LAYERS) for k in ("mix", "ffn", "ple")] + ["final"]

        def stage_norm(name, gain):
            n = NORMS.index(name)

            def pe_(pe):
                pe_norm(pe, n)
                end_stage(pe, "tensor")

            def act_(act):
                act_norm_stats(act, n)
                evac_norm(act, "act", XT_AT[name], gain)
                end_stage(act, "scalar")

            def dve_(dve):
                dve_norm_scale(dve, n, nt_xn).then_inc(sig("norm_xn"), 1)
                evac_norm(dve, "dve", XT_AT[name], gain)
                end_stage(dve, "vector")

            def pool_(pool):
                end_stage(pool, "gpsimd")

            return pe_, act_, dve_, pool_

        def stage_turn(name, src):
            def pe_(pe):
                for c in range(KC):
                    for t in range(NT):
                        mm = pe.transpose(ps[:, c // 2, (c % 2) * S + t * P:(c % 2) * S + (t + 1) * P],
                                          src[:, t, c::KC], ident[:])
                    mm.then_inc(sig("xT_psum"), 1)
                end_stage(pe, "tensor")

            def act_(act):
                evac_norm(act, "act", XT_AT[name], None)
                end_stage(act, "scalar")

            def dve_(dve):
                evac_norm(dve, "dve", XT_AT[name], None)
                end_stage(dve, "vector")

            def pool_(pool):
                end_stage(pool, "gpsimd")

            return pe_, act_, dve_, pool_

        def stage_project(name, xT, act_copy=None, dve_copy=None, act_more=None, dve_more=None):
            def pe_(pe):
                pe_project(pe, name, xT)
                end_stage(pe, "tensor")

            def act_(act):
                if act_copy:
                    evacuate(act, name, "act", lambda j, src: act_copy(act, j, src))
                if act_more:
                    act_more(act)
                end_stage(act, "scalar")

            def dve_(dve):
                if dve_copy:
                    evacuate(dve, name, "dve", lambda j, src: dve_copy(dve, j, src))
                if dve_more:
                    dve_more(dve)
                end_stage(dve, "vector")

            def pool_(pool):
                end_stage(pool, "gpsimd")

            return pe_, act_, dve_, pool_

        P1_LOADS = [
            (gla_bT[:], d["b_gla_a"][0].rearrange("(h p) -> p h", p=P)),
            (gla_og[:], d["gla_out_norm_g"].to_broadcast([P, GD])),
            (gla_a2[:], d["w_gla_a2"][0]),
            (dil_gT[:, 0, :], d["dil_q_norm_g"][0].rearrange("g p -> p g")),
            (dil_gT[:, 1, :], d["dil_k_norm_g"][0].rearrange("g p -> p g")),
            (g2T[:], d["norm2_g"][0].rearrange("(p c) -> p c", c=KC)),
            (r1_w[:, :, 0:N_GROUPS], d["w_router_group"][0].rearrange("(p c) n -> p c n", c=KC)),
            (r1_w[:, :, N_GROUPS:36], d["w_router_expert"][0].rearrange("(p c) n -> p c n", c=KC)),
            (r1_b[:, 0:N_GROUPS], d["b_router_group"].to_broadcast([P, N_GROUPS])),
            (r1_b[:, N_GROUPS:36], d["b_router_expert"].to_broadcast([P, NE1])),
            (pos_i[:], d["positions_2"][0].rearrange("(t p) -> p t", p=P)),
            (r2_w[:], d["router_w_2"][0].rearrange("(p c) n -> p c n", c=KC)),
            (r2_b[:], d["router_b_2"].to_broadcast([P, NE2])),
        ]
        for l in range(LAYERS):
            for k, g in enumerate(("g_mix_2", "g_ffn_2", "g_ple_2")):
                P1_LOADS.append((l_gT[:, 3 * l + k, :], d[g][l].rearrange("(p c) -> p c", c=KC)))

        def layer_loads(l):
            lot = [(l_mu[:], d["rw_mu_2"][l:l + 1].to_broadcast([P, 1024]))]
            for k, n in enumerate(("rw_w0_2", "rw_a0_2", "rw_k_k_2", "rw_k_a_2", "rw_r_k_2", "rw_gn_g_2", "rw_gn_b_2",
                                   "gm_ln_g_2", "gm_ln_b_2")):
                src = d[n][l:l + 1]
                if len(src.shape) == 3:
                    src = src.rearrange("a h n -> a (h n)")
                lot.append((l_row[:, k, :], src.to_broadcast([P, 256])))
            lot += [(l_bsT[:], d["gm_bs_2"][l].rearrange("h p -> p h")),
                    (l_lora[0:64, 0, :], d["rw_w_up_2"][l]),
                    (l_lora[64:128, 0, :], d["rw_a_up_2"][l]),
                    (l_lora[:, 1, :], d["rw_g_up_2"][l]),
                    (l_ws[:], d["gm_ws_2"][l].rearrange("h t s -> t h s")),
                    (l_posT[0:64, :], d["nsa_cmp_pos_2"][l].rearrange("(i k) n -> k n i", k=2)[0]),
                    (l_posT[64:128, :], d["nsa_cmp_pos_2"][l].rearrange("(i k) n -> k n i", k=2)[1]),
                    (l_w2[:, 0, :], d["nsa_kc_w2_2"][l]),
                    (l_w2[:, 1, :], d["nsa_kc_w2_2"][l]),
                    (l_w2[:, 2, :], d["nsa_vc_w2_2"][l])]
            return lot

        N_LAYER_LOADS = len(layer_loads(0))

        def load_layer(eng, l):
            for dst, src in layer_loads(l):
                eng.dma_start(dst, src).then_inc(sig("layer_params"), 16)

        MI = Arena(arena)
        MI.at = NT * D + D
        m_row, m_col, m_xor = [MI.take(S).bitcast(I32) for _ in range(3)]
        m_rowf, m_colf, m_t, m_u = [MI.take(S) for _ in range(4)]
        m_b16 = MI.take(NCH)
        m_half = MI.take(2)
        m_cmp = MI.take(NT, 16)
        m_i16 = MI.take(64).bitcast(I32)
        m_half_i = m_i16[:, 16:18]
        m_cmp_i = m_i16[:, 18:50].rearrange("p (t n) -> p t n", t=NT)
        m_desc_i = MI.take(32).bitcast(I32)

        def setup_pool(pool):
            pool.iota(m_row, [[0, S]], base=0, channel_multiplier=1)
            pool.iota(m_col, [[1, S]], base=0, channel_multiplier=0)
            pool.iota(m_i16[:, 0:NCH], [[-GCH, NCH]], base=0, channel_multiplier=1)
            pool.iota(m_half_i, [[-RC, 2]], base=0, channel_multiplier=1)
            for t in range(NT):
                pool.iota(m_cmp_i[:, t, :], [[-CST, 16]], base=t * P - (CB - 1), channel_multiplier=1)
            pool.iota(m_desc_i, [[-1, 32]], base=32, channel_multiplier=0).then_inc(sig("iota_done"), 1)
            end_stage(pool, "gpsimd")

        def setup_act(act):
            act.wait_ge(sig("x_ready"), 32)
            end_stage(act, "scalar")

        def setup_dve(dve):
            dve.wait_ge(sig("iota_done"), 1)
            dve.tensor_copy(m_rowf, m_row)
            vstep(dve, dve.tensor_copy(m_colf, m_col))
            vstep(dve, dve.tensor_tensor(diff[:], m_colf[:, 0:P], m_rowf[:, 0:P], ALU.subtract))
            vstep(dve, dve.tensor_scalar(ident[:], diff[:], 0.0, None, ALU.is_equal))
            end_stage(dve, "vector")

        def setup_pe(pe):
            end_stage(pe, "tensor")

        def masks_dve(dve):
            dve.tensor_tensor(m_xor[:, 0:P], m_row[:, 0:P], m_col[:, 0:P], ALU.bitwise_xor)
            vstep(dve, dve.tensor_tensor(negdist[:], m_colf, m_rowf, ALU.subtract))
            vstep(dve, dve.tensor_copy(xor_f[:], m_xor[:, 0:P]))
            vstep(dve, dve.tensor_copy(m_xor, negdist[:]))
            dve.tensor_scalar(same_chunk[:], xor_f[:], float(RC), None, ALU.is_lt)
            dve.tensor_scalar(gla_mask[:], xor_f[:], float(GCH), None, ALU.is_lt)
            dve.tensor_scalar(causal_up[:], diff[:], 0.0, None, ALU.is_ge)
            dve.tensor_scalar(m_u[:, 0:P], diff[:], 0.0, None, ALU.is_lt)
            dve.tensor_scalar(m_u[:, P:S], diff[:], 0.0, None, ALU.is_gt)
            dve.tensor_scalar(shift_dn_edge[:], diff[:], float(1 - P), None, ALU.is_equal)
            dve.tensor_scalar(shift_up[:], diff[:], -1.0, None, ALU.is_equal)
            dve.tensor_scalar(shift_up_edge[:], diff[:], float(P - 1), None, ALU.is_equal)
            vstep(dve, dve.tensor_scalar(shift_dn[:], diff[:], 1.0, None, ALU.is_equal))
            dve.tensor_tensor(shift_dn[:], shift_dn[:], ident[:], ALU.subtract)
            dve.tensor_tensor(tri_inc[:], causal_up[:], same_chunk[:], ALU.mult)
            dve.tensor_tensor(tri_str[:], m_u[:, P:S], same_chunk[:], ALU.mult)
            vstep(dve, dve.tensor_tensor(gla_mask[:], gla_mask[:], causal_up[:], ALU.mult))
            for k in range(6):
                b = float(1 << k)
                dve.scalar_tensor_tensor(out=low_b[:, k, :], in0=xor_f[:], scalar=b, in1=m_u[:, 0:P],
                                         op0=ALU.is_ge, op1=ALU.mult)
                vstep(dve, dve.scalar_tensor_tensor(out=up_b[:, k, :], in0=xor_f[:], scalar=b, in1=m_u[:, P:S],
                                                    op0=ALU.is_ge, op1=ALU.mult))
                dve.scalar_tensor_tensor(out=low_b[:, k, :], in0=xor_f[:], scalar=2 * b, in1=low_b[:, k, :],
                                         op0=ALU.is_lt, op1=ALU.mult)
                vstep(dve, dve.scalar_tensor_tensor(out=up_b[:, k, :], in0=xor_f[:], scalar=2 * b, in1=up_b[:, k, :],
                                                    op0=ALU.is_lt, op1=ALU.mult))
            vstep(dve, dve.tensor_scalar(negdist[:], negdist[:], float(-P), None, ALU.add))
            vstep(dve, dve.tensor_scalar(m_t, negdist[:], 0.0, None, ALU.is_le))
            dve.tensor_scalar(causal_neg[:], m_t, BIG, -BIG, ALU.mult, ALU.add)
            vstep(dve, dve.scalar_tensor_tensor(out=dil_mask[:, 0, :], in0=negdist[:], scalar=-128.0, in1=m_t,
                                                op0=ALU.is_ge, op1=ALU.mult))
            for g, r in ((1, 4), (2, 16)):
                vstep(dve, dve.tensor_scalar(m_row, m_xor, r - 1, None, ALU.bitwise_and))
                vstep(dve, dve.tensor_copy(m_rowf, m_row))
                vstep(dve, dve.scalar_tensor_tensor(out=dil_mask[:, g, :], in0=m_rowf, scalar=0.0, in1=m_t,
                                                    op0=ALU.is_equal, op1=ALU.mult))
            dve.tensor_scalar(dil_mask[:], dil_mask[:], BIG, -BIG, ALU.mult, ALU.add)
            vstep(dve, dve.tensor_scalar(m_row, m_col, GCH - 1, None, ALU.bitwise_and))
            vstep(dve, dve.tensor_copy(m_rowf, m_row))
            dve.tensor_scalar(scan_keep[:], m_rowf, 0.0, None, ALU.not_equal)
            dve.tensor_copy(m_b16, m_i16[:, 0:NCH])
            dve.tensor_copy(m_half, m_half_i)
            vstep(dve, dve.tensor_copy(m_cmp, m_cmp_i))
            vstep(dve, dve.tensor_scalar(m_t[:, 0:NCH], m_b16, float(GCH), None, ALU.is_lt))
            dve.scalar_tensor_tensor(out=block16[:], in0=m_b16, scalar=0.0, in1=m_t[:, 0:NCH], op0=ALU.is_ge, op1=ALU.mult)
            vstep(dve, dve.tensor_scalar(m_t[:, 16:18], m_half, float(RC), None, ALU.is_lt))
            dve.scalar_tensor_tensor(out=half_ind[:], in0=m_half, scalar=0.0, in1=m_t[:, 16:18], op0=ALU.is_ge, op1=ALU.mult)
            vstep(dve, dve.tensor_scalar(cmp_ok[:], m_cmp, 0.0, None, ALU.is_ge))
            dve.tensor_scalar(cmp_neg[:], cmp_ok[:], BIG, -BIG, ALU.mult, ALU.add)
            dve.tensor_copy(desc[:], m_desc_i)
            dve.tensor_copy(slot_no[:], m_colf[:, 0:P])
            dve.memset(ones[:], 1.0)
            for k in range(ROPE_HALF):
                dve.memset(freq[:, k:k + 1], INV_FREQ[k])

        B1 = Arena(arena)
        ogT = B1.take(GW // P, S)
        oaT = B1.take(GW // P, S)
        b1_at = B1.at
        MA = Arena(arena)
        MA.at = b1_at
        g_qT, g_kT = MA.take(GH, S), MA.take(GH, S)
        g_lrT = MA.take(S)
        g_y, g_a, g_b, g_c = [MA.take(GH, S) for _ in range(4)]
        g_att = MA.take(GH * NT, P)
        g_ke = MA.take(GH * NT, P)
        g_vm = MA.take(2, NCH, GD)
        g_st = MA.take(NT, NCH, GD)
        g_dec = MA.take(GH, S // GCH)
        za = MA.take(NT, ZA)
        g_oT = g_a
        g_otok = g_b.rearrange("p h s -> p (h s)").rearrange("p (t h v) -> p t h v", t=NT, h=GH)
        g_sq = g_c.rearrange("p h s -> p (h s)").rearrange("p (t h v) -> p t h v", t=NT, h=GH)
        g_sil = g_y.rearrange("p h s -> p (h s)").rearrange("p (t h v) -> p t h v", t=NT, h=GH)
        COMBOS = [(h, t) for h in range(GH) for t in range(NT)]

        def flat(ap):
            return ap.rearrange("p a b -> p (a b)")

        def gla_pe(pe):
            for k, c0 in ((0, 0), (2, GW)):
                for h in range(GH):
                    for t in range(NT):
                        mm = pe.transpose(ps[:, k + h // 2, (h % 2) * S + t * P:(h % 2) * S + (t + 1) * P],
                                          za[:, t, c0 + h * GD:c0 + (h + 1) * GD], ident[:])
                mm.then_inc(sig("gla_turned"), 1)
            for t in range(NT):
                mm = pe.transpose(ps[0:RANK, 4, t * P:(t + 1) * P], za[:, t, 4 * GW:ZA], ident[:])
            mm.then_inc(sig("gla_turned"), 1)
            pe.wait_ge(*ended("gla_lr", 1))
            for h in range(GH):
                mm = pe.matmul(ps[:, 5 + h // 2, (h % 2) * S:(h % 2 + 1) * S], gla_a2[:, h * GD:(h + 1) * GD],
                               g_lrT[0:RANK, :], start=True, stop=True)
            mm.then_inc(sig("gla_logit"), 1)
            pe.wait_ge(*ended("gla_scaled", 1))
            for k, (h, t) in enumerate(COMBOS):
                mm = pe.matmul(ps[:, k // 4, (k % 4) * P:(k % 4 + 1) * P], g_kT[:, h, t * P:(t + 1) * P],
                               g_qT[:, h, t * P:(t + 1) * P], start=True, stop=True)
            mm.then_inc(sig("gla_scores"), 1)
            for k, (h, t) in enumerate(COMBOS):
                mm = pe.transpose(ps[:, 2 + k // 4, (k % 4) * P:(k % 4 + 1) * P], g_y[:, h, t * P:(t + 1) * P], ident[:])
            mm.then_inc(sig("gla_ke_turned"), 1)
            pe.wait_ge(*ended("gla_att", 1))
            pe.wait_ge(*ended("gla_ke", 1))

            def kv(k):
                pe.wait_ge(*ended("gla_vm", k + 1))
                if k >= 2:
                    pe.wait_ge(*ended("gla_kv_used", k - 1))
                vm = g_vm[:, k % 2].rearrange("p n v -> p (n v)")
                for b in range(2):
                    mm = pe.matmul(ps[:, 2 * (k % 2) + b, :], g_ke[:, k, :], vm[:, b * 512:(b + 1) * 512],
                                   start=True, stop=True)
                mm.then_inc(sig("gla_kv"), 1)

            kv(0)
            for k, (h, t) in enumerate(COMBOS):
                if k + 1 < len(COMBOS):
                    kv(k + 1)
                oT = ps[:, 4 + k // 4, (k % 4) * P:(k % 4 + 1) * P]
                pe.matmul(oT, za[:, t, 2 * GW + h * GD:2 * GW + (h + 1) * GD], g_att[:, k, :], start=True, stop=False)
                pe.wait_ge(*ended("gla_state", k + 1))
                for n in range(NCH):
                    if t == 0 and n == 0:
                        continue
                    mm = pe.matmul(oT[:, n * GCH:(n + 1) * GCH], g_st[:, t, n, :],
                                   g_qT[:, h, t * P + n * GCH:t * P + (n + 1) * GCH], start=False, stop=(n == NCH - 1))
                mm.then_inc(sig("gla_o"), 1)
            pe.wait_ge(*ended("gla_oT", 1))
            for k, (h, t) in enumerate(COMBOS):
                mm = pe.transpose(ps[:, 6 + t, h * GD:(h + 1) * GD], g_oT.rearrange("p h s -> p (h s)")[:, k * P:(k + 1) * P],
                                  ident[:])
            mm.then_inc(sig("gla_o_turned"), 1)
            pe.wait_ge(*ended("gla_gated", 1))
            for c in range(GW // P):
                for t in range(NT):
                    mm = pe.transpose(ps[:, c // 2, (c % 2) * S + t * P:(c % 2) * S + (t + 1) * P],
                                      g_otok[:, t].rearrange("p h v -> p (h v)")[:, c::GW // P], ident[:])
            mm.then_inc(sig("gla_out"), 1)
            end_stage(pe, "tensor")

        def gla_act(act):
            act.wait_ge(*ended("gla_turned", 1))
            act.mul(flat(g_qT), ps[:, 0:2, :].rearrange("p a b -> p (a b)"), float(GD) ** -0.5)
            act.wait_ge(*ended("gla_turned", 3))
            act.copy(g_lrT[0:RANK, :], ps[0:RANK, 4, 0:S]).then_inc(sig("gla_lr"), 1)
            act.wait_ge(*ended("gla_y", 1))
            astep(act, act.activation(flat(g_a), flat(g_y), ACT.Abs))
            astep(act, act.activation(flat(g_a), flat(g_a), ACT.Exp, scale=-1.0))
            act.activation(flat(g_a), flat(g_a), ACT.Ln, bias=1.0).then_inc(sig("gla_ln"), 1)
            act.wait_ge(*ended("gla_cum", 1))
            act.activation(flat(g_b), flat(g_a), ACT.Exp, scale=1.0 / TAU).then_inc(sig("gla_exp"), 1)
            act.activation(flat(g_c), flat(g_a), ACT.Exp, scale=-1.0 / TAU).then_inc(sig("gla_exp"), 1)
            act.wait_ge(*ended("gla_cum", 2))
            act.activation(flat(g_y), flat(g_y), ACT.Exp, scale=1.0 / TAU).then_inc(sig("gla_exp"), 1)
            act.wait_ge(*ended("gla_ke_turned", 1))
            act.copy(flat(g_ke), ps[:, 2:4, :].rearrange("p a b -> p (a b)")).then_inc(sig("gla_ke"), 1)
            act.wait_ge(*ended("gla_o", len(COMBOS)))
            act.copy(flat(g_oT), ps[:, 4:6, :].rearrange("p a b -> p (a b)")).then_inc(sig("gla_oT"), 1)
            act.activation(g_sil.rearrange("p t h v -> p t (h v)"), za[:, :, 3 * GW:4 * GW], ACT.Silu).then_inc(sig("gla_silu"), 1)
            act.wait_ge(*ended("gla_o_turned", 1))
            act.copy(g_otok.rearrange("p t h v -> p (t h v)"), ps[:, 6:8, :].rearrange("p a b -> p (a b)"))
            act.activation(g_sq.rearrange("p t h v -> p (t h v)"), ps[:, 6:8, :].rearrange("p a b -> p (a b)"),
                           ACT.Square).then_inc(sig("gla_sq"), 1)
            act.wait_ge(*ended("gla_ms", 1))
            act.activation(small[:, 16:24], small[:, 8:16], ACT.Sqrt).then_inc(sig("gla_rt"), 1)
            act.wait_ge(*ended("gla_out", 1))
            act.copy(flat(ogT), ps[:, 0:2, :].rearrange("p a b -> p (a b)"))
            end_stage(act, "scalar")

        def gla_dve(dve):
            dve.wait_ge(*ended("gla_turned", 2))
            dve.tensor_copy(flat(g_kT), ps[:, 2:4, :].rearrange("p a b -> p (a b)"))
            dve.wait_ge(*ended("gla_logit", 1))
            for h in range(GH):
                ins = dve.tensor_scalar(g_y[:, h, :], ps[:, 5 + h // 2, (h % 2) * S:(h % 2 + 1) * S], gla_bT[:, h:h + 1],
                                        None, ALU.add)
            ins.then_inc(sig("gla_y"), 1)
            dve.wait_ge(*ended("gla_ln", 1))
            vstep(dve, dve.scalar_tensor_tensor(out=flat(g_y), in0=flat(g_y), scalar=0.0, in1=flat(g_a), op0=ALU.min,
                                                op1=ALU.subtract))
            for h in range(GH):
                ins = dve.tensor_tensor_scan(g_a[:, h, :], scan_keep[:], g_y[:, h, :], 0.0, ALU.mult, ALU.add)
            ins.then_inc(sig("gla_cum"), 1)
            dve.wait_ge(*ended("gla_cum", 1))
            a4 = g_a.rearrange("p h (n i) -> p (h n) i", i=GCH)
            y4 = g_y.rearrange("p h (n i) -> p (h n) i", i=GCH)
            dve.tensor_tensor(y4, a4[:, :, GCH - 1:GCH].to_broadcast([P, GH * S // GCH, GCH]), a4,
                              ALU.subtract).then_inc(sig("gla_cum"), 1)
            dve.wait_ge(*ended("gla_exp", 3))
            b4 = g_b.rearrange("p h (n i) -> p h n i", i=GCH)
            dve.tensor_copy(g_dec, b4[:, :, :, GCH - 1])
            dve.tensor_tensor(flat(g_qT), flat(g_qT), flat(g_b), ALU.mult)
            vstep(dve, dve.tensor_tensor(flat(g_y), flat(g_y), flat(g_kT), ALU.mult))
            dve.tensor_tensor(flat(g_kT), flat(g_kT), flat(g_c), ALU.mult).then_inc(sig("gla_scaled"), 1)
            dve.wait_ge(*ended("gla_scores", 1))
            dve.tensor_tensor(g_att, ps[:, 0:2, :].rearrange("p a (b n) -> p (a b) n", n=P),
                              gla_mask[:].unsqueeze(1).to_broadcast([P, GH * NT, P]), ALU.mult).then_inc(sig("gla_att"), 1)
            for k, (h, t) in enumerate(COMBOS):
                dve.wait_ge(*ended("gla_kv", k + 1))
                if k >= 2:
                    dve.wait_ge(*ended("gla_o", k - 1))
                for n in range(NCH):
                    add = ps[:, 2 * (k % 2) + n // 4, (n % 4) * GD:(n % 4 + 1) * GD]
                    last = n == NCH - 1
                    if last and t == NT - 1:
                        dve.drain().then_inc(sig("gla_state"), 1)
                        continue
                    dst = g_st[:, t + 1, 0, :] if last else g_st[:, t, n + 1, :]
                    if last:
                        if k >= 1:
                            dve.wait_ge(*ended("gla_o", k))
                        dve.drain().then_inc(sig("gla_state"), 1)
                    if t == 0 and n == 0:
                        ins = dve.tensor_copy(dst, add)
                    else:
                        ins = dve.scalar_tensor_tensor(out=dst, in0=g_st[:, t, n, :],
                                                       scalar=g_dec[:, h, t * NCH + n:t * NCH + n + 1],
                                                       in1=add, op0=ALU.mult, op1=ALU.add)
                    vstep(dve, ins)
                dve.drain().then_inc(sig("gla_kv_used"), 1)
            dve.wait_ge(*ended("gla_sq", 1))
            vstep(dve, dve.tensor_reduce(small[:, 0:8], g_sq.rearrange("p t h v -> p (t h) v"), AX, ALU.add))
            dve.tensor_scalar(small[:, 8:16], small[:, 0:8], 1.0 / GD, EPS, ALU.mult, ALU.add).then_inc(sig("gla_ms"), 1)
            dve.wait_ge(*ended("gla_rt", 1))
            vstep(dve, dve.reciprocal(small[:, 24:32], small[:, 16:24]))
            o8 = g_otok.rearrange("p t h v -> p (t h) v")
            vstep(dve, dve.tensor_tensor(o8, o8, small[:, 24:32].unsqueeze(2).to_broadcast([P, NT * GH, GD]), ALU.mult))
            vstep(dve, dve.tensor_tensor(o8, o8, gla_og[:].unsqueeze(1).to_broadcast([P, NT * GH, GD]), ALU.mult))
            dve.wait_ge(*ended("gla_silu", 1))
            dve.tensor_tensor(o8, o8, g_sil.rearrange("p t h v -> p (t h) v"), ALU.mult).then_inc(sig("gla_gated"), 1)
            end_stage(dve, "vector")

        def gla_pool(pool):
            for k, (h, t) in enumerate(COMBOS):
                if k >= 2:
                    pool.wait_ge(*ended("gla_kv", k - 1))
                v = za[:, t, 2 * GW + h * GD:2 * GW + (h + 1) * GD]
                pool.tensor_tensor(g_vm[:, k % 2], v.unsqueeze(1).to_broadcast([P, NCH, GD]),
                                   block16[:].unsqueeze(2).to_broadcast([P, NCH, GD]), ALU.mult).then_inc(sig("gla_vm"), 1)
            end_stage(pool, "gpsimd")

        MB = Arena(arena)
        MB.at = b1_at
        zb = MB.take(NT, ZB)
        zb5 = zb.rearrange("p t (g k h e) -> p t g k h e", g=DG, k=3, h=DH)
        t_sq = MB.take(2 * DH, DD)
        t_qk = MB.take(DG, 2, S)
        t_s0 = MB.take(DG, P)
        t_s1 = MB.take(DG, S)
        t_pT = MB.take(9, P)
        t_o = MB.take(NT, GW)
        t_ss = MB.take(NT, DG, 2 * DH)
        t_rs = MB.take(NT, DG, 2 * DH)
        t_mx = MB.take(NT * DG)
        t_nm = MB.take(NT)
        t_den = MB.take(NT)
        t_rd = MB.take(NT)

        def qk_psum(g, k):
            return ps[:, ((0, 1), (2, 7))[k][g // 2], (g % 2) * S:(g % 2 + 1) * S]

        def dil_pe(pe):
            pe.wait_ge(sig("dil_normed"), 1)
            for h in range(DH):
                if h >= 1:
                    pe.wait_ge(sig("dil_pT"), h)
                for g in range(DG):
                    for k in range(2):
                        for t in range(NT):
                            mm = pe.transpose(qk_psum(g, k)[:, t * P:(t + 1) * P], zb5[:, t, g, k, h, :], ident[:])
                mm.then_inc(sig("dil_turned"), 1)
                pe.wait_ge(sig("dil_qT"), h + 1)
                pe.wait_ge(sig("dil_kT"), h + 1)
                if h >= 1:
                    pe.wait_ge(sig("dil_max"), h)
                for g in range(DG):
                    pe.matmul(ps[:, 3, g * P:(g + 1) * P], t_qk[:, g, 0, 0:P], t_qk[:, g, 1, 0:P], start=True, stop=True)
                for g in range(DG):
                    mm = pe.matmul(ps[:, 4 + g // 2, (g % 2) * S:(g % 2 + 1) * S], t_qk[:, g, 0, P:S], t_qk[:, g, 1, :],
                                   start=True, stop=True)
                mm.then_inc(sig("dil_scores"), 1)
                pe.wait_ge(sig("dil_probs"), h + 1)
                for g in range(DG):
                    pe.transpose(ps[:, 0, g * P:(g + 1) * P], t_s0[:, g, :], ident[:])
                for g in range(DG):
                    for b in range(2):
                        q = 2 * g + b
                        mm = pe.transpose(ps[:, 1 + q // 4, (q % 4) * P:(q % 4 + 1) * P], t_s1[:, g, b * P:(b + 1) * P], ident[:])
                mm.then_inc(sig("dil_pturned"), 1)
                pe.wait_ge(sig("dil_pT"), h + 1)
                if h >= 1:
                    pe.wait_ge(sig("dil_o"), h)
                for g in range(DG):
                    pe.matmul(ps[:, 6, 0:DD], t_pT[:, g, :], zb5[:, 0, g, 2, h, :], start=(g == 0), stop=(g == DG - 1))
                for g in range(DG):
                    for b in range(2):
                        mm = pe.matmul(ps[:, 6, DD:2 * DD], t_pT[:, 3 + 2 * g + b, :], zb5[:, b, g, 2, h, :],
                                       start=(g == 0 and b == 0), stop=(g == DG - 1 and b == 1))
                mm.then_inc(sig("dil_pv"), 1)
            pe.wait_ge(sig("dil_o"), DH)
            for c in range(GW // P):
                for t in range(NT):
                    mm = pe.transpose(ps[:, c // 2, (c % 2) * S + t * P:(c % 2) * S + (t + 1) * P],
                                      t_o[:, t, c::GW // P], ident[:])
            mm.then_inc(sig("dil_out"), 1)
            end_stage(pe, "tensor")

        def dil_act(act):
            act.wait_ge(sig("dil_ms"), 1)
            act.activation(t_rs.rearrange("p t g k -> p (t g k)"), t_ss.rearrange("p t g k -> p (t g k)"),
                           ACT.Sqrt).then_inc(sig("dil_rt"), 1)
            for h in range(DH):
                act.wait_ge(sig("dil_turned"), h + 1)
                if h >= 1:
                    act.wait_ge(sig("dil_scores"), h)
                for g in range(DG):
                    ins = act.activation(t_qk[:, g, 0, :], qk_psum(g, 0), ACT.Identity, scale=dil_gT[:, 0, g:g + 1])
                ins.then_inc(sig("dil_qT"), 1)
                act.wait_ge(sig("dil_max"), h + 1)
                act.activation(t_s0, t_s0, ACT.Exp, bias=t_nm[:, 0:1], accum_out=t_den[:, 0:1])
                act.activation(t_s1, t_s1, ACT.Exp, bias=t_nm[:, 1:2], accum_out=t_den[:, 1:2]).then_inc(sig("dil_probs"), 1)
                act.wait_ge(sig("dil_pturned"), h + 1)
                act.copy(t_pT[:, 0:3, :], ps[:, 0, 0:3 * P].rearrange("p (g n) -> p g n", n=P))
                act.copy(t_pT[:, 3:9, :].rearrange("p g n -> p (g n)"),
                         ps[:, 1:3, :].rearrange("p a b -> p (a b)")[:, 0:6 * P]).then_inc(sig("dil_pT"), 1)
            act.wait_ge(sig("dil_out"), 1)
            act.copy(flat(oaT), ps[:, 0:2, :].rearrange("p a b -> p (a b)"))
            end_stage(act, "scalar")

        def dil_dve(dve):
            for t in range(NT):
                for g in range(DG):
                    qk = zb5[:, t, g, 0:2].rearrange("p k h e -> p (k h) e")
                    vstep(dve, dve.tensor_tensor(t_sq, qk, qk, ALU.mult))
                    vstep(dve, dve.tensor_reduce(t_ss[:, t, g, :], t_sq, AX, ALU.add))
            ss, rs = [a.rearrange("p t g k -> p (t g k)") for a in (t_ss, t_rs)]
            dve.tensor_scalar(ss, ss, 1.0 / DD, EPS, ALU.mult, ALU.add).then_inc(sig("dil_ms"), 1)
            dve.wait_ge(sig("dil_rt"), 1)
            vstep(dve, dve.reciprocal(ss, rs))
            dve.tensor_scalar(dil_gT[:, 0, :], dil_gT[:, 0, :], float(DD) ** -0.5, None, ALU.mult)
            for t in range(NT):
                for g in range(DG):
                    qk = zb5[:, t, g, 0:2].rearrange("p k h e -> p (k h) e")
                    ins = dve.tensor_tensor(qk, qk, t_ss[:, t, g, :].unsqueeze(2).to_broadcast([P, 2 * DH, DD]), ALU.mult)
            ins.then_inc(sig("dil_normed"), 1)
            for h in range(DH):
                dve.wait_ge(sig("dil_turned"), h + 1)
                if h >= 1:
                    dve.wait_ge(sig("dil_scores"), h)
                for g in range(DG):
                    ins = dve.tensor_scalar(t_qk[:, g, 1, :], qk_psum(g, 1), dil_gT[:, 1, g:g + 1], None, ALU.mult)
                ins.then_inc(sig("dil_kT"), 1)
                dve.wait_ge(sig("dil_scores"), h + 1)
                if h >= 1:
                    dve.wait_ge(sig("dil_pturned"), h)
                for g in range(DG):
                    sl = SLOPES[g * DH + h]
                    dve.scalar_tensor_tensor(out=t_s0[:, g, :], in0=negdist[:, P:S], scalar=sl,
                                             in1=ps[:, 3, g * P:(g + 1) * P], op0=ALU.mult, op1=ALU.add)
                    ins = dve.scalar_tensor_tensor(out=t_s1[:, g, :], in0=negdist[:], scalar=sl,
                                                   in1=ps[:, 4 + g // 2, (g % 2) * S:(g % 2 + 1) * S], op0=ALU.mult, op1=ALU.add)
                vstep(dve, ins)
                dve.tensor_tensor(t_s0, t_s0, dil_mask[:, :, P:S], ALU.add)
                vstep(dve, dve.tensor_tensor(t_s1, t_s1, dil_mask[:], ALU.add))
                dve.tensor_reduce(t_mx[:, 0:1], t_s0.rearrange("p g n -> p (g n)"), AX, ALU.max)
                vstep(dve, dve.tensor_reduce(t_mx[:, 1:2], t_s1.rearrange("p g n -> p (g n)"), AX, ALU.max))
                if h >= 1:
                    dve.wait_ge(sig("dil_probs"), h)
                dve.tensor_scalar(t_nm, t_mx[:, 0:2], -1.0, None, ALU.mult).then_inc(sig("dil_max"), 1)
                dve.wait_ge(sig("dil_probs"), h + 1)
                vstep(dve, dve.reciprocal(t_rd, t_den))
                dve.wait_ge(sig("dil_pv"), h + 1)
                for t in range(NT):
                    ins = dve.tensor_scalar(t_o[:, t, h * DD:(h + 1) * DD], ps[:, 6, t * DD:(t + 1) * DD], t_rd[:, t:t + 1],
                                            None, ALU.mult)
                ins.then_inc(sig("dil_o"), 1)
            end_stage(dve, "vector")

        def idle_pool(pool):
            end_stage(pool, "gpsimd")

        MC = Arena(arena)
        MC.at = b1_at
        c_bias = MC.take(2 * D)
        c_gate = MC.take(NT, 2 * D)
        c_y = MC.take(NT, D)
        c_t = MC.take(NT, D)

        def gates_copy(dve, j, src):
            return dve.tensor_tensor(c_gate[:, j.tile, j.col:j.col + j.n], src, c_bias[:, j.col:j.col + j.n], ALU.add)

        def y_gla_copy(dve, j, src):
            return dve.tensor_tensor(c_y[:, j.tile, j.col:j.col + j.n], src, c_gate[:, j.tile, j.col:j.col + j.n], ALU.mult)

        def y_att_copy(dve, j, src):
            return dve.tensor_tensor(c_t[:, j.tile, j.col:j.col + j.n], src,
                                     c_gate[:, j.tile, D + j.col:D + j.col + j.n], ALU.mult)

        def residual_copy(dve, j, src):
            cols = x[:, j.tile, j.col:j.col + j.n]
            return dve.tensor_tensor(cols, cols, src, ALU.add)

        MR = Arena(arena)
        MR_AT, MR_SIZE = NT * D + 3600, 320
        MR.at = MR_AT
        r_log = MR.take(NT, 36)
        r_gs, r_oh1, r_oh2, r_em = MR.take(N_GROUPS), MR.take(32), MR.take(32), MR.take(32)
        r_c = MR.take(16)
        r_hit = MR.take(NT, NE2)
        r_place = MR.take(NT, NE2)
        r_count = MR.take(NE2)
        assert MR.at <= MR_AT + MR_SIZE

        def router_pe(pe, w, n, f):
            for t in range(NT):
                for c in range(KC):
                    mm = pe.matmul(ps[:, 4 + t, 0:n], hT[:, c, t * P:(t + 1) * P], w[:, c, :], start=(c == 0), stop=(c == KC - 1))
            mm.then_inc(sig("router_logits"), 1)
            pe.wait_ge(sig("routed"), f.number)
            nb = f.buckets
            for t in range(NT):
                pe.matmul(ps[:, 6, t * nb:(t + 1) * nb], causal_up[:], r_hit[:, t, 0:nb], start=True, stop=(t == 0))
                if t:
                    pe.matmul(ps[:, 6, t * nb:(t + 1) * nb], ones[:], r_hit[:, t - 1, 0:nb], start=False, stop=True)
            for t in range(NT):
                mm = pe.matmul(ps[:, 6, NT * nb:(NT + 1) * nb], ones[:], r_hit[:, t, 0:nb], start=(t == 0), stop=(t == NT - 1))
            mm.then_inc(sig("placed"), 1)
            end_stage(pe, "tensor")

        def place_dve(dve, f):
            nb = f.buckets
            dve.drain().then_inc(sig("routed"), 1)
            dve.wait_ge(sig("placed"), f.number)
            upto = ps[:, 6, 0:NT * nb].rearrange("p (t n) -> p t n", t=NT)
            vstep(dve, dve.tensor_tensor(r_place[:, :, 0:nb], upto, r_hit[:, :, 0:nb], ALU.mult))
            dve.tensor_scalar(r_place[:, :, 0:nb], r_place[:, :, 0:nb], -1.0, None, ALU.add)
            vstep(dve, dve.tensor_reduce(r_count[:, 0:1], ps[:, 6, NT * nb:(NT + 1) * nb], AX, ALU.max))
            c = 0 if f.name == "moe1" else 1
            dve.tensor_copy(most[:, c:c + 1], r_count[:, 0:1]).then_inc(sig("counted"), 1)

        def first_max(dve, v, n, mx, tie, hot):
            vstep(dve, dve.tensor_reduce(mx, v, AX, ALU.max))
            vstep(dve, dve.tensor_scalar(hot, v, mx, None, ALU.is_equal))
            vstep(dve, dve.tensor_tensor(hot, hot, desc[:, 32 - n:32], ALU.mult))
            vstep(dve, dve.tensor_reduce(tie, hot, AX, ALU.max))
            vstep(dve, dve.tensor_scalar(hot, hot, tie, None, ALU.is_equal))

        def top_two(dve, v, n, gate, scale, turn):
            first_max(dve, v, n, r_c[:, 0:1], r_c[:, 1:2], r_oh1[:, 0:n])
            vstep(dve, dve.scalar_tensor_tensor(out=v, in0=r_oh1[:, 0:n], scalar=-4 * BIG, in1=v, op0=ALU.mult, op1=ALU.add))
            first_max(dve, v, n, r_c[:, 2:3], r_c[:, 3:4], r_oh2[:, 0:n])
            dve.tensor_tensor(r_c[:, 4:5], r_c[:, 2:3], r_c[:, 0:1], ALU.subtract).then_inc(sig("router_gap"), 1)
            dve.wait_ge(sig("router_exp"), turn)
            vstep(dve, dve.tensor_scalar(r_c[:, 6:7], r_c[:, 5:6], 1.0, None, ALU.add))
            vstep(dve, dve.reciprocal(r_c[:, 7:8], r_c[:, 6:7]))
            if scale is not None:
                vstep(dve, dve.tensor_tensor(r_c[:, 7:8], r_c[:, 7:8], scale, ALU.mult))
            vstep(dve, dve.tensor_tensor(r_c[:, 8:9], r_c[:, 7:8], r_c[:, 5:6], ALU.mult))
            vstep(dve, dve.tensor_scalar(gate, r_oh1[:, 0:n], r_c[:, 7:8], None, ALU.mult))
            vstep(dve, dve.scalar_tensor_tensor(out=gate, in0=r_oh2[:, 0:n], scalar=r_c[:, 8:9], in1=gate, op0=ALU.mult, op1=ALU.add))

        def router1_act(act):
            for t in range(NT):
                act.wait_ge(sig("router_group"), t + 1)
                act.activation(r_gs, r_log[:, t, 0:N_GROUPS], ACT.Exp, bias=r_c[:, 9:10], accum_out=r_c[:, 10:11])\
                    .then_inc(sig("router_gexp"), 1)
                act.wait_ge(sig("router_gap"), t + 1)
                act.activation(r_c[:, 5:6], r_c[:, 4:5], ACT.Exp).then_inc(sig("router_exp"), 1)
            end_stage(act, "scalar")

        def router1_dve(dve):
            dve.wait_ge(sig("router_logits"), 1)
            for t in range(NT):
                lg = r_log[:, t]
                vstep(dve, dve.tensor_tensor(lg, ps[:, 4 + t, 0:36], r1_b[:], ALU.add))
                hot = r_oh2[:, 0:N_GROUPS]
                first_max(dve, lg[:, 0:N_GROUPS], N_GROUPS, r_c[:, 11:12], r_c[:, 12:13], hot)
                dve.tensor_copy(r_hit[:, t, 0:N_GROUPS], hot)
                dve.tensor_scalar(r_c[:, 9:10], r_c[:, 11:12], -1.0, None, ALU.mult).then_inc(sig("router_group"), 1)
                e8 = lg[:, N_GROUPS:36].rearrange("p (g k) -> p g k", g=N_GROUPS)
                m8 = r_em.rearrange("p (g k) -> p g k", g=N_GROUPS)
                vstep(dve, dve.tensor_tensor(m8, e8, hot.unsqueeze(2).to_broadcast([P, N_GROUPS, PER_GROUP]), ALU.mult))
                vstep(dve, dve.tensor_scalar(hot, hot, BIG, -BIG, ALU.mult, ALU.add))
                vstep(dve, dve.tensor_tensor(m8, m8, hot.unsqueeze(2).to_broadcast([P, N_GROUPS, PER_GROUP]), ALU.add))
                dve.wait_ge(sig("router_gexp"), t + 1)
                vstep(dve, dve.reciprocal(r_c[:, 13:14], r_c[:, 10:11]))
                top_two(dve, r_em, NE1, gate_w[:, t, :], r_c[:, 13:14], t + 1)
            place_dve(dve, moe1)
            end_stage(dve, "vector")

        def router2_act(act):
            for t in range(NT):
                act.wait_ge(sig("router_gap"), NT + t + 1)
                act.activation(r_c[:, 5:6], r_c[:, 4:5], ACT.Exp).then_inc(sig("router_exp"), 1)
            end_stage(act, "scalar")

        def router2_dve(dve):
            dve.wait_ge(sig("router_logits"), 2)
            for t in range(NT):
                vstep(dve, dve.tensor_tensor(r_log[:, t, 0:NE2], ps[:, 4 + t, 0:NE2], r2_b[:], ALU.add))
                top_two(dve, r_log[:, t, 0:NE2], NE2, gate_w[:, t, 0:NE2], None, NT + t + 1)
                vstep(dve, dve.tensor_tensor(r_hit[:, t, :], r_oh1[:, 0:NE2], r_oh2[:, 0:NE2], ALU.add))
            place_dve(dve, moe2)
            end_stage(dve, "vector")

        MF = Arena(arena)
        MF.at = NT * D
        f_sg, f_hid = MF.take(2, FB), MF.take(2, FB)
        MF.take(2, NT, FB // P, P)
        e_y = MF.take(D)
        e_sel = MF.take(NT, P)
        e_selT = MF.take(S)
        e_gate = MF.take(PER_GROUP)
        assert MF.at <= MR_AT
        MX = Arena(arena_parts)
        MX.at = NT * D + 2 * 2 * FB
        x_hidT, x_hidT_lo = [MX.take(2, FB // P, P) for _ in range(2)]
        MX.at = MR_AT + MR_SIZE
        w_hi = [MX.take(KC, 2 * FB) for _ in range(2)]
        d_hi = [MX.take(FB // P, D) for _ in range(2)]
        e_hT, e_hT_lo = [hT_parts[:].rearrange("p c s -> p (c s)")[:, k * KC * P:(k + 1) * KC * P]
                         .rearrange("p (c n) -> p c n", c=KC) for k in range(2)]

        h_hi = arena_parts[:, 0:KC * S].rearrange("p (c s) -> p c s", c=KC)

        def f32(ap):
            return ap.bitcast(F32)

        def ffn_turn(pe, hid, dst):
            for c in range(FB // P):
                mm = pe.transpose(dst[:, c * P:(c + 1) * P], hid[:, c::FB // P], ident[:])
            return mm

        def ring_gu(f, k, tensor=ring):
            return tensor[:, f.slots[k], 0:GU].rearrange("p (c n) -> p c n", c=KC)

        def ring_down(f, k, tensor=ring):
            return tensor[:, f.slots[k], GU:SLOT].rearrange("p (c n) -> p c n", c=FB // P)

        def matmul3(pe, dst, a_hi, a_lo, b_hi, b_lo, first, last):
            pe.matmul(dst, a_hi, b_hi, start=first, stop=False, skip_group_check=True)
            pe.matmul(dst, a_hi, b_lo, start=False, stop=False, skip_group_check=True)
            return pe.matmul(dst, a_lo, b_hi, start=False, stop=last, skip_group_check=True)

        def dense_gu_pieces(k, j):
            return 6 * k + 2 + j

        def dense_down_pieces(k, c):
            return 6 * k + 6 + c

        def dense_pe(pe, f):
            for t in range(NT):
                for b in range(2):
                    pe.matmul(ps[:, 2 * t + b, :], ident[:], x[:, t, b * 512:(b + 1) * 512], start=True, stop=False,
                              skip_group_check=True)

            def turn(k, t):
                pe.wait_ge(sig("ffn_hid"), NT * k + t + 1)
                ffn_turn(pe, f_hid[:, t, :], ps[:, 6 + t, :]).then_inc(sig("ffn_turned"), 1)

            def down(k, t):
                pe.wait_ge(sig("ffn_hidT"), NT * k + t + 1)
                for c in range(FB // P):
                    pe.wait_ge(sig("ffn_split"), dense_down_pieces(k, c))
                    for b in range(2):
                        cols = slice(b * 512, (b + 1) * 512)
                        mm = matmul3(pe, ps[:, 2 * t + b, :], x_hidT[:, t, c, :], x_hidT_lo[:, t, c, :],
                                     d_hi[k % 2][:, c, cols], ring_down(f, k, ring_parts)[:, c, cols],
                                     False, k == f.steps - 1 and c == FB // P - 1)
                if t == NT - 1:
                    mm.then_inc(ffn_used, 1)

            held = None
            for k in range(f.steps):
                for t in range(NT):
                    tok = slice(t * P, (t + 1) * P)
                    for c in range(KC):
                        if c == 2 and held:
                            turn(*held)
                        if c % 2 == 0:
                            pe.wait_ge(sig("ffn_split"), dense_gu_pieces(k, c // 2))
                        mm = matmul3(pe, ps[:, 4 + t, :], h_hi[:, c, tok], hT_parts[:, c, tok], w_hi[k % 2][:, c, :],
                                     ring_gu(f, k, ring_parts)[:, c, :], c == 0, c == KC - 1)
                    mm.then_inc(sig("ffn_gu"), 1)
                    if held:
                        down(*held)
                    held = (k, t)
            turn(*held)
            down(*held)
            pe.drain().then_inc(sig("ffn_end"), 1)
            end_stage(pe, "tensor")

        def dense_act(act, f):
            def upper_gu(k, pieces):
                act.wait_ge(slot_ready[f.slots[k]], f.ready0[f.slots[k]] + 48 * (k // SLOTS + 1))
                for j in pieces:
                    c = slice(2 * j, 2 * j + 2)
                    act.copy(w_hi[k % 2][:, c, :], ring_gu(f, k)[:, c, :]).then_inc(sig("ffn_upper"), 1)

            def hidden(k, t):
                act.wait_ge(sig("ffn_turned"), NT * k + t + 1)
                act.copy(x_hidT[:, t].rearrange("p c n -> p (c n)"), ps[:, 6 + t, 0:FB]).then_inc(sig("ffn_hidT_upper"), 1)

            act.copy(h_hi, hT[:]).then_inc(sig("ffn_upper"), 1)
            upper_gu(0, [0, 1, 2, 3])
            held = None
            for k in range(f.steps):
                for t in range(NT):
                    if t == 0:
                        for c in range(FB // P):
                            act.copy(d_hi[k % 2][:, c, :], ring_down(f, k)[:, c, :]).then_inc(sig("ffn_upper"), 1)
                    if held:
                        hidden(*held)
                    held = (k, t)
                    if k + 1 < f.steps:
                        upper_gu(k + 1, [2 * t, 2 * t + 1])
                    act.wait_ge(sig("ffn_gu"), NT * k + t + 1)
                    act.activation(f_sg[:, t, :], ps[:, 4 + t, 0:FB], ACT.Silu).then_inc(sig("ffn_silu"), 1)
            hidden(*held)
            act.wait_ge(sig("ffn_end"), 1)
            act.copy(x[:, 0, :], ps[:, 0:2, :].rearrange("p a b -> p (a b)"))
            end_stage(act, "scalar")

        def dense_dve(dve, f):
            def lower_gu(k, pieces):
                for j in pieces:
                    c = slice(2 * j, 2 * j + 2)
                    dve.wait_ge(sig("ffn_upper"), dense_gu_pieces(k, j))
                    dve.tensor_tensor(ring_gu(f, k, ring_parts)[:, c, :], ring_gu(f, k)[:, c, :], f32(w_hi[k % 2][:, c, :]),
                                      ALU.subtract).then_inc(sig("ffn_split"), 1)

            def hidden(k, t):
                dve.wait_ge(sig("ffn_hidT_upper"), NT * k + t + 1)
                flat_hi, flat_lo = [a[:, t].rearrange("p c n -> p (c n)") for a in (x_hidT, x_hidT_lo)]
                dve.tensor_tensor(flat_lo, ps[:, 6 + t, 0:FB], f32(flat_hi), ALU.subtract).then_inc(sig("ffn_hidT"), 1)

            dve.wait_ge(sig("ffn_upper"), 1)
            dve.tensor_tensor(hT_parts[:], hT[:], f32(h_hi), ALU.subtract).then_inc(sig("ffn_split"), 1)
            lower_gu(0, [0, 1, 2, 3])
            held = None
            for k in range(f.steps):
                for t in range(NT):
                    if t == 0:
                        for c in range(FB // P):
                            dve.wait_ge(sig("ffn_upper"), dense_down_pieces(k, c))
                            dve.tensor_tensor(ring_down(f, k, ring_parts)[:, c, :], ring_down(f, k)[:, c, :],
                                              f32(d_hi[k % 2][:, c, :]), ALU.subtract).then_inc(sig("ffn_split"), 1)
                    if held:
                        hidden(*held)
                    held = (k, t)
                    if k + 1 < f.steps:
                        lower_gu(k + 1, [2 * t, 2 * t + 1])
                    dve.wait_ge(sig("ffn_silu"), NT * k + t + 1)
                    dve.tensor_tensor(f_hid[:, t, :], ps[:, 4 + t, FB:2 * FB], f_sg[:, t, :], ALU.mult)\
                        .then_inc(sig("ffn_hid"), 1)
            hidden(*held)
            dve.wait_ge(sig("ffn_end"), 1)
            dve.tensor_copy(x[:, 1, :], ps[:, 2:4, :].rearrange("p a b -> p (a b)"))
            end_stage(dve, "vector")

        def stage_dense(f):
            return (lambda pe: dense_pe(pe, f)), (lambda act: dense_act(act, f)), (lambda dve: dense_dve(dve, f)), idle_pool

        ADD_BANKS = (2, 3, 4, 7)
        assert 2 * P == S

        def gu_pieces(f, g, k, j):
            before = 6 * (k - 1) + 4 if k else 0
            return 6 * f.steps * g + before + j + 1

        def down_pieces(f, g, k, j):
            before = 6 * k + (8 if k + 1 < f.steps else 4)
            return 6 * f.steps * g + before + j + 1

        def moe_gather(pe, f, m, g):
            pe.wait_ge(*m.at("sel", g + 1))
            for c in range(KC):
                for t in range(NT):
                    mm = pe.matmul(ps[:, 5 + c // 4, (c % 4) * P:(c % 4 + 1) * P], nt_xn[:, t, c::KC], e_sel[:, t, :],
                                   start=(t == 0), stop=(t == NT - 1))
            mm.then_inc(m("gathered"), 1)

        def moe_places(pe, f, m, g):
            pe.wait_ge(*m.at("rows", g + 1))
            for t in range(NT):
                pe.transpose(ps[:, 5, t * P:(t + 1) * P], e_sel[:, t, :], ident[:])
            for t in range(NT):
                cols = slice(g * f.e, (g + 1) * f.e) if isinstance(g, int) else bass.ds(g * f.e, f.e)
                mm = pe.matmul(ps[:, 5, S:S + f.e], e_sel[:, t, :], gate_w[:, t, cols], start=(t == 0), stop=(t == NT - 1))
            mm.then_inc(m("sel_turned"), 1)

        def moe_pe_bucket(pe, f, m, g, last):
            def turn(k):
                pe.wait_ge(*m.at("hid", g * f.steps + k + 1))
                if k == 0:
                    pe.wait_ge(*m.at("added", 4 * g + 3))
                ffn_turn(pe, f_hid[:, k % 2, :], ps[:, 4, :]).then_inc(m("turned"), 1)

            def down(k):
                pe.wait_ge(*m.at("hidT", g * f.steps + k + 1))
                for c in range(FB // P):
                    pe.wait_ge(*m.at("split", down_pieces(f, g, k, c)))
                    for b in range(2):
                        cols = slice(b * 512, (b + 1) * 512)
                        mm = matmul3(pe, ps[:, b, :], x_hidT[:, k % 2, c, :], x_hidT_lo[:, k % 2, c, :],
                                     d_hi[k % 2][:, c, cols], ring_down(f, k, ring_parts)[:, c, cols],
                                     k == 0 and c == 0, k == f.steps - 1 and c == FB // P - 1)
                mm.then_inc(m("used"), 1)

            for k in range(f.steps):
                if k == 0:
                    pe.wait_ge(*m.at("rows", g + 1))
                if k < 2:
                    pe.wait_ge(*m.at("added", 4 * g + k + 1))
                for c in range(KC):
                    if c == 2 and k:
                        turn(k - 1)
                    if c % 2 == 0:
                        pe.wait_ge(*m.at("split", gu_pieces(f, g, k, c // 2)))
                    mm = matmul3(pe, ps[:, 2 + k % 2, :], e_hT[:, c, :], e_hT_lo[:, c, :], w_hi[k % 2][:, c, :],
                                 ring_gu(f, k, ring_parts)[:, c, :], c == 0, c == KC - 1)
                mm.then_inc(m("gu"), 1)
                if k:
                    down(k - 1)
            turn(f.steps - 1)
            down(f.steps - 1)
            if not last:
                moe_gather(pe, f, m, g + 1)
            pe.wait_ge(*m.at("y", g + 1))
            pe.wait_ge(*m.at("added", 4 * g + 4))
            for t in range(NT):
                for b in range(2):
                    pe.matmul(ps[:, ADD_BANKS[2 * t + b], :], e_selT[:, t * P:(t + 1) * P], e_y[:, b * 512:(b + 1) * 512],
                              start=True, stop=True).then_inc(m("scattered"), 1)
            if not last:
                moe_places(pe, f, m, g + 1)

        def act_upper_gu(act, f, m, g, k, pieces):
            if pieces[0] == 0:
                act.wait_ge(*m.at(f"slot{f.slots[k]}_ready", 32 * (g * f.fills[f.slots[k]] + f.nth[k])))
            for j in pieces:
                c = slice(2 * j, 2 * j + 2)
                act.copy(w_hi[k % 2][:, c, :], ring_gu(f, k)[:, c, :]).then_inc(m("upper"), 1)

        def moe_act_rows(act, f, m, g):
            act.wait_ge(*m.at("gathered", g + 1))
            for c in range(KC):
                ins = act.activation(e_hT[:, c, :], ps[:, 5 + c // 4, (c % 4) * P:(c % 4 + 1) * P], ACT.Identity,
                                     scale=f.gain[:, c:c + 1])
            ins.then_inc(m("rows_upper"), 1)
            act.wait_ge(*m.at("sel_turned", g + 1))
            act.copy(e_selT, ps[:, 5, 0:S])
            act.copy(e_gate[:, 0:f.e], ps[:, 5, S:S + f.e]).then_inc(m("places"), 1)

        def moe_act_bucket(act, f, m, g, last):
            def hidden(k):
                act.wait_ge(*m.at("turned", g * f.steps + k + 1))
                act.copy(x_hidT[:, k % 2].rearrange("p c n -> p (c n)"), ps[:, 4, 0:FB]).then_inc(m("hidT_upper"), 1)

            for k in range(f.steps):
                ahead = k + 1 < f.steps
                if ahead:
                    act_upper_gu(act, f, m, g, k + 1, [0])
                if k:
                    hidden(k - 1)
                if ahead:
                    act_upper_gu(act, f, m, g, k + 1, [1, 2, 3])
                act.wait_ge(*m.at("gu", g * f.steps + k + 1))
                act.activation(f_sg[:, k % 2, :], ps[:, 2 + k % 2, 0:FB], ACT.Silu).then_inc(m("silu"), 1)
                act.wait_ge(*m.at(f"down{f.slots[k]}_ready", 16 * (g * f.fills[f.slots[k]] + f.nth[k])))
                for c in range(FB // P):
                    act.copy(d_hi[k % 2][:, c, :], ring_down(f, k)[:, c, :]).then_inc(m("upper"), 1)
            hidden(f.steps - 1)
            if not last:
                act_upper_gu(act, f, m, g + 1, 0, [0, 1, 2, 3])
                moe_act_rows(act, f, m, g + 1)

        def moe_dve_sel(dve, f, m, g):
            for t in range(NT):
                place = r_place[:, t, g:g + 1] if isinstance(g, int) else r_place[:, t, bass.ds(g, 1)]
                ins = dve.tensor_scalar(e_sel[:, t, :], slot_no[:], place, None, ALU.is_equal)
            ins.then_inc(m("sel"), 1)

        def dve_lower_gu(dve, f, m, g, k, pieces):
            for j in pieces:
                c = slice(2 * j, 2 * j + 2)
                dve.wait_ge(*m.at("upper", gu_pieces(f, g, k, j)))
                dve.tensor_tensor(ring_gu(f, k, ring_parts)[:, c, :], ring_gu(f, k)[:, c, :], f32(w_hi[k % 2][:, c, :]),
                                  ALU.subtract)\
                    .then_inc(m("split"), 1)

        def moe_dve_rows(dve, f, m, g):
            dve.wait_ge(*m.at("rows_upper", g + 1))
            for c in range(KC):
                ins = dve.scalar_tensor_tensor(out=e_hT_lo[:, c, :], in0=ps[:, 5 + c // 4, (c % 4) * P:(c % 4 + 1) * P],
                                               scalar=f.gain[:, c:c + 1], in1=f32(e_hT[:, c, :]), op0=ALU.mult, op1=ALU.subtract)
            ins.then_inc(m("rows"), 1)

        def moe_dve_bucket(dve, f, m, g, last):
            def hidden(k):
                dve.wait_ge(*m.at("hidT_upper", g * f.steps + k + 1))
                flat_hi, flat_lo = [a[:, k % 2].rearrange("p c n -> p (c n)") for a in (x_hidT, x_hidT_lo)]
                dve.tensor_tensor(flat_lo, ps[:, 4, 0:FB], f32(flat_hi), ALU.subtract).then_inc(m("hidT"), 1)

            dve.wait_ge(*m.at("places", g + 1))
            if not last:
                moe_dve_sel(dve, f, m, g + 1)
            for k in range(f.steps):
                ahead = k + 1 < f.steps
                if ahead:
                    dve_lower_gu(dve, f, m, g, k + 1, [0])
                if k:
                    hidden(k - 1)
                if ahead:
                    dve_lower_gu(dve, f, m, g, k + 1, [1, 2, 3])
                dve.wait_ge(*m.at("silu", g * f.steps + k + 1))
                dve.scalar_tensor_tensor(out=f_hid[:, k % 2, :], in0=ps[:, 2 + k % 2, FB:2 * FB],
                                         scalar=e_gate[:, k // f.nb:k // f.nb + 1], in1=f_sg[:, k % 2, :],
                                         op0=ALU.mult, op1=ALU.mult).then_inc(m("hid"), 1)
                for c in range(FB // P):
                    dve.wait_ge(*m.at("upper", down_pieces(f, g, k, c)))
                    dve.tensor_tensor(ring_down(f, k, ring_parts)[:, c, :], ring_down(f, k)[:, c, :],
                                      f32(d_hi[k % 2][:, c, :]), ALU.subtract).then_inc(m("split"), 1)
            hidden(f.steps - 1)
            if not last:
                dve_lower_gu(dve, f, m, g + 1, 0, [0, 1])
            dve.wait_ge(*m.at("used", (g + 1) * f.steps))
            dve.tensor_copy(e_y, ps[:, 0:2, :].rearrange("p a b -> p (a b)")).then_inc(m("y"), 1)
            if not last:
                dve_lower_gu(dve, f, m, g + 1, 0, [2, 3])
                moe_dve_rows(dve, f, m, g + 1)
            for q in range(4):
                dve.wait_ge(*m.at("scattered", 4 * g + q + 1))
                cols = x[:, q // 2, (q % 2) * 512:(q % 2 + 1) * 512]
                dve.tensor_tensor(cols, cols, ps[:, ADD_BANKS[q], :], ALU.add).then_inc(m("added"), 1)

        def moe_pass(eng, bucket, f, m):
            with eng.Fori(0, f.buckets - 1) as g:
                bucket(eng, f, m, g, False)
            bucket(eng, f, m, f.buckets - 1, True)

        def moe_pe_pass(pe, f, m):
            moe_gather(pe, f, m, 0)
            moe_places(pe, f, m, 0)
            moe_pass(pe, moe_pe_bucket, f, m)

        def moe_act_pass(act, f, m):
            act_upper_gu(act, f, m, 0, 0, [0, 1, 2, 3])
            moe_act_rows(act, f, m, 0)
            moe_pass(act, moe_act_bucket, f, m)

        def moe_dve_pass(dve, f, m):
            moe_dve_sel(dve, f, m, 0)
            dve.drain().then_inc(m("added"), 4)
            dve_lower_gu(dve, f, m, 0, 0, [0, 1, 2, 3])
            moe_dve_rows(dve, f, m, 0)
            moe_pass(dve, moe_dve_bucket, f, m)

        def stage_moe(f):
            m = Pass(f, 0)

            def pe_(pe):
                moe_pe_pass(pe, f, m)
                end_stage(pe, "tensor")

            def act_(act):
                moe_act_pass(act, f, m)
                end_stage(act, "scalar")

            def dve_(dve):
                moe_dve_pass(dve, f, m)
                end_stage(dve, "vector")

            return pe_, act_, dve_, idle_pool

        def stage_moe_rest(f):
            m = Pass(f, 1)

            def pe_(pe):
                with overfull(pe, f):
                    moe_pe_pass(pe, f, m)
                pe.end_ifs()
                end_stage(pe, "tensor")

            def act_(act):
                with overfull(act, f):
                    moe_act_pass(act, f, m)
                act.end_ifs()
                end_stage(act, "scalar")

            def dve_(dve):
                with overfull(dve, f):
                    dve.tensor_scalar(r_place[:, :, 0:f.buckets], r_place[:, :, 0:f.buckets], -float(P), None, ALU.add).then_inc(m("shifted"), 1)
                    dve.wait_ge(*m.at("shifted", 1))
                    moe_dve_pass(dve, f, m)
                dve.end_ifs()
                end_stage(dve, "vector")
                if f is moe1:
                    dve.wait_ge(sig("rest_streamed"), 1)
                    for n, s in sems.items():
                        if n.startswith("moe_rest_"):
                            dve.sem_clear(s)

            return pe_, act_, dve_, idle_pool

        ML = Arena(arena)
        z = ML.take(NT, ZW)
        ycat = ML.take(NT, D)
        ml_at = ML.at

        def z_copy_act(act, j, src):
            return act.copy(z[:, j.tile, j.col:j.col + j.n], src)

        def z_copy_dve(dve, j, src):
            return dve.tensor_copy(z[:, j.tile, j.col:j.col + j.n], src)

        def rope_dve(dve):
            a, b = small[:, 32:48], small[:, 48:64]
            a2, b2 = [v.rearrange("p (t n) -> p t n", t=NT) for v in (a, b)]
            vstep(dve, dve.tensor_copy(small[:, 64:66], pos_i[:]))
            vstep(dve, dve.tensor_tensor(a2, small[:, 64:66].unsqueeze(2).to_broadcast([P, NT, ROPE_HALF]),
                                         freq[:].unsqueeze(1).to_broadcast([P, NT, ROPE_HALF]), ALU.mult))
            magic = 1.5 * 2.0 ** 23
            vstep(dve, dve.tensor_scalar(b, a, 1.0 / (2 * np.pi), magic, ALU.mult, ALU.add))
            vstep(dve, dve.tensor_scalar(b, b, -magic, None, ALU.add))
            rest = 2 * np.pi
            for bits in (8, 9, None):
                if bits is None:
                    part = float(np.float32(rest))
                else:
                    e = np.floor(np.log2(abs(rest)))
                    q = 2.0 ** (e - bits)
                    part = float(np.floor(rest / q) * q)
                rest -= part
                vstep(dve, dve.scalar_tensor_tensor(out=a, in0=b, scalar=-part, in1=a, op0=ALU.mult, op1=ALU.add))
            lim = float(np.nextafter(np.float32(np.pi), np.float32(0)))
            dve.tensor_scalar(a, a, lim, -lim, ALU.min, ALU.max).then_inc(sig("rope_angle"), 1)
            dve.wait_ge(sig("rope_sin"), 1)
            c = cos_t[:].rearrange("p t n -> p (t n)")
            vstep(dve, dve.tensor_tensor(c, c, c, ALU.mult))
            dve.tensor_scalar(c, c, -2.0, 1.0, ALU.mult, ALU.add)

        def rope_act(act):
            act.wait_ge(sig("rope_angle"), 1)
            a = small[:, 32:48]
            act.activation(sin_t[:].rearrange("p t n -> p (t n)"), a, ACT.Sin)
            act.activation(cos_t[:].rearrange("p t n -> p (t n)"), a, ACT.Sin, scale=0.5).then_inc(sig("rope_sin"), 1)

        MG = Arena(arena)
        MG.at = ml_at
        s_v = MG.take(NT, AH, HD)
        s_sq = MG.take(NT, AH, HD)
        s_wT = MG.take(AH, P)
        s_u = MG.take(NT, AW)

        def gating(l):
            def pe_(pe):
                for h in range(AH):
                    mm = pe.transpose(ps[:, 0, h * P:(h + 1) * P], l_ws[:, h, :], ident[:])
                mm.then_inc(sig("gat_wT"), 1)
                pe.wait_ge(sig("gat_v"), l + 1)
                for h in range(AH):
                    mm = pe.matmul(ps[:, 1, h * P:(h + 1) * P], s_wT[:, h, :], s_v[:, :, h, :], start=True, stop=True)
                mm.then_inc(sig("gat_mixed"), 1)
                end_stage(pe, "tensor")

            def act_(act):
                act.activation(s_v.rearrange("p t h n -> p t (h n)"), z[:, :, AW:2 * AW], ACT.Gelu_apprx_tanh)\
                    .then_inc(sig("gat_gelu"), 1)
                act.activation(s_u, z[:, :, 0:AW], ACT.Gelu_apprx_tanh).then_inc(sig("gat_gelu"), 1)
                act.wait_ge(sig("gat_var"), l + 1)
                act.activation(small[:, 24:32], small[:, 16:24], ACT.Sqrt).then_inc(sig("gat_sd"), 1)
                end_stage(act, "scalar")

            def dve_(dve):
                v8 = s_v.rearrange("p t h n -> p (t h) n")
                q8 = s_sq.rearrange("p t h n -> p (t h) n")
                dve.wait_ge(sig("gat_wT"), l + 1)
                dve.tensor_tensor(s_wT, ps[:, 0, :].rearrange("p (h n) -> p h n", h=AH),
                                  causal_up[:].unsqueeze(1).to_broadcast([P, AH, P]), ALU.mult)
                dve.wait_ge(sig("gat_gelu"), 2 * l + 1)
                vstep(dve, dve.tensor_reduce(small[:, 0:8], v8, AX, ALU.add))
                vstep(dve, dve.tensor_scalar(small[:, 8:16], small[:, 0:8], 1.0 / HD, None, ALU.mult))
                vstep(dve, dve.tensor_tensor(v8, v8, small[:, 8:16].unsqueeze(2).to_broadcast([P, 8, HD]), ALU.subtract))
                vstep(dve, dve.tensor_tensor(q8, v8, v8, ALU.mult))
                vstep(dve, dve.tensor_reduce(small[:, 0:8], q8, AX, ALU.add))
                dve.tensor_scalar(small[:, 16:24], small[:, 0:8], 1.0 / HD, LN_EPS, ALU.mult, ALU.add).then_inc(sig("gat_var"), 1)
                dve.wait_ge(sig("gat_sd"), l + 1)
                vstep(dve, dve.reciprocal(small[:, 0:8], small[:, 24:32]))
                vstep(dve, dve.tensor_tensor(v8, v8, small[:, 0:8].unsqueeze(2).to_broadcast([P, 8, HD]), ALU.mult))
                vf = s_v.rearrange("p t h n -> p t (h n)")
                vstep(dve, dve.tensor_tensor(vf, vf, l_row[:, 7, :].unsqueeze(1).to_broadcast([P, NT, AW]), ALU.mult))
                dve.tensor_tensor(vf, vf, l_row[:, 8, :].unsqueeze(1).to_broadcast([P, NT, AW]), ALU.add)\
                    .then_inc(sig("gat_v"), 1)
                dve.wait_ge(sig("gat_mixed"), l + 1)
                dve.wait_ge(sig("gat_gelu"), 2 * l + 2)
                for h in range(AH):
                    dve.scalar_tensor_tensor(out=ycat[:, :, h * HD:(h + 1) * HD],
                                             in0=ps[:, 1, h * P:(h + 1) * P].rearrange("p (t n) -> p t n", t=NT),
                                             scalar=l_bsT[:, h:h + 1], in1=s_u[:, :, h * HD:(h + 1) * HD],
                                             op0=ALU.add, op1=ALU.mult)
                end_stage(dve, "vector")

            return pe_, act_, dve_, idle_pool

        MW = Arena(arena)
        MW.at = ml_at
        HP = BH // 2
        half_t = lambda: MW.take(NT, BW)
        w_lw, w_a, w_g, w_kk, w_km, w_R, w_K, w_A, w_Ke, w_B, w_Be = [half_t() for _ in range(11)]
        w_loT = MW.take(NT, S)
        w_AT, w_RT, w_BT, w_KT = [MW.take(HP, S) for _ in range(4)]
        w_MT, w_RB, w_RK = [[MW.take(BH, P) for _ in range(NT)] for _ in range(3)]
        w_TT = MW.take(BH, P)
        w_WT = w_lw.rearrange("p t n -> p (t n)").rearrange("p (h n) -> p h n", h=HP)
        w_htmp = w_loT[:, 1, :].rearrange("p (h n) -> p h n", h=HP)
        w_T, w_Lm, w_LTm, w_Yb = [hT_flat[:, k * 512:(k + 1) * 512].rearrange("p (h n) -> p h n", h=BH) for k in range(4)]
        w_L, w_LT = [z[:, k, 0:512].rearrange("p (h n) -> p h n", h=BH) for k in range(2)]
        w_Zb = ycat[:, 0, 512:1024].rearrange("p (h n) -> p h n", h=BH)
        w_lora = ycat[:, :, 512:768]
        w_H = ycat[:, 1, 512:768].rearrange("p (h n) -> p h n", h=HP)
        w_mv = w_loT[:, 0, :]
        w_Uv, w_U = w_kk, w_a
        w_y = w_lw
        w_ss = small[:, 0:8]
        w_cend = small[:, 96:104]
        LEV = 6
        zr, zk, zv = [z[:, :, ZB0 + k * BW:ZB0 + (k + 1) * BW] for k in range(3)]

        def row(k):
            return l_row[:, k, :].unsqueeze(1).to_broadcast([P, NT, BW])

        def heads(ap):
            return ap.rearrange("p t (h n) -> p t h n", h=BH)

        def per_head(v):
            return v.rearrange("p (t h) -> p t h", t=NT).unsqueeze(3).to_broadcast([P, NT, BH, HD])

        def rwkv(l):
            def at(name, k, per):
                return ended(name, k, l, per)

            def pe_(pe):
                for t in range(NT):
                    for b in range(2):
                        cols = slice(ZB0 + b * 512, ZB0 + (b + 1) * 512)
                        mm = pe.matmul(ps[:, 2 * t + b, :], shift_dn[:], z[:, t, cols], start=True, stop=(t == 0))
                        if t:
                            mm = pe.matmul(ps[:, 2 * t + b, :], shift_dn_edge[:], z[:, t - 1, cols], start=False, stop=True)
                mm.then_inc(sig("rw_shift"), 1)
                pe.wait_ge(*at("rw_lora", 1, 1))
                for k in range(2):
                    for t in range(NT):
                        mm = pe.transpose(ps[:, 4, k * S + t * P:k * S + (t + 1) * P], w_lora[:, t, k * P:(k + 1) * P], ident[:])
                mm.then_inc(sig("rw_loT_psum"), 1)
                pe.wait_ge(*at("rw_loT", 1, 1))
                for t in range(NT):
                    tok = slice(t * P, (t + 1) * P)
                    pe.matmul(ps[:, 5, t * BW:(t + 1) * BW], w_loT[0:64, 0, tok], l_lora[0:64, 0, :], start=True, stop=True)
                    pe.matmul(ps[:, 6, t * BW:(t + 1) * BW], w_loT[64:128, 0, tok], l_lora[64:128, 0, :], start=True, stop=True)
                    mm = pe.matmul(ps[:, 7, t * BW:(t + 1) * BW], w_loT[:, 1, tok], l_lora[:, 1, :], start=True, stop=True)
                mm.then_inc(sig("rw_lin"), 1)
                pe.wait_ge(*at("rw_lw", 1, 1))
                for k, m in enumerate((tri_inc, tri_str, same_chunk)):
                    for t in range(NT):
                        pe.matmul(ps[:, k, t * BW:(t + 1) * BW], m[:], w_lw[:, t, :], start=True, stop=True)
                for t in range(NT):
                    for p in range(HP):
                        q = 2 * (t * HP + p)
                        mm = pe.matmul(ps[:, 3, q:q + 2], w_lw[:, t, p * P:(p + 1) * P], half_ind[:], start=True, stop=True)
                mm.then_inc(sig("rw_cum"), 1)
                pe.wait_ge(*at("rw_rkab", 1, 1))
                for q, a in enumerate((w_A, w_R, w_B, w_K)):
                    for p in range(HP):
                        for t in range(NT):
                            mm = pe.transpose(ps[:, q, p * S + t * P:p * S + (t + 1) * P], a[:, t, p * P:(p + 1) * P], ident[:])
                    mm.then_inc(sig("rw_turned"), 1)
                pe.wait_ge(*at("rw_AT", 1, 1))
                pe.wait_ge(*at("rw_BT", 1, 1))
                for t in range(NT):
                    tok = slice(t * P, (t + 1) * P)
                    if t:
                        pe.wait_ge(*at("rw_Uv", t, NT))
                    for s in range(2):
                        half = slice(64 * s, 64 * s + 64)
                        for k, (a, b) in enumerate(((w_BT, w_AT), (w_AT, w_BT), (w_KT, w_AT), (w_BT, w_RT), (w_KT, w_RT))):
                            for p in range(HP):
                                c = (k % 2) * S + p * P
                                mm = pe.matmul(ps[:, 3 * s + k // 2, c:c + P], a[half, p, tok], b[half, p, tok],
                                               start=True, stop=True)
                    mm.then_inc(sig("rw_scores"), 1)
                    for k in range(1, LEV):
                        n = t * (LEV - 1) + k
                        pe.wait_ge(*at("rw_tt", t * LEV + k, NT * LEV))
                        pe.wait_ge(*at("rw_lm", n, NT * (LEV - 1)))
                        for h in range(BH):
                            mm = pe.matmul(ps[:, 6, h * P:(h + 1) * P], w_Lm[:, h, :], w_TT[:, h, :], start=True, stop=True)
                        mm.then_inc(sig("rw_y_psum"), 1)
                        pe.wait_ge(*at("rw_t", t * (LEV - 1) + k, NT * (LEV - 1)))
                        if k + 1 < LEV:
                            for h in range(BH):
                                mm = pe.matmul(ps[:, 7, h * P:(h + 1) * P], w_LTm[:, h, :], w_T[:, h, :], start=True, stop=True)
                            mm.then_inc(sig("rw_z_psum"), 1)
                        pe.wait_ge(*at("rw_y", n, NT * (LEV - 1)))
                        for h in range(BH):
                            mm = pe.matmul(ps[:, 6, h * P:(h + 1) * P], w_T[:, h, :], w_Yb[:, h, :], start=True, stop=True)
                        if k + 1 == LEV:
                            mm.then_inc(sig("rw_dt"), 1)
                        else:
                            pe.wait_ge(*at("rw_z", t * (LEV - 2) + k, NT * (LEV - 2)))
                            for h in range(BH):
                                mm = pe.matmul(ps[:, 7, h * P:(h + 1) * P], w_TT[:, h, :], w_Zb[:, h, :], start=True, stop=True)
                            mm.then_inc(sig("rw_dt"), 1)
                    pe.wait_ge(*at("rw_tt", (t + 1) * LEV, NT * LEV))
                    pe.wait_ge(*at("rw_masked", t + 1, NT))
                    for s in range(2):
                        for p in range(HP):
                            h = 2 * p + s
                            pe.matmul(ps[64 * s:64 * s + 64, 0, p * P:(p + 1) * P], w_A[:, t, h * HD:(h + 1) * HD],
                                      w_TT[:, s * HP + p, :], start=True, stop=True)
                            mm = pe.matmul(ps[:, 1, h * HD:(h + 1) * HD], w_MT[t][:, s * HP + p, :], zv[:, t, h * HD:(h + 1) * HD],
                                           start=True, stop=True)
                    mm.then_inc(sig("rw_mv_psum"), 1)
                    pe.wait_ge(*at("rw_mv", t + 1, NT))
                    for s in range(2):
                        for p in range(HP):
                            h = 2 * p + s
                            mm = pe.matmul(ps[:, 2, h * HD:(h + 1) * HD], w_TT[:, s * HP + p, :], w_mv[:, h * HD:(h + 1) * HD],
                                           start=True, stop=True)
                    mm.then_inc(sig("rw_Uv_psum"), 1)
                pe.wait_ge(*at("rw_Uv", NT, NT))
                for t in range(NT):
                    for h in range(BH):
                        i = (h % 2) * HP + h // 2
                        pe.matmul(ps[:, 4 + t, h * HD:(h + 1) * HD], w_RK[t][:, i, :], zv[:, t, h * HD:(h + 1) * HD],
                                  start=(h == 0), stop=False, skip_group_check=True)
                chunks = S // RC
                for n in range(chunks):
                    t, o = n * RC // P, n * RC % P
                    part, tok = slice(o, o + RC), slice(n * RC, (n + 1) * RC)
                    if n:
                        pe.wait_ge(*at("rw_H", n, chunks - 1))
                        for p in range(HP):
                            pe.matmul(ps[part, 3, p * P:(p + 1) * P], w_WT[:, p, tok], w_H[:, p, :], start=True, stop=True)
                        for p in range(HP):
                            mm = pe.matmul(ps[part, 4 + t, p * P:(p + 1) * P], w_RT[:, p, tok], w_H[:, p, :],
                                           start=False, stop=False, skip_group_check=True)
                        mm.then_inc(sig("rw_WH"), 1)
                    pe.wait_ge(*at("rw_U", n + 1, chunks))
                    if n + 1 < chunks:
                        for p in range(HP):
                            cols = slice(p * P, (p + 1) * P)
                            pe.matmul(ps[:, 6, cols], w_Be[part, t, cols], w_U[part, t, cols], start=True, stop=False)
                            mm = pe.matmul(ps[:, 6, cols], w_Ke[part, t, cols], z[part, t, ZB0 + 2 * BW + p * P:ZB0 + 2 * BW + (p + 1) * P],
                                           start=False, stop=True)
                        mm.then_inc(sig("rw_dH"), 1)
                for t in range(NT):
                    for h in range(BH):
                        i = (h % 2) * HP + h // 2
                        mm = pe.matmul(ps[:, 4 + t, h * HD:(h + 1) * HD], w_RB[t][:, i, :], w_U[:, t, h * HD:(h + 1) * HD],
                                       start=False, stop=(h == BH - 1), skip_group_check=True)
                mm.then_inc(sig("rw_Y"), 1)
                end_stage(pe, "tensor")

            def act_(act):
                act.wait_ge(*at("rw_mixed", 1, 1))
                act.activation(w_lora[:, :, 0:64], z[:, :, ZB0 + 768:ZB0 + 832], ACT.Tanh)
                act.copy(w_lora[:, :, 64:128], z[:, :, ZB0 + 832:ZB0 + 896])
                act.activation(w_lora[:, :, 128:256], z[:, :, ZB0 + 896:ZB0 + 1024], ACT.Sigmoid).then_inc(sig("rw_lora"), 1)
                act.wait_ge(*at("rw_logit", 1, 1))
                act.activation(w_lw, w_lw, ACT.Sigmoid).then_inc(sig("rw_sig"), 1)
                act.activation(w_a, w_a, ACT.Sigmoid).then_inc(sig("rw_sig"), 1)
                act.copy(w_g.rearrange("p t n -> p (t n)"), ps[:, 7, :])
                act.wait_ge(*at("rw_kk2", 1, 1))
                act.activation(small[:, 16:24], small[:, 8:16], ACT.Sqrt).then_inc(sig("rw_kkrt"), 1)
                act.wait_ge(*at("rw_cum", 1, 1))
                f = lambda a: a.rearrange("p t n -> p (t n)")
                act.copy(f(w_Ke), ps[:, 2, :])
                act.activation(f(w_R), ps[:, 0, :], ACT.Exp)
                act.activation(f(w_K), ps[:, 0, :], ACT.Exp, scale=-1.0).then_inc(sig("rw_total"), 1)
                act.activation(f(w_A), ps[:, 1, :], ACT.Exp)
                act.activation(w_cend, ps[:, 3, 0:8], ACT.Exp)
                act.wait_ge(*at("rw_toend", 1, 1))
                act.activation(f(w_Ke), f(w_Ke), ACT.Exp).then_inc(sig("rw_exp"), 1)
                act.wait_ge(*at("rw_turned", 2, 4))
                act.copy(w_AT, ps[:, 0, :].rearrange("p (h n) -> p h n", h=HP))
                act.copy(w_RT, ps[:, 1, :].rearrange("p (h n) -> p h n", h=HP)).then_inc(sig("rw_AT"), 1)
                for t in range(NT):
                    act.wait_ge(*at("rw_scores", t + 1, NT))
                    for s in range(2):
                        act.copy(w_LT[:, s * HP:(s + 1) * HP, :], ps[:, 3 * s, 0:S].rearrange("p (h n) -> p h n", h=HP))
                        ins = act.copy(w_L[:, s * HP:(s + 1) * HP, :], ps[:, 3 * s, S:2 * S].rearrange("p (h n) -> p h n", h=HP))
                    ins.then_inc(sig("rw_L"), 1)
                    for k in range(1, LEV):
                        act.wait_ge(*at("rw_y_psum", t * (LEV - 1) + k, NT * (LEV - 1)))
                        act.copy(w_Yb, ps[:, 6, :].rearrange("p (h n) -> p h n", h=BH)).then_inc(sig("rw_y"), 1)
                    act.wait_ge(*at("rw_mv_psum", t + 1, NT))
                    act.copy(w_WT[:, :, t * P:(t + 1) * P], ps[:, 0, 0:S].rearrange("p (h n) -> p h n", h=HP))
                    act.copy(w_mv, ps[:, 1, 0:BW]).then_inc(sig("rw_mv"), 1)
                act.wait_ge(*at("rw_var", 1, 1))
                act.activation(small[:, 24:32], small[:, 16:24], ACT.Sqrt).then_inc(sig("rw_sd"), 1)
                end_stage(act, "scalar")

            def pool_(pool):
                for t in range(NT):
                    pool.wait_ge(*at("rw_L", t + 1, NT))
                    for k in range(1, LEV):
                        if t or k > 1:
                            pool.wait_ge(*at("rw_y_psum", t * (LEV - 1) + k - 1, NT * (LEV - 1)))
                            pool.wait_ge(*at("rw_z_psum", t * (LEV - 2) + min(k - 1, LEV - 2), NT * (LEV - 2)))
                        pool.tensor_tensor(w_Lm, w_L, low_b[:, k, :].unsqueeze(1).to_broadcast([P, BH, P]), ALU.mult)
                        pool.tensor_tensor(w_LTm, w_LT, up_b[:, k, :].unsqueeze(1).to_broadcast([P, BH, P]), ALU.mult)\
                            .then_inc(sig("rw_lm"), 1)
                end_stage(pool, "gpsimd")

            def dve_(dve):
                f = lambda a: a.rearrange("p t n -> p (t n)")
                dve.wait_ge(*at("rw_shift", 1, 1))
                mixt = arena[:, ml_at + 5 * 512:ml_at + 5 * 512 + 1024]
                for t in range(NT):
                    zb_t = z[:, t, ZB0:ZC0]
                    vstep(dve, dve.tensor_tensor(mixt, ps[:, 2 * t:2 * t + 2, :].rearrange("p a b -> p (a b)"), l_mu[:], ALU.mult))
                    ins = dve.tensor_tensor(zb_t, zb_t, mixt, ALU.add)
                    if t + 1 < NT:
                        vstep(dve, ins)
                ins.then_inc(sig("rw_mixed"), 1)
                dve.wait_ge(*at("rw_mixed", 1, 1))
                dve.wait_ge(*at("rw_loT_psum", 1, 1))
                dve.tensor_copy(w_loT.rearrange("p t n -> p (t n)"), ps[:, 4, :]).then_inc(sig("rw_loT"), 1)
                vstep(dve, dve.tensor_tensor(w_kk, zk, row(2), ALU.mult))
                vstep(dve, dve.tensor_tensor(w_B, w_kk, w_kk, ALU.mult))
                vstep(dve, dve.tensor_reduce(w_ss, w_B.rearrange("p t (h n) -> p (t h) n", h=BH), AX, ALU.add))
                dve.tensor_scalar(small[:, 8:16], w_ss, 1e-24, None, ALU.max).then_inc(sig("rw_kk2"), 1)
                dve.wait_ge(*at("rw_lin", 1, 1))
                dve.tensor_tensor(w_lw, ps[:, 5, :].rearrange("p (t n) -> p t n", t=NT), row(0), ALU.add)
                dve.tensor_tensor(w_a, ps[:, 6, :].rearrange("p (t n) -> p t n", t=NT), row(1), ALU.add)\
                    .then_inc(sig("rw_logit"), 1)
                dve.wait_ge(*at("rw_sig", 1, 2))
                dve.tensor_scalar(f(w_lw), f(w_lw), -float(np.exp(-0.5)), None, ALU.mult).then_inc(sig("rw_lw"), 1)
                dve.wait_ge(*at("rw_kkrt", 1, 1))
                vstep(dve, dve.reciprocal(small[:, 0:8], small[:, 16:24]))
                vstep(dve, dve.tensor_tensor(heads(w_kk), heads(w_kk), per_head(small[:, 0:8]), ALU.mult))
                dve.wait_ge(*at("rw_sig", 2, 2))
                vstep(dve, dve.scalar_tensor_tensor(out=w_km, in0=w_a, scalar=-1.0, in1=row(3), op0=ALU.add, op1=ALU.mult))
                vstep(dve, dve.scalar_tensor_tensor(out=w_km, in0=w_km, scalar=1.0, in1=zk, op0=ALU.add, op1=ALU.mult))
                vstep(dve, dve.tensor_tensor(f(w_B), f(w_kk), f(w_a), ALU.mult))
                dve.wait_ge(*at("rw_total", 1, 1))
                dve.tensor_tensor(f(w_Ke), f(w_Ke), ps[:, 0, :], ALU.subtract).then_inc(sig("rw_toend"), 1)
                dve.wait_ge(*at("rw_exp", 1, 1))
                dve.tensor_tensor(w_R, w_R, zr, ALU.mult)
                dve.scalar_tensor_tensor(out=f(w_A), in0=f(w_kk), scalar=-1.0, in1=f(w_A), op0=ALU.mult, op1=ALU.mult)
                vstep(dve, dve.tensor_tensor(f(w_Be), f(w_B), f(w_Ke), ALU.mult))
                dve.tensor_tensor(f(w_Ke), f(w_km), f(w_Ke), ALU.mult)
                vstep(dve, dve.tensor_tensor(f(w_B), f(w_B), f(w_K), ALU.mult))
                dve.tensor_tensor(f(w_K), f(w_K), f(w_km), ALU.mult).then_inc(sig("rw_rkab"), 1)
                dve.wait_ge(*at("rw_turned", 4, 4))
                dve.tensor_copy(w_BT, ps[:, 2, :].rearrange("p (h n) -> p h n", h=HP))
                dve.tensor_copy(w_KT, ps[:, 3, :].rearrange("p (h n) -> p h n", h=HP)).then_inc(sig("rw_BT"), 1)
                for t in range(NT):
                    dve.wait_ge(*at("rw_scores", t + 1, NT))
                    dve.wait_ge(*at("rw_L", t + 1, NT))
                    idn = ident[:].unsqueeze(1).to_broadcast([P, BH, P])
                    dve.tensor_tensor(w_T, w_L, low_b[:, 0, :].unsqueeze(1).to_broadcast([P, BH, P]), ALU.mult)
                    vstep(dve, dve.tensor_tensor(w_TT, w_LT, up_b[:, 0, :].unsqueeze(1).to_broadcast([P, BH, P]), ALU.mult))
                    dve.tensor_tensor(w_TT, w_TT, idn, ALU.add).then_inc(sig("rw_tt"), 1)
                    dve.tensor_tensor(w_T, w_T, idn, ALU.add).then_inc(sig("rw_t"), 1)
                    for s in range(2):
                        hs = slice(s * HP, (s + 1) * HP)
                        for k, (dst, m) in enumerate(((w_MT[t], tri_str), (w_RB[t], tri_inc), (w_RK[t], tri_inc))):
                            c = (k % 2) * S
                            ins = dve.tensor_tensor(dst[:, hs, :], ps[:, 3 * s + 1 + k // 2, c:c + S].rearrange("p (h n) -> p h n", h=HP),
                                                    m[:].unsqueeze(1).to_broadcast([P, HP, P]), ALU.mult)
                    ins.then_inc(sig("rw_masked"), 1)
                    for k in range(1, LEV):
                        n = t * (LEV - 1) + k
                        if k + 1 < LEV:
                            dve.wait_ge(*at("rw_z_psum", t * (LEV - 2) + k, NT * (LEV - 2)))
                            dve.tensor_copy(w_Zb, ps[:, 7, :].rearrange("p (h n) -> p h n", h=BH)).then_inc(sig("rw_z"), 1)
                        dve.wait_ge(*at("rw_dt", n, NT * (LEV - 1)))
                        dve.tensor_tensor(w_TT, w_TT, ps[:, 6, :].rearrange("p (h n) -> p h n", h=BH), ALU.add)\
                            .then_inc(sig("rw_tt"), 1)
                        if k + 1 < LEV:
                            dve.tensor_tensor(w_T, w_T, ps[:, 7, :].rearrange("p (h n) -> p h n", h=BH), ALU.add)\
                                .then_inc(sig("rw_t"), 1)
                    dve.wait_ge(*at("rw_Uv_psum", t + 1, NT))
                    dve.tensor_copy(w_Uv[:, t, :], ps[:, 2, 0:BW]).then_inc(sig("rw_Uv"), 1)
                dve.wait_ge(*at("rw_Uv", NT, NT))
                chunks = S // RC
                for n in range(chunks):
                    t, o = n * RC // P, n * RC % P
                    part = slice(o, o + RC)
                    if n:
                        dve.wait_ge(*at("rw_WH", n, chunks - 1))
                        dve.tensor_tensor(w_U[part, t, :], ps[part, 3, 0:BW], w_Uv[part, t, :], ALU.add).then_inc(sig("rw_U"), 1)
                    else:
                        dve.tensor_copy(w_U[part, t, :], w_Uv[part, t, :]).then_inc(sig("rw_U"), 1)
                    if n + 1 < chunks:
                        dve.wait_ge(*at("rw_dH", n + 1, chunks - 1))
                        dst = w_htmp if n else w_H
                        ins = dve.tensor_tensor(dst, ps[:, 6, 0:HP * P].rearrange("p (h n) -> p h n", h=HP),
                                                same_chunk[:].unsqueeze(1).to_broadcast([P, HP, P]), ALU.mult)
                        if n:
                            vstep(dve, ins)
                            for p in range(HP):
                                q = 2 * (t * HP + p) + n % 2
                                ins = dve.scalar_tensor_tensor(out=w_H[:, p, :], in0=w_H[:, p, :], scalar=w_cend[:, q:q + 1],
                                                               in1=w_htmp[:, p, :], op0=ALU.mult, op1=ALU.add)
                        ins.then_inc(sig("rw_H"), 1)
                dve.wait_ge(*at("rw_Y", 1, 1))
                Y = ps[:, 4:6, 0:BW]
                y8 = w_y.rearrange("p t (h n) -> p (t h) n", h=BH)
                vstep(dve, dve.tensor_copy(w_y, Y))
                vstep(dve, dve.tensor_reduce(small[:, 0:8], y8, AX, ALU.add))
                vstep(dve, dve.tensor_scalar(small[:, 8:16], small[:, 0:8], 1.0 / HD, None, ALU.mult))
                vstep(dve, dve.tensor_tensor(heads(w_y), heads(w_y), per_head(small[:, 8:16]), ALU.subtract))
                vstep(dve, dve.tensor_tensor(f(w_B), f(w_y), f(w_y), ALU.mult))
                vstep(dve, dve.tensor_reduce(small[:, 0:8], w_B.rearrange("p t (h n) -> p (t h) n", h=BH), AX, ALU.add))
                dve.tensor_scalar(small[:, 16:24], small[:, 0:8], 1.0 / HD, GN_EPS, ALU.mult, ALU.add).then_inc(sig("rw_var"), 1)
                vstep(dve, dve.tensor_tensor(w_km, w_km, zr, ALU.mult))
                vstep(dve, dve.tensor_tensor(w_km, w_km, row(4), ALU.mult))
                vstep(dve, dve.tensor_reduce(small[:, 32:40], w_km.rearrange("p t (h n) -> p (t h) n", h=BH), AX, ALU.add))
                vstep(dve, dve.tensor_tensor(heads(w_km), heads(zv), per_head(small[:, 32:40]), ALU.mult))
                dve.wait_ge(*at("rw_sd", 1, 1))
                vstep(dve, dve.reciprocal(small[:, 0:8], small[:, 24:32]))
                vstep(dve, dve.tensor_tensor(heads(w_y), heads(w_y), per_head(small[:, 0:8]), ALU.mult))
                vstep(dve, dve.tensor_tensor(w_y, w_y, row(5), ALU.mult))
                vstep(dve, dve.tensor_tensor(w_y, w_y, row(6), ALU.add))
                vstep(dve, dve.tensor_tensor(f(w_y), f(w_y), f(w_km), ALU.add))
                dve.tensor_tensor(ycat[:, :, AW:AW + BW], w_y, w_g, ALU.mult)
                end_stage(dve, "vector")

            return pe_, act_, dve_, pool_

        MN = Arena(arena)
        MN.at = ml_at
        n_qT = MN.take(CH // 2, S)
        n_qrT = MN.take(CH // 2, S)
        n_kT = MN.take(2, CG, S)
        n_rt = MN.take(4, NT, CH, ROPE_HALF)
        n_blk = MN.take(4, 16, NCMP)
        n_hid = MN.take(4, 16)
        n_kcT = MN.take(CG, 16)
        n_hv = MN.take(2, CH // 2, 16)
        n_vbd = MN.take(CH, HD)
        n_sc = MN.take(NT, CH, 16)
        n_pcT = MN.take(S)
        n_cs = MN.take(2, NT * CH)
        n_sm = [MN.take(4, S) for _ in range(2)]
        n_pT = [MN.take(4, 2, P) for _ in range(2)]
        n_mx, n_den, n_rd = [MN.take(8 * 4) for _ in range(3)]
        n_o = MN.take(4, HD)
        n_gate = MN.take(NT, 3 * CH)
        n_qr = z[:, :, 512:1024]
        n_k2 = hT_flat[:, 0:NT * 2 * CG * 2 * HD].rearrange("p (t k g s n) -> p t k g s n", t=NT, k=2, g=CG, s=2)
        n_kc2 = z[:, :, 0:512].rearrange("p t (q k n) -> p t q k n", q=4, k=2)
        GROUPS = [(br, t, s) for br in range(2) for t in range(NT) for s in range(2)]
        SCALE = HD ** -0.5

        def nsa(l):
            def at(name, k, per):
                return ended(name, k, l, per)

            def y_of(t, s):
                return ycat[:, t, AW + BW:D].rearrange("p (h s n) -> p h s n", h=CH // 2, s=2)[:, :, s, :]

            def gate_of(t, s, br):
                return n_gate[:, t, :].rearrange("p (h s b) -> p h s b", s=2, b=3)[:, :, s, br]

            def pe_(pe):
                for t in range(NT):
                    mm = pe.matmul(ps[:, 0, t * S:(t + 1) * S], shift_up[:], z[:, t, CKC:CKS], start=True, stop=(t == NT - 1))
                    if t + 1 < NT:
                        mm = pe.matmul(ps[:, 0, t * S:(t + 1) * S], shift_up_edge[:], z[:, t + 1, CKC:CKS], start=False, stop=True)
                mm.then_inc(sig("nsa_next"), 1)
                for p in range(CH // 2):
                    for t in range(NT):
                        mm = pe.transpose(ps[:, 1 + p // 2, (p % 2) * S + t * P:(p % 2) * S + (t + 1) * P],
                                          z[:, t, CQ + p * P:CQ + (p + 1) * P], ident[:])
                mm.then_inc(sig("nsa_q"), 1)
                pe.wait_ge(*at("nsa_pairs", 1, 1))
                for q in range(4):
                    for t in range(NT):
                        mm = pe.transpose(ps[:, 3 + q // 2, (q % 2) * S + t * P:(q % 2) * S + (t + 1) * P],
                                          n_kc2[:, t, q].rearrange("p k n -> p (k n)"), ident[:])
                mm.then_inc(sig("nsa_blkT"), 1)
                pe.wait_ge(*at("nsa_blk", 1, 1))
                u = cmp_unit[l]
                pe.wait_ge(slot_ready[u.slot], u.ready)
                for q in range(4):
                    for i in range(16):
                        mm = pe.matmul(ps[:, 5, q * 16:q * 16 + NCMP], u.view[:, q // 2, i, :], n_blk[:, q, i, :],
                                       start=(i == 0), stop=(i == 15))
                mm.then_inc(cmp_w_used, 1)
                pe.wait_ge(*at("nsa_hid", 1, 1))
                pe.matmul(ps[:, 6, 0:CG * 16], l_w2[:, 0:2, :].rearrange("p k n -> p (k n)"),
                          n_hid[:, 0:2, :].rearrange("p q n -> p (q n)"), start=True, stop=True)
                mm = pe.matmul(ps[:, 6, 64:64 + HD], n_hv.rearrange("p s h n -> p (s h n)"), l_w2[:, 2, :], start=True, stop=True)
                mm.then_inc(sig("nsa_cmp"), 1)
                pe.wait_ge(*at("nsa_kc", 1, 1))
                pe.wait_ge(*at("nsa_qT", 1, 1))
                for s in range(2):
                    half = slice(64 * s, 64 * s + 64)
                    for t in range(NT):
                        for p in range(CH // 2):
                            c = (t * 4 + p) * 16
                            mm = pe.matmul(ps[:, 3 + s, c:c + 16], n_qT[half, p, t * P:(t + 1) * P], n_kcT[half, p // 2, :],
                                           start=True, stop=True)
                mm.then_inc(sig("nsa_sc"), 1)
                pe.wait_ge(*at("nsa_rot", 1, 1))
                for p in range(CH // 2):
                    for t in range(NT):
                        mm = pe.transpose(ps[:, 1 + p // 2, (p % 2) * S + t * P:(p % 2) * S + (t + 1) * P],
                                          n_qr[:, t, p * P:(p + 1) * P], ident[:])
                mm.then_inc(sig("nsa_qr"), 1)
                pe.wait_ge(*at("nsa_vbd", 1, 1))
                for k in range(2):
                    for g in range(CG):
                        for t in range(NT):
                            mm = pe.transpose(ps[:, 6 + k, g * S + t * P:g * S + (t + 1) * P],
                                              n_k2[:, t, k, g].rearrange("p s n -> p (s n)"), ident[:])
                mm.then_inc(sig("nsa_k"), 1)
                pe.wait_ge(*at("nsa_pc", 1, 1))
                for t in range(NT):
                    mm = pe.transpose(ps[:, 0, t * P:(t + 1) * P], n_sc[:, t].rearrange("p h n -> p (h n)"), ident[:])
                mm.then_inc(sig("nsa_pcturned"), 1)
                pe.wait_ge(*at("nsa_pcT", 1, 1))
                for t in range(NT):
                    mm = pe.matmul(ps[:, 3 + t, :], n_pcT[:, t * P:(t + 1) * P], n_vbd.rearrange("p h n -> p (h n)"),
                                   start=True, stop=True)
                mm.then_inc(sig("nsa_oc"), 1)
                pe.wait_ge(*at("nsa_kT", 1, 1))
                pe.wait_ge(*at("nsa_ocdone", 1, 1))

                def scores(k):
                    br, t, s = GROUPS[k]
                    half = slice(64 * s, 64 * s + 64)
                    if k >= 2:
                        pe.wait_ge(*at("nsa_max", k - 1, 8))
                    for p in range(CH // 2):
                        nk = (t + 1) * P
                        c = p * nk
                        mm = pe.matmul(ps[:, 2 * (k % 2) + c // 512, c % 512:c % 512 + nk], n_qrT[half, p, t * P:(t + 1) * P],
                                       n_kT[half, br, p // 2, 0:nk], start=True, stop=True)
                    mm.then_inc(sig("nsa_scores"), 1)

                scores(0)
                for k, (br, t, s) in enumerate(GROUPS):
                    if k + 1 < len(GROUPS):
                        scores(k + 1)
                    pe.wait_ge(*at("nsa_probs", k + 1, 8))
                    if k >= 1:
                        pe.wait_ge(*at("nsa_pT", k, 8))
                    for p in range(CH // 2):
                        for b in range(t + 1):
                            q = p * (t + 1) + b
                            mm = pe.transpose(ps[:, 4 + q // 4, (q % 4) * P:(q % 4 + 1) * P], n_sm[k % 2][:, p, b * P:(b + 1) * P], ident[:])
                    mm.then_inc(sig("nsa_pturned"), 1)
                    pe.wait_ge(*at("nsa_pT", k + 1, 8))
                    if k >= 2:
                        pe.wait_ge(*at("nsa_o", k - 1, 8))
                    for p in range(CH // 2):
                        g = p // 2
                        c0 = (CVS, CVW)[br] + g * HD
                        for b in range(t + 1):
                            mm = pe.matmul(ps[:, 6 + k % 2, p * HD:(p + 1) * HD], n_pT[k % 2][:, p, b, :], z[:, b, c0:c0 + HD],
                                           start=(b == 0), stop=(b == t))
                    mm.then_inc(sig("nsa_pv"), 1)
                end_stage(pe, "tensor")

            def act_(act):
                act.activation(n_gate, z[:, :, CGT:ZW], ACT.Sigmoid)
                act.wait_ge(*at("nsa_q", 1, 1))
                act.copy(n_qT.rearrange("p h n -> p (h n)"), ps[:, 1:3, :].rearrange("p a b -> p (a b)")).then_inc(sig("nsa_qT"), 1)
                act.wait_ge(cmp_w_used, l + 1)
                act.wait_ge(*at("nsa_hid0", 1, 1))
                act.activation(n_hid[:, :, 0:NCMP], ps[:, 5, 0:64].rearrange("p (q n) -> p q n", q=4)[:, :, 0:NCMP],
                               ACT.Gelu_apprx_tanh).then_inc(sig("nsa_gelu"), 1)
                act.wait_ge(*at("nsa_cmax", 1, 1))
                act.activation(n_sc, n_sc, ACT.Exp).then_inc(sig("nsa_cexp"), 1)
                act.wait_ge(*at("nsa_qr", 1, 1))
                act.copy(n_qrT.rearrange("p h n -> p (h n)"), ps[:, 1:3, :].rearrange("p a b -> p (a b)"))
                act.wait_ge(*at("nsa_k", 1, 1))
                act.copy(n_kT.rearrange("p k g n -> p (k g n)"), ps[:, 6:8, :].rearrange("p a b -> p (a b)")).then_inc(sig("nsa_kT"), 1)
                for k, (br, t, s) in enumerate(GROUPS):
                    nk = (t + 1) * P
                    act.wait_ge(*at("nsa_max", k + 1, 8))
                    for p in range(CH // 2):
                        ins = act.activation(n_sm[k % 2][:, p, 0:nk], n_sm[k % 2][:, p, 0:nk], ACT.Exp,
                                             bias=n_mx[:, 4 * k + p:4 * k + p + 1], accum_out=n_den[:, 4 * k + p:4 * k + p + 1])
                    ins.then_inc(sig("nsa_probs"), 1)
                    act.wait_ge(*at("nsa_pturned", k + 1, 8))
                    if t == 0:
                        ins = act.copy(n_pT[k % 2][:, :, 0, :], ps[:, 4, :].rearrange("p (h n) -> p h n", n=P))
                    else:
                        ins = act.copy(n_pT[k % 2].rearrange("p h b n -> p (h b n)"), ps[:, 4:6, :].rearrange("p a b -> p (a b)"))
                    ins.then_inc(sig("nsa_pT"), 1)
                end_stage(act, "scalar")

            def rotate(dve, dst, src, n):
                a = src.rearrange("p t (h n) -> p t h n", n=HD)
                o = dst.rearrange("p t (h n) -> p t h n", n=HD)
                a1, a2 = a[:, :, :, 0:ROPE_HALF], a[:, :, :, ROPE_HALF:2 * ROPE_HALF]
                c, s = [v[:].unsqueeze(2).to_broadcast([P, NT, n, ROPE_HALF]) for v in (cos_t, sin_t)]
                r = [n_rt[:, k, :, 0:n, :] for k in range(4)]
                dve.tensor_tensor(r[0], a1, c, ALU.mult)
                dve.tensor_tensor(r[1], a2, s, ALU.mult)
                dve.tensor_tensor(r[2], a1, s, ALU.mult)
                vstep(dve, dve.tensor_tensor(r[3], a2, c, ALU.mult))
                dve.tensor_tensor(o[:, :, :, 0:ROPE_HALF], r[0], r[1], ALU.subtract)
                ins = dve.tensor_tensor(o[:, :, :, ROPE_HALF:2 * ROPE_HALF], r[2], r[3], ALU.add)
                vstep(dve, ins)

            def dve_(dve):
                dve.wait_ge(*at("nsa_next", 1, 1))
                for t in range(NT):
                    dve.tensor_copy(n_kc2[:, t, :, 0, :], z[:, t, CKC:CKS].rearrange("p (q n) -> p q n", q=4))
                    ins = dve.tensor_copy(n_kc2[:, t, :, 1, :], ps[:, 0, t * S:(t + 1) * S].rearrange("p (q n) -> p q n", q=4))
                ins.then_inc(sig("nsa_pairs"), 1)
                dve.memset(n_hid, 0.0).then_inc(sig("nsa_hid0"), 1)
                dve.wait_ge(*at("nsa_blkT", 1, 1))
                for q in range(4):
                    rows = ps[:, 3 + q // 2, (q % 2) * S:(q % 2 + 1) * S]
                    src = bass.AP(tensor=rows.tensor, offset=rows.offset, ap=[list(rows.ap[0]), [2, 16], [CST, NCMP]])
                    ins = dve.tensor_tensor(n_blk[:, q], src, l_posT[:].unsqueeze(2).to_broadcast([P, 16, NCMP]), ALU.add)
                ins.then_inc(sig("nsa_blk"), 1)
                vstep(dve, dve.tensor_copy(n_qr, z[:, :, CQ:CKC]))
                rotate(dve, n_qr, z[:, :, CQ:CKC], CH)
                rotate(dve, z[:, :, CKS:CVS], z[:, :, CKS:CVS], CG)
                rotate(dve, z[:, :, CKW:CVW], z[:, :, CKW:CVW], CG)
                for t in range(NT):
                    for k, c0 in enumerate((CKS, CKW)):
                        keys = z[:, t, c0:c0 + CG * HD].rearrange("p (g n) -> p g n", g=CG)
                        ins = dve.tensor_copy(n_k2[:, t, k], keys.unsqueeze(2).to_broadcast([P, CG, 2, HD]))
                ins.then_inc(sig("nsa_rot"), 1)
                dve.wait_ge(*at("nsa_gelu", 1, 1))
                for g in range(CG):
                    for s in range(2):
                        ins = dve.tensor_copy(n_hv[:, s, 2 * g:2 * g + 2, :], n_hid[:, 2 + g, :].unsqueeze(1).to_broadcast([P, 2, 16]))
                ins.then_inc(sig("nsa_hid"), 1)
                dve.wait_ge(*at("nsa_cmp", 1, 1))
                dve.tensor_copy(n_kcT.rearrange("p g n -> p (g n)"), ps[:, 6, 0:CG * 16]).then_inc(sig("nsa_kc"), 1)
                dve.tensor_tensor(n_vbd, ps[:, 6, 64:64 + HD].unsqueeze(1).to_broadcast([P, CH, HD]),
                                  block16[:].unsqueeze(2).to_broadcast([P, CH, HD]), ALU.mult).then_inc(sig("nsa_vbd"), 1)
                dve.wait_ge(*at("nsa_sc", 1, 1))
                for s in range(2):
                    for t in range(NT):
                        c = t * 64
                        ins = dve.scalar_tensor_tensor(out=n_sc[:, t, 4 * s:4 * s + 4, :], in0=ps[:, 3 + s, c:c + 64].rearrange("p (h n) -> p h n", h=4),
                                                       scalar=SCALE, in1=cmp_ok[:, t, :].unsqueeze(1).to_broadcast([P, 4, 16]),
                                                       op0=ALU.mult, op1=ALU.mult)
                vstep(dve, ins)
                for t in range(NT):
                    ins = dve.tensor_tensor(n_sc[:, t], n_sc[:, t], cmp_neg[:, t, :].unsqueeze(1).to_broadcast([P, CH, 16]), ALU.add)
                vstep(dve, ins)
                sc16 = n_sc.rearrange("p t h n -> p (t h) n")
                vstep(dve, dve.tensor_reduce(n_cs[:, 0, :], sc16, AX, ALU.max))
                dve.tensor_tensor(sc16, sc16, n_cs[:, 0, :].unsqueeze(2).to_broadcast([P, 16, 16]), ALU.subtract).then_inc(sig("nsa_cmax"), 1)
                dve.wait_ge(*at("nsa_cexp", 1, 1))
                vstep(dve, dve.tensor_reduce(n_cs[:, 0, :], sc16, AX, ALU.add))
                vstep(dve, dve.reciprocal(n_cs[:, 1, :], n_cs[:, 0, :]))
                vstep(dve, dve.tensor_tensor(sc16, sc16, n_cs[:, 1, :].unsqueeze(2).to_broadcast([P, 16, 16]), ALU.mult))
                for t in range(NT):
                    ins = dve.tensor_tensor(n_sc[:, t], n_sc[:, t], cmp_ok[:, t, :].unsqueeze(1).to_broadcast([P, CH, 16]), ALU.mult)
                ins.then_inc(sig("nsa_pc"), 1)
                dve.wait_ge(*at("nsa_pcturned", 1, 1))
                dve.tensor_copy(n_pcT, ps[:, 0, 0:S]).then_inc(sig("nsa_pcT"), 1)
                dve.wait_ge(*at("nsa_oc", 1, 1))
                dve.wait_ge(*at("nsa_kT", 1, 1))
                for t in range(NT):
                    for s in range(2):
                        o = ps[:, 3 + t, s * 256:(s + 1) * 256].rearrange("p (h n) -> p h n", h=4)
                        ins = dve.tensor_tensor(y_of(t, s), o, gate_of(t, s, 0).unsqueeze(2).to_broadcast([P, 4, HD]), ALU.mult)
                ins.then_inc(sig("nsa_ocdone"), 1)
                dve.wait_ge(*at("nsa_ocdone", 1, 1))

                def finish(k):
                    br, t, s = GROUPS[k]
                    q = slice(4 * k, 4 * k + 4)
                    dve.wait_ge(*at("nsa_probs", k + 1, 8))
                    vstep(dve, dve.reciprocal(n_rd[:, q], n_den[:, q]))
                    vstep(dve, dve.tensor_tensor(n_rd[:, q], n_rd[:, q], gate_of(t, s, 1 + br), ALU.mult))
                    dve.wait_ge(*at("nsa_pv", k + 1, 8))
                    vstep(dve, dve.tensor_tensor(n_o, ps[:, 6 + k % 2, 0:256].rearrange("p (h n) -> p h n", h=4),
                                                 n_rd[:, q].unsqueeze(2).to_broadcast([P, 4, HD]), ALU.mult))
                    ins = dve.tensor_tensor(y_of(t, s), y_of(t, s), n_o, ALU.add)
                    ins.then_inc(sig("nsa_o"), 1)
                    dve.wait_ge(*at("nsa_o", k + 1, 8))

                for k, (br, t, s) in enumerate(GROUPS):
                    nk = (t + 1) * P
                    dve.wait_ge(*at("nsa_scores", k + 1, 8))
                    if k >= 2:
                        dve.wait_ge(*at("nsa_pturned", k - 1, 8))
                    for p in range(CH // 2):
                        c = p * nk
                        ins = dve.tensor_tensor_reduce(out=n_sm[k % 2][:, p, 0:nk], in0=ps[:, 2 * (k % 2) + c // 512, c % 512:c % 512 + nk],
                                                       in1=causal_neg[:, S - nk:S], scale=SCALE, scalar=-3e38, op0=ALU.add, op1=ALU.max,
                                                       accum_out=n_mx[:, 4 * k + p:4 * k + p + 1])
                    vstep(dve, ins)
                    dve.tensor_scalar(n_mx[:, 4 * k:4 * k + 4], n_mx[:, 4 * k:4 * k + 4], -1.0, None, ALU.mult).then_inc(sig("nsa_max"), 1)
                    if k >= 1:
                        finish(k - 1)
                finish(len(GROUPS) - 1)
                end_stage(dve, "vector")

            return pe_, act_, dve_, idle_pool

        MP = Arena(arena)
        MP.at = 8192
        p_gate = MP.take(NT, D)
        p_rows = MP.take(NT, PLE)
        p_rowsT = MP.take(PLE // P, S)
        p_t = MP.take(NT, D)

        def ple_gate_act(act, j, src):
            return act.activation(p_gate[:, j.tile, j.col:j.col + j.n], src, ACT.Sigmoid)

        def ple_turn(l):
            def pe_(pe):
                for c in range(PLE // P):
                    for t in range(NT):
                        mm = pe.transpose(ps[:, 4, c * S + t * P:c * S + (t + 1) * P], p_rows[:, t, c::PLE // P], ident[:])
                mm.then_inc(sig("ple_turned"), 1)
                end_stage(pe, "tensor")

            def act_(act):
                act.wait_ge(sig("ple_turned"), l + 1)
                act.copy(p_rowsT.rearrange("p c s -> p (c s)"), ps[:, 4, :])
                end_stage(act, "scalar")

            return pe_, act_, lambda dve: end_stage(dve, "vector"), idle_pool

        def ple_copy(dve, j, src):
            t = p_t[:, j.tile, j.col:j.col + j.n]
            vstep(dve, dve.tensor_tensor(t, src, p_gate[:, j.tile, j.col:j.col + j.n], ALU.mult))
            cols = x[:, j.tile, j.col:j.col + j.n]
            return dve.tensor_tensor(cols, cols, t, ALU.add)

        def gates_act(act):
            act.wait_ge(evac_dve, jobs_of["gates"][-1].evac)
            act.activation(c_gate, c_gate, ACT.Sigmoid)

        def gates_load(act):
            act.dma_start(c_bias, d["b_branch_gate"].to_broadcast([P, 2 * D])).then_inc(sig("gate_bias"), 16)

        def with_before(stage, act_first=None, dve_first=None, act_last=None):
            pe_, act_, dve_, pool_ = stage

            def act2(act):
                if act_first:
                    act_first(act)
                act_(act)

            def dve2(dve):
                if dve_first:
                    dve_first(dve)
                dve_(dve)

            return pe_, act2, dve2, pool_

        def sum_dve(dve):
            dve.wait_ge(evac_dve, jobs_of["y_att"][-1].evac)
            for t in range(NT):
                dve.tensor_tensor(c_y[:, t, :], c_y[:, t, :], c_t[:, t, :], ALU.add)

        def za_copy(act, j, src):
            return act.copy(za[:, j.tile, j.col:j.col + j.n], src)

        def zb_copy_act(act, j, src):
            return act.copy(zb[:, j.tile, j.col:j.col + j.n], src)

        def zb_copy_dve(dve, j, src):
            return dve.tensor_copy(zb[:, j.tile, j.col:j.col + j.n], src)

        def params_wait(act):
            act.wait_ge(sig("params"), 16 * len(P1_LOADS))
            act.wait_ge(sig("layer_params"), 16 * N_LAYER_LOADS)

        MO = Arena(arena)
        o_gain = MO.take(D)
        o_y = MO.take(NT, D)

        def final_stage():
            n = NORMS.index("final")

            def act_(act):
                act.dma_start(o_gain, d["g_final_2"].rearrange("(a n) -> a n", a=1).to_broadcast([P, D])).then_inc(sig("final_gain"), 16)
                act_norm_stats(act, n)
                act.wait_ge(sig("final_out"), 1)
                act.dma_start(out[0].rearrange("(t p) n -> p t n", p=P), o_y).then_inc(sig("stored"), 16)
                act.wait_ge(sig("stored"), 16)
                end_stage(act, "scalar")

            def dve_(dve):
                vstep(dve, dve_norm_scale(dve, n, o_y))
                dve.wait_ge(sig("final_gain"), 16)
                for t in range(NT):
                    ins = dve.tensor_tensor(o_y[:, t, :], o_y[:, t, :], o_gain, ALU.mult)
                ins.then_inc(sig("final_out"), 1)
                end_stage(dve, "vector")

            return (lambda pe: end_stage(pe, "tensor")), act_, dve_, idle_pool

        stages = [
            (setup_pe, setup_act, setup_dve, setup_pool),
            stage_norm("n1", g1T),
            stage_project("in_a", hT, za_copy, act_more=params_wait, dve_more=masks_dve),
            (gla_pe, gla_act, gla_dve, gla_pool),
            stage_project("in_b", hT, zb_copy_act, zb_copy_dve),
            (dil_pe, dil_act, dil_dve, idle_pool),
            with_before(stage_project("gates", hT, dve_copy=gates_copy, act_more=gates_act), act_first=gates_load,
                        dve_first=lambda dve: dve.wait_ge(sig("gate_bias"), 16)),
            stage_project("y_gla", ogT, dve_copy=y_gla_copy),
            stage_project("y_att", oaT, dve_copy=y_att_copy, dve_more=sum_dve),
            stage_turn("ym", c_y),
            stage_project("out_1", hT, dve_copy=residual_copy),
            stage_norm("n2", g2T),
            ((lambda pe: router_pe(pe, r1_w, 36, moe1)), router1_act, router1_dve, idle_pool),
            stage_moe(moe1),
            stage_moe_rest(moe1),
        ]
        for l in range(LAYERS):
            first = rope_act if l == 0 else None
            stages += [
                with_before(stage_norm(f"mix{l}", l_gT[:, 3 * l:3 * l + 1, :].rearrange("p a c -> p (a c)")),
                            act_first=first, dve_first=rope_dve if l == 0 else None),
                stage_project(f"in_{l}", hT, z_copy_act, z_copy_dve),
                gating(l),
                rwkv(l),
                nsa(l),
                with_before(stage_turn(f"cat{l}", ycat), act_first=(lambda act: load_layer(act, 1)) if l == 0 else None),
                stage_project(f"out_{l}_2", hT, dve_copy=residual_copy),
                stage_norm(f"ffn{l}", l_gT[:, 3 * l + 1:3 * l + 2, :].rearrange("p a c -> p (a c)")),
            ]
            if l % 2:
                stages.append(((lambda pe: router_pe(pe, r2_w, NE2, moe2)), router2_act, router2_dve, idle_pool))

            def ple_load(act, l=l):
                act.dma_start(p_rows, d["p_2"][l, 0].rearrange("(t p) n -> p t n", p=P)).then_inc(sig("ple_rows"), 16)
                if l == 0:
                    act.wait_ge(sig("layer_params"), 2 * 16 * N_LAYER_LOADS)

            def ple_wait(act, l=l):
                act.wait_ge(sig("ple_rows"), 16 * (l + 1))

            stages += [stage_dense(ffn)] if l == 0 else [stage_moe(moe2), stage_moe_rest(moe2)]
            stages += [
                with_before(stage_norm(f"ple{l}", l_gT[:, 3 * l + 2:3 * l + 3, :].rearrange("p a c -> p (a c)")), act_first=ple_load),
                stage_project(f"ple_g{l}", hT, ple_gate_act, act_more=ple_wait),
                ple_turn(l),
                stage_project(f"ple_p{l}", p_rowsT, dve_copy=ple_copy),
            ]
        stages.append(final_stage())

        block = ctx.enter_context(nc.Block())

        @block.sync
        def _(sp):
            sp.dma_start(x[:], d["x"][0].rearrange("(t p) n -> p t n", p=P)).then_inc(sig("x_ready"), 16)
            sp.dma_start(g1T[:], d["norm1_g"][0].rearrange("(p c) -> p c", c=KC)).then_inc(sig("x_ready"), 16)
            stream(sp, units[0:SLOTS])
            for dst, src in P1_LOADS:
                sp.dma_start(dst, src).then_inc(sig("params"), 16)
            load_layer(sp, 0)
            stream(sp, units[SLOTS:n_units_1])
            stream_moe(sp, moe1)
            at = n_units_1
            for l in range(LAYERS):
                stream(sp, units[at:n_units_2[l]])
                if l == 0:
                    stream_dense(sp, ffn)
                else:
                    stream_moe(sp, moe2)
                stream(sp, units[n_units_2[l]:n_units_3[l]])
                at = n_units_3[l]

        @block.tensor
        def _(pe):
            for s in stages:
                s[0](pe)

        @block.scalar
        def _(act):
            for s in stages:
                s[1](act)

        @block.vector
        def _(dve):
            for s in stages:
                s[2](dve)

        @block.gpsimd
        def _(pool):
            for s in stages:
                s[3](pool)


NAMES = """x norm1_g w_in w_gla_a2 b_gla_a gla_out_norm_g dil_q_norm_g dil_k_norm_g w_proj_gla
    w_proj_attn w_branch_gate b_branch_gate w_out norm2_g w_router_group b_router_group
    w_router_expert b_router_expert w_gate w_up w_down p_2 positions_2 g_mix_2 w_in_2
    w_out_2 gm_ln_g_2 gm_ln_b_2 gm_ws_2 gm_bs_2 rw_mu_2 rw_w0_2 rw_w_up_2 rw_a0_2
    rw_a_up_2 rw_g_up_2 rw_k_k_2 rw_k_a_2 rw_r_k_2 rw_gn_g_2 rw_gn_b_2 nsa_cmp_pos_2
    nsa_kc_w1_2 nsa_kc_w2_2 nsa_vc_w1_2 nsa_vc_w2_2 g_ffn_2 ffn_w1_2 ffn_w3_2 ffn_w2_2
    router_w_2 router_b_2 moe_w1_2 moe_w3_2 moe_w2_2 g_ple_2 ple_gate_w_2 ple_proj_w_2
    g_final_2""".split()


def kernel(**inputs):
    import concourse.bacc as bacc
    from concourse.bass_utils import run_bass_kernel_spmd

    nc = bacc.Bacc("TRN2", target_bir_lowering=False, num_devices=1)
    arrays = {n: np.ascontiguousarray(inputs[n]) for n in NAMES}
    d = {n: nc.dram_tensor(f"in_{n}", a.shape, mybir.dt.from_np(a.dtype), kind="ExternalInput").ap()
         for n, a in arrays.items()}
    out = nc.dram_tensor("out", (1, S, D), F32, kind="ExternalOutput").ap()
    emit(nc, d, out)
    r = run_bass_kernel_spmd(nc, [{f"in_{n}": a for n, a in arrays.items()}], core_ids=[0])
    return r.results[0]["out"]
```
